# Optimizing a Trainium2 kernel written in Bass

```python
import math
import jax, jax.numpy as jnp
from jax import lax
import numpy as np

D_MODEL = 1024
BATCH = 1
SEQ = 256
DEPTH = 2

GRID_W = 64
CTX_LEN = 256

HEAD_DIM = 128
N_Q_HEADS = D_MODEL // HEAD_DIM
N_KV_HEADS = 2
GQA_GROUP = N_Q_HEADS // N_KV_HEADS
Q_BLOCK = 128
ROPE_THETA = 10000.0
ROPE_AXIS_DIM = HEAD_DIM // 2
ATTN_SCALE = HEAD_DIM ** -0.5

D_HYENA = D_MODEL
HYENA_ORDER = 2
HYENA_BANDS = 16
HYENA_EMB = 1 + 2 * HYENA_BANDS
HYENA_FILTER_HIDDEN = 64
SHORT_CONV = 3
DECAY_TARGET = 1e-2
FAST_DECAY_PCT = 0.3
SLOW_DECAY_PCT = 1.5
MIN_DECAY = math.log(DECAY_TARGET) / FAST_DECAY_PCT
MAX_DECAY = math.log(DECAY_TARGET) / SLOW_DECAY_PCT

D_FNET = D_MODEL
FNET_GROUPS = 4
FNET_GROUP_DIM = D_FNET // FNET_GROUPS

D_FF = 4 * D_MODEL

N_BRANCH = 3
N_MOD = 6

Q_W = N_Q_HEADS * HEAD_DIM
KV_W = N_KV_HEADS * HEAD_DIM
HY_W = (HYENA_ORDER + 1) * D_HYENA
OFF_Q = 0
OFF_K = OFF_Q + Q_W
OFF_V = OFF_K + KV_W
OFF_HY = OFF_V + KV_W
OFF_FN = OFF_HY + HY_W
OFF_G = OFF_FN + D_FNET
D_IN = OFF_G + N_BRANCH * D_MODEL

ALPHA = (2 * DEPTH) ** 0.25
BETA = (8 * DEPTH) ** -0.25
LN_EPS = 1e-6
RMS_EPS = 1e-6
KERN_EPS = 1e-6

kernel_name = 'hybrid_hyena_fnet_gqa_flow_block'

def layer_norm(x, g, b):
    xf = x.astype(jnp.float32)
    mu = jnp.mean(xf, -1, keepdims=True)
    var = jnp.mean(jnp.square(xf - mu), -1, keepdims=True)
    return ((xf - mu) * lax.rsqrt(var + LN_EPS)).astype(x.dtype) * g + b

def rms_norm(x, g):
    xf = x.astype(jnp.float32)
    return (xf * lax.rsqrt(jnp.mean(jnp.square(xf), -1, keepdims=True) + RMS_EPS)).astype(x.dtype) * g

def modulate(x, shift, scale):
    return x * (1.0 + scale) + shift

def split_heads(t, n_heads):
    b, n, _ = t.shape
    return t.reshape(b, n, n_heads, HEAD_DIM).transpose(0, 2, 1, 3)

def merge_heads(t):
    b, h, n, d = t.shape
    return t.transpose(0, 2, 1, 3).reshape(b, n, h * d)

def axial_rope_tables(rows):
    row = jnp.repeat(jnp.arange(rows, dtype=jnp.float32), GRID_W)
    col = jnp.tile(jnp.arange(GRID_W, dtype=jnp.float32), rows)
    inv_freq = ROPE_THETA ** (-jnp.arange(ROPE_AXIS_DIM // 2, dtype=jnp.float32) * 2.0 / ROPE_AXIS_DIM)
    ang_r = row[:, None] * inv_freq[None, :]
    ang_c = col[:, None] * inv_freq[None, :]
    return jnp.cos(ang_r), jnp.sin(ang_r), jnp.cos(ang_c), jnp.sin(ang_c)

def rope_1d(x, cos, sin):
    x1, x2 = jnp.split(x, 2, -1)
    return jnp.concatenate([x1 * cos - x2 * sin, x1 * sin + x2 * cos], -1)

def apply_axial_rope(x, cos_r, sin_r, cos_c, sin_c):
    x_row, x_col = jnp.split(x, 2, -1)
    return jnp.concatenate([rope_1d(x_row, cos_r, sin_r), rope_1d(x_col, cos_c, sin_c)], -1)

def gqa_attend(q, k, v):
    s = jnp.einsum('bgrqd,bgkd->bgrqk', q, k).astype(jnp.float32) * ATTN_SCALE
    p = jax.nn.softmax(s, axis=-1).astype(v.dtype)
    return jnp.einsum('bgrqk,bgkd->bgrqd', p, v)

def blockwise_attention(q, k, v):
    b, h, n, d = q.shape
    n_blk = n // Q_BLOCK
    qb = q.reshape(b, N_KV_HEADS, GQA_GROUP, n_blk, Q_BLOCK, d).transpose(3, 0, 1, 2, 4, 5)
    ob = lax.map(lambda qi: gqa_attend(qi, k, v), qb)
    return ob.transpose(1, 2, 3, 0, 4, 5).reshape(b, h, n, d)

def kv_heads(p_kv, k_gain):
    k = rms_norm(split_heads(p_kv[..., :KV_W], N_KV_HEADS), k_gain)
    v = split_heads(p_kv[..., KV_W:], N_KV_HEADS)
    return k, v

def short_conv(u, w, b):
    n = u.shape[1]
    pad = SHORT_CONV // 2
    up = jnp.pad(u, ((0, 0), (pad, SHORT_CONV - 1 - pad), (0, 0)))
    out = b
    for j in range(SHORT_CONV):
        out = out + up[:, j:j + n] * w[j]
    return out

def hyena_kernel(n, lp):
    dt = lp['hy_w1'].dtype
    t = jnp.linspace(0.0, 1.0, n, dtype=jnp.float32)[:, None]
    w = (2.0 * math.pi / n) * jnp.arange(n, dtype=jnp.float32)[:, None]
    f = jnp.linspace(1e-4, HYENA_BANDS - 1, HYENA_BANDS, dtype=jnp.float32)[None, :]
    emb = jnp.concatenate([t, jnp.cos(f * w), -jnp.sin(f * w)], -1).astype(dt)
    h = jnp.sin(lp['hy_freq1'] * (emb @ lp['hy_w1'] + lp['hy_b1']))
    h = jnp.sin(lp['hy_freq2'] * (h @ lp['hy_w2'] + lp['hy_b2']))
    h = (h @ lp['hy_w3']).astype(jnp.float32).reshape(n, 2, HYENA_ORDER, D_HYENA)
    deltas = jnp.linspace(MIN_DECAY, MAX_DECAY, D_HYENA, dtype=jnp.float32)
    h = h * jnp.exp(-t * jnp.abs(deltas))[:, None, None, :]
    kern = jnp.concatenate([h[:, 0], jnp.zeros_like(h[:1, 0]), h[:0:-1, 1]], 0)
    return kern * lax.rsqrt(jnp.sum(jnp.square(kern), 0, keepdims=True) + KERN_EPS)

def bidirectional_long_conv(u, kf, skip):
    n = u.shape[1]
    uf = jnp.fft.rfft(u.astype(jnp.float32), n=2 * n, axis=1)
    y = jnp.fft.irfft(uf * kf[None], n=2 * n, axis=1)[:, :n]
    return (y + u.astype(jnp.float32) * skip.astype(jnp.float32)).astype(u.dtype)

def hyena_branch(p_hy, lp, kern):
    u = short_conv(p_hy, lp['conv_w'], lp['conv_b'])
    xs = jnp.split(u, HYENA_ORDER + 1, -1)
    kf = jnp.fft.rfft(kern, axis=0)
    z = xs[HYENA_ORDER]
    for o in range(HYENA_ORDER):
        z = xs[o] * bidirectional_long_conv(z, kf[:, o], lp['hy_skip'][o])
    return z

def fnet_mix(u):
    b, n, _ = u.shape
    ug = u.reshape(b, n, FNET_GROUPS, FNET_GROUP_DIM).astype(jnp.float32)
    y = jnp.fft.fft2(ug, axes=(1, 3), norm='ortho').real
    return y.reshape(b, n, D_FNET).astype(u.dtype)

def parallel_merge(p, o_att, lp, kern):
    y_att = o_att @ lp['w_att_o']
    y_hy = hyena_branch(p[..., OFF_HY:OFF_FN], lp, kern) @ lp['w_hy_o']
    y_fn = fnet_mix(p[..., OFF_FN:OFF_G]) @ lp['w_fn_o']
    g_att, g_hy, g_fn = jnp.split(jax.nn.sigmoid(p[..., OFF_G:D_IN]), N_BRANCH, -1)
    return (g_att * y_att + g_hy * y_hy + g_fn * y_fn) @ lp['w_out'] + lp['b_out']

def context_mixer(p, lp, kern):
    q = rms_norm(split_heads(p[..., OFF_Q:OFF_K], N_Q_HEADS), lp['q_gain'])
    k, v = kv_heads(p[..., OFF_K:OFF_HY], lp['k_gain'])
    b, h, n, d = q.shape
    o = gqa_attend(q.reshape(b, N_KV_HEADS, GQA_GROUP, n, d), k, v).reshape(b, h, n, d)
    return parallel_merge(p, merge_heads(o), lp, kern), k, v

def latent_mixer(p, lp, kern, rope, k_ctx, v_ctx):
    q = apply_axial_rope(rms_norm(split_heads(p[..., OFF_Q:OFF_K], N_Q_HEADS), lp['q_gain']), *rope)
    k_lat, v_lat = kv_heads(p[..., OFF_K:OFF_HY], lp['k_gain'])
    k_lat = apply_axial_rope(k_lat, *rope)
    k = jnp.concatenate([k_lat, k_ctx], 2)
    v = jnp.concatenate([v_lat, v_ctx], 2)
    o = blockwise_attention(q, k, v)
    return parallel_merge(p, merge_heads(o), lp, kern)

def sq_relu_mlp(h, lp):
    return jnp.square(jax.nn.relu(h @ lp['w_mlp1'] + lp['b_mlp1'])) @ lp['w_mlp2'] + lp['b_mlp2']

def setup_inputs(seed: int = 0) -> dict:
    key = jax.random.key(seed)
    ks = iter(jax.random.split(key, 40))

    def nrm(shape, scale):
        return jax.random.normal(next(ks), shape, jnp.float32) * scale

    def gain(shape):
        return 1.0 + nrm(shape, 0.01)

    fh = HYENA_FILTER_HIDDEN
    return {
        'x': nrm((BATCH, SEQ, D_MODEL), 1.0),
        'c': nrm((BATCH, D_MODEL), 1.0),
        'ctx': nrm((BATCH, CTX_LEN, D_MODEL), 1.0),
        'c_ctx': nrm((D_MODEL,), 1.0),
        'w_ada': nrm((DEPTH, D_MODEL, N_MOD * D_MODEL), D_MODEL ** -0.5),
        'b_ada': nrm((DEPTH, N_MOD * D_MODEL), 0.01),
        'w_in': nrm((DEPTH, D_MODEL, D_IN), D_MODEL ** -0.5),
        'b_in': nrm((DEPTH, D_IN), 0.01),
        'conv_w': nrm((DEPTH, SHORT_CONV, HY_W), SHORT_CONV ** -0.5),
        'conv_b': nrm((DEPTH, HY_W), 0.01),
        'hy_w1': nrm((DEPTH, HYENA_EMB, fh), HYENA_EMB ** -0.5),
        'hy_b1': nrm((DEPTH, fh), 0.01),
        'hy_freq1': gain((DEPTH, fh)),
        'hy_w2': nrm((DEPTH, fh, fh), fh ** -0.5),
        'hy_b2': nrm((DEPTH, fh), 0.01),
        'hy_freq2': gain((DEPTH, fh)),
        'hy_w3': nrm((DEPTH, fh, 2 * HYENA_ORDER * D_HYENA), fh ** -0.5),
        'hy_skip': nrm((DEPTH, HYENA_ORDER, D_HYENA), 0.1),
        'q_gain': gain((DEPTH, HEAD_DIM)),
        'k_gain': gain((DEPTH, HEAD_DIM)),
        'w_att_o': nrm((DEPTH, Q_W, D_MODEL), Q_W ** -0.5),
        'w_hy_o': nrm((DEPTH, D_HYENA, D_MODEL), D_HYENA ** -0.5),
        'w_fn_o': nrm((DEPTH, D_FNET, D_MODEL), D_FNET ** -0.5),
        'w_out': nrm((DEPTH, D_MODEL, D_MODEL), BETA * D_MODEL ** -0.5),
        'b_out': nrm((DEPTH, D_MODEL), 0.01),
        'ln1_g': gain((DEPTH, D_MODEL)),
        'ln1_b': nrm((DEPTH, D_MODEL), 0.01),
        'w_mlp1': nrm((DEPTH, D_MODEL, D_FF), D_MODEL ** -0.5),
        'b_mlp1': nrm((DEPTH, D_FF), 0.01),
        'w_mlp2': nrm((DEPTH, D_FF, D_MODEL), BETA * D_FF ** -0.5),
        'b_mlp2': nrm((DEPTH, D_MODEL), 0.01),
        'ln2_g': gain((DEPTH, D_MODEL)),
        'ln2_b': nrm((DEPTH, D_MODEL), 0.01),
    }

def reference(x, c, ctx, c_ctx, w_ada, b_ada, w_in, b_in, conv_w, conv_b,
              hy_w1, hy_b1, hy_freq1, hy_w2, hy_b2, hy_freq2, hy_w3, hy_skip,
              q_gain, k_gain, w_att_o, w_hy_o, w_fn_o, w_out, b_out, ln1_g, ln1_b,
              w_mlp1, b_mlp1, w_mlp2, b_mlp2, ln2_g, ln2_b):
    n_lat = x.shape[1]
    n_ctx = ctx.shape[1]
    ROWS = n_lat // GRID_W
    rope = tuple(t.astype(x.dtype) for t in axial_rope_tables(ROWS))
    s_lat = jax.nn.silu(c)
    s_ctx = jax.nn.silu(c_ctx)
    for i in range(DEPTH):
        last = i == DEPTH - 1
        lp = dict(conv_w=conv_w[i], conv_b=conv_b[i], hy_w1=hy_w1[i], hy_b1=hy_b1[i],
                  hy_freq1=hy_freq1[i], hy_w2=hy_w2[i], hy_b2=hy_b2[i], hy_freq2=hy_freq2[i],
                  hy_w3=hy_w3[i], hy_skip=hy_skip[i], q_gain=q_gain[i], k_gain=k_gain[i],
                  w_att_o=w_att_o[i], w_hy_o=w_hy_o[i], w_fn_o=w_fn_o[i], w_out=w_out[i],
                  b_out=b_out[i], w_mlp1=w_mlp1[i], b_mlp1=b_mlp1[i], w_mlp2=w_mlp2[i],
                  b_mlp2=b_mlp2[i])
        mod_l = (s_lat @ w_ada[i] + b_ada[i]).reshape(x.shape[0], 1, N_MOD, D_MODEL)
        mod_c = (s_ctx @ w_ada[i] + b_ada[i]).reshape(1, 1, N_MOD, D_MODEL)

        h_c = modulate(ctx, mod_c[:, :, 0], mod_c[:, :, 1])
        if last:
            k_c, v_c = kv_heads(h_c @ w_in[i][:, OFF_K:OFF_HY] + b_in[i][OFF_K:OFF_HY], lp['k_gain'])
        else:
            y_c, k_c, v_c = context_mixer(h_c @ w_in[i] + b_in[i], lp, hyena_kernel(n_ctx, lp))
            ctx = layer_norm(ALPHA * ctx + mod_c[:, :, 2] * y_c, ln1_g[i], ln1_b[i])
            y_c = sq_relu_mlp(modulate(ctx, mod_c[:, :, 3], mod_c[:, :, 4]), lp)
            ctx = layer_norm(ALPHA * ctx + mod_c[:, :, 5] * y_c, ln2_g[i], ln2_b[i])

        h_l = modulate(x, mod_l[:, :, 0], mod_l[:, :, 1])
        y_l = latent_mixer(h_l @ w_in[i] + b_in[i], lp, hyena_kernel(n_lat, lp), rope, k_c, v_c)
        x = layer_norm(ALPHA * x + mod_l[:, :, 2] * y_l, ln1_g[i], ln1_b[i])
        y_l = sq_relu_mlp(modulate(x, mod_l[:, :, 3], mod_l[:, :, 4]), lp)
        x = layer_norm(ALPHA * x + mod_l[:, :, 5] * y_l, ln2_g[i], ln2_b[i])
    return x


_drawn_inputs = setup_inputs


def setup_inputs(seed=0):
    import zlib

    import numpy as np

    out = dict(_drawn_inputs(seed))
    spreads = {}
    factors = {'ctx': 6.191,
     'b_in': 3.188,
     'conv_b': 2.723,
     'hy_freq1': 7.146,
     'hy_freq2': 5.86,
     'q_gain': 8.0,
     'k_gain': 8.0,
     'b_out': 8.0,
     'ln1_g': 3.719,
     'ln1_b': 8.542,
     'b_mlp1': 8.0,
     'b_mlp2': 37.81,
     'ln2_g': 3.748,
     'ln2_b': 9.727}
    for name, (base, spread) in spreads.items():
        noise = np.random.default_rng([zlib.crc32(name.encode()), seed]).standard_normal(out[name].shape)
        drawn = base * np.exp(spread * noise) if base else spread * noise
        out[name] = __import__('jax').numpy.asarray(drawn.astype(out[name].dtype))
    for name, factor in factors.items():
        out[name] = (out[name] * factor).astype(out[name].dtype)
    return out
```

```python
import math
from contextlib import ExitStack

import numpy as np
import concourse.bass as bass
from concourse import mybir

F32 = mybir.dt.float32
F32R = mybir.dt.float32r
ALU = mybir.AluOpType
ACT = mybir.ActivationFunctionType
AX = mybir.AxisListType

P = 128
D = 1024
NC = D // P
S = 256
T = 2 * S
DEPTH = 2
HEAD = 128
NH = D // HEAD
NKV = 2
GRID_W = 64
FF = 4 * D
OFF_K = D
OFF_V = OFF_K + NKV * HEAD
OFF_HY = OFF_V + NKV * HEAD
OFF_FN = OFF_HY + 3 * D
OFF_G = OFF_FN + D
D_IN = OFF_G + 3 * D
UC = 256
UW = NC * UC
NG = D // UC
BANDS = 16
EMB = 1 + 2 * BANDS
FH = 64
ALPHA = (2 * DEPTH) ** 0.25
LN_EPS = 1e-6
RMS_EPS = 1e-6
KERN_EPS = 1e-6
ATTN_SCALE = HEAD ** -0.5
RAW = 3
TWO_PI = 2.0 * math.pi
PI_HI = 6.28125
PI_LO = TWO_PI - PI_HI
ROUND = 1.5 * 2.0 ** 23
BELOW_PI = 3.1415925

VEC = {}
_at = 0
for _name, _n in (("b_in", D_IN // P), ("b_ada", 6 * NC), ("b_mlp1", FF // P), ("b_mlp2", NC), ("b_out", NC),
                  ("ln1_g", NC), ("ln1_b", NC), ("ln2_g", NC), ("ln2_b", NC), ("conv_w", 9 * NC),
                  ("conv_b", 3 * NC), ("hy_skip", 2 * NC), ("q_gain", 1), ("k_gain", 1),
                  ("hy_b1", 1), ("hy_freq1", 1), ("hy_b2", 1), ("hy_freq2", 1)):
    VEC[_name] = _at
    _at += _n
NVEC = _at

CON = {}
_at = 0
for _name, _n in (("hy_fwd", 4 * P), ("hy_inv", 4 * P), ("fnet", 4 * S), ("rope_cos", S), ("rope_sin", S),
                  ("swap", P), ("ident", P), ("ones", P), ("mean", P), ("emb", S), ("notfirst", 1), ("epsln", 1), ("epsrms", 1), ("epskern", 1)):
    CON[_name] = _at
    _at += _n
NCON = _at



def layer_units(l):
    return ([("ada", l, j) for j in range(24)],)


def mixing(l, spare):
    out = []

    def unit(*s):
        out.append(s)
        if spare:
            out.append(spare.pop(0))

    streams = (0, 1) if l == 0 else (1,)
    out += [("f1", l), ("f2", l)]
    out.append(("hprep", l))
    z = []
    for cg in range(NG):
        for part in (2, 0, 1):
            unit("hy", l, cg, part)
            out += z[:7]
            z = z[7:]
        out += z
        z = []
        for o in range(2):
            z += [("K0", l, cg, o), ("KN", l, cg, o), ("K1", l, cg, o)]
        for s in streams:
            for o in range(2):
                z += [("T", l, cg, s, o), ("F", l, cg, s, o), ("I", l, cg, s, o)]
            z.append(("hsplit", l, cg, s))
    out += z
    for j in range(NG):
        unit("gate", l, 1, j)
        unit("proj", l, 1, j)
    for g in range(NG):
        unit("fn", l, g)
        for s in streams:
            out += [("S1", l, g, s), ("S2", l, g, s)]
    for j in range(NG):
        unit("gate", l, 2, j)
        unit("proj", l, 2, j)
    unit("k", l)
    out += [("KR1", l)]
    unit("v", l)
    out += [("KR2", l), ("KR3", l)]
    items = []
    for j in range(4):
        unit("q", l, j)
        out.append(("QR", l, j))
        for i in range(2):
            for s in streams:
                for qc in range(2):
                    items.append((l, 2 * j + i, s, qc))
                    out.append(("SC",) + items[-1])
                    if len(items) > 1:
                        out.append(("TP",) + items[-2])
                    if len(items) > 2:
                        out.append(("PV",) + items[-3])
                    out.append(("SN",) + items[-1])
    out += [("TP",) + items[-1], ("PV",) + items[-2], ("PV",) + items[-1]]
    out.append(("xback", l))
    for j in range(NG):
        unit("gate", l, 0, j)
    for j in range(NG):
        unit("proj", l, 0, j)
        out.append(("msplit", l, j))
    while spare:
        out.append(spare.pop(0))
    if l == 0:
        out.append(("coefB", 0))
        out.append(("coefA", 1))
        out.append(("coefB", 1))
    for j in range(NG):
        unit("out", l, j)
    return out


def norm(l, which):
    out = [("lnm", l, which)]
    for c in range(NC):
        out.append(("lnd", l, which, c))
        out.append(("lnsq", l, which, c))
    out += [("lnv", l, which), ("lnb", l, which)]
    for c in range(NC):
        out.append(("lnn", l, which, c))
        out.append(("lnx", l, which, c))
    return out


def modulated(l, which):
    out = [("hb1", l, which, 0)]
    for c in range(NC):
        if c + 1 < NC:
            out.append(("hb1", l, which, c + 1))
        out.append(("hb2", l, which, c))
    return out


def mlp(l):
    out = []

    def up(g):
        for j in range(4):
            out.append(("mlp1", l, g, j))
            out.append(("msq", l, g, j))

    def down(g):
        for j in range(4):
            out.append(("mlp2", l, g, j))

    up(0)
    up(1)
    down(0)
    up(2)
    down(1)
    up(3)
    down(2)
    down(3)
    return out


def schedule():
    out = [("silu",)]
    out += [("ada", 0, j) for j in range(8)] + [("coefA", 0)] + modulated(0, 0)
    spare = [("ada", 0, j) for j in range(8, 24)] + [("ada", 1, j) for j in range(24)]
    for l in range(DEPTH):
        out += mixing(l, spare)
        out += norm(l, 0)
        out += modulated(l, 1)
        out += mlp(l)
        out += norm(l, 1)
        if l + 1 < DEPTH:
            out += [("xout", l)] + modulated(l + 1, 0)
    return out


SCHEDULE = schedule()
UNIT = ("ada", "hy", "gate", "proj", "fn", "k", "v", "q", "out", "mlp1", "mlp2")
AUX = ("f1", "f2", "K0", "K1", "KN", "T", "F", "I", "S1", "S2", "KR1", "KR2", "KR3", "QR", "SC", "TP", "PV",
       "lnm", "lnv", "lnb")
ACT_PART = ("silu", "ada", "hy", "gate", "fn", "k", "v", "q", "mlp1", "f1", "f2", "K0", "K1", "KN", "T", "F", "I",
            "S1", "S2", "KR1", "QR", "SC", "TP", "PV", "lnv", "lnsq", "lnx", "hb2", "msplit", "msq", "hsplit")
DVE_PART = ("silu", "hy", "proj", "out", "mlp1", "mlp2", "f1", "f2", "K0", "K1", "KN", "F", "I", "S2", "KR1", "KR2",
            "KR3", "QR", "SC", "SN", "PV", "lnm", "lnd", "lnv", "lnb", "lnn", "hb1", "hb2", "msplit", "msq",
            "hsplit", "coefA", "coefB", "hprep")
AT = {s: n for n, s in enumerate(SCHEDULE)}
UNITS = [s for s in SCHEDULE if s[0] in UNIT]
UNIT_NO = {s: n for n, s in enumerate(UNITS)}
AUXES = [s for s in SCHEDULE if s[0] in AUX]
AUX_NO = {s: n for n, s in enumerate(AUXES)}


def ends(part):
    n, out = 0, []
    for s in SCHEDULE:
        n += s[0] in part
        out.append(n)
    return out


ACT_ENDS = ends(ACT_PART)
DVE_ENDS = ends(DVE_PART)
assert len(AT) == len(SCHEDULE)


def build_program(nc, a, out_dram):
    es = ExitStack()
    with es:
        def sb(name, shape, dt=F32):
            return es.enter_context(nc.sbuf_tensor(name, shape, dt))

        def sem(name):
            return es.enter_context(nc.semaphore(name))

        raw = sb("raw", [P, RAW, UW])
        wh = sb("wh", [P, 2, UW], F32R)
        wl = sb("wl", [P, 2, UW], F32R)
        hh = sb("hh", [P, NC, T], F32R)
        hl = sb("hl", [P, NC, T], F32R)
        oh = sb("oh", [P, NC, T], F32R)
        ol = sb("ol", [P, NC, T], F32R)
        xs = sb("xs", [P, NC * T])
        ms = sb("ms", [P, NC * T])
        st = sb("st", [P, 4, T])
        cons = sb("cons", [P, NCON])
        vecs = sb("vecs", [P, DEPTH, NVEC])
        mods = sb("mods", [P, DEPTH, 6 * NC, 2])
    

        scale1 = sb("scale1", [P, DEPTH, 2, NC, 2])
        gateb = sb("gateb", [P, DEPTH, 2, NC, 2])
        gainb = sb("gainb", [P, DEPTH, NH + NKV])
        cvec = sb("cvec", [P, NC, 2])
        csig = sb("csig", [P, NC, 2])
        sh = sb("sh", [P, NC, 2], F32R)
        sl = sb("sl", [P, NC, 2], F32R)
        fw1 = sb("fw1", [EMB, DEPTH, FH])
        fw2 = sb("fw2", [FH, DEPTH, FH])
        bv = sb("bv", [1, DEPTH, NKV * HEAD])
        fh1 = sb("fh1", [FH, S])
        fh2 = sb("fh2", [FH, S])
        ksc = sb("ksc", [P, 2, 2])
        small = sb("small", [P, 64])
        inner = ExitStack()
        s2 = inner.enter_context(nc.sbuf_tensor("s2", [P, 2 * NC * T], F32))
        inner.close()
        bh = sb("bh", [P, NC, T], F32R)
        bl = sb("bl", [P, NC, T], F32R)

        gemm = es.enter_context(nc.psum_tensor("gemm", [P, 4, T], F32))
        aux = es.enter_context(nc.psum_tensor("aux", [P, 2, 2, T], F32))

        raw_in = [sem(f"raw_in{i}") for i in range(RAW)]
        x_in = sem("x_in")
        vec_in = sem("vec_in")
        filt_in = sem("filt_in")
        xback_in = sem("xback_in")
        x_kept = sem("x_kept")
        hi_made = sem("hi_made")
        lo_made = sem("lo_made")
        unit_summed = sem("unit_summed")
        aux_summed = sem("aux_summed")
        act_step_done = sem("act_step_done")
        dve_step_done = sem("dve_step_done")
        act_chain = sem("act_chain")
        dve_chain = sem("dve_chain")
        stored = sem("stored")

        x_kept_dram = nc.dram_tensor("x_kept_dram", (P, NC, T), F32, kind="Internal").ap()

        X = xs[:, :].rearrange("p (c t) -> p c t", c=NC)
        M = ms[:, :].rearrange("p (c t) -> p c t", c=NC)

        def con(name, n, parts=P):
            return cons[0:parts, CON[name]:CON[name] + n]

        def vec(l, name, i=0, parts=P):
            return vecs[0:parts, l, VEC[name] + i:VEC[name] + i + 1]

        fwd = con("hy_fwd", 4 * P).rearrange("p (c a k) -> p c a k", c=2, a=2)
        inv = con("hy_inv", 4 * P).rearrange("p (c a k) -> p c a k", c=2, a=2)
        fcs = con("fnet", 4 * S).rearrange("p (k c n) -> p k c n", k=2, c=2)
        rope_c = con("rope_cos", S)
        rope_s = con("rope_sin", S)
        swap = con("swap", P)
        ident = con("ident", P)
        ones = con("ones", P)
        mean = con("mean", P)

        pad = s2[:, 0:1032].rearrange("p (i s t) -> p i s t", i=2, s=2)
        hyu = [s2[:, 1040 + 3072 * b:1040 + 3072 * (b + 1)].rearrange("p (x i t) -> p x i t", x=3, i=2) for b in (0, 1)]
        kf = xs[:, 0:2048].rearrange("p (o h c n) -> p o h c n", o=2, h=2, c=2)
        zt = xs[:, 2048:2560].rearrange("p (a n) -> p a n", a=2)
        ec = xs[:, 2560:3072]
        dec = xs[:, 3072:3584].rearrange("p (a n) -> p a n", a=2)
        hu = ms[:, 0:1024].rearrange("p (h c n) -> p h c n", h=2, c=2)
        ht = ms[:, 1024:2048].rearrange("p (h c n) -> p h c n", h=2, c=2)
        hy_y = ms[:, 2048:3072].rearrange("p (h c n) -> p h c n", h=2, c=2)
        w3 = ms[0:FH, 3072:4096].rearrange("p (o n) -> p o n", o=2)
        G = s2[:, 0:4096].rearrange("p (i t) -> p i t", i=NC)
        gtmp = s2[:, 4096:5120].rearrange("p (i t) -> p i t", i=2)
        pf = [xs[:, 1024 * b:1024 * (b + 1)].rearrange("p (i t) -> p i t", i=2) for b in (0, 1)]
        xcs = [xs[:, 2048 + 1024 * b:3072 + 1024 * b].rearrange("p (t c n) -> p t c n", t=2, c=2) for b in (0, 1)]
        K = xs[:, 0:1024].rearrange("p (g t) -> p g t", g=2)
        V = xs[:, 1024:2048].rearrange("p (t n) -> p t n", t=4)
        PR = [xs[:, 2048 + 512 * b:2560 + 512 * b] for b in (0, 1)]
        PT = [xs[:, 3072 + 512 * b:3584 + 512 * b].rearrange("p (k q) -> p k q", k=4) for b in (0, 1)]
        QG = [s2[:, 1024 * b:1024 * (b + 1)].rearrange("p (i t) -> p i t", i=2) for b in (0, 1)]
        QSQ = s2[:, 2048:3072].rearrange("p (i t) -> p i t", i=2)
        RT = s2[:, 3072:4096].rearrange("p (k i t) -> p k i t", k=2, i=2)
        DG = s2[:, 4096:5120].rearrange("p (k t) -> p k t", k=8)
        rk = small[:, 0:8]
        rq = [small[:, 8:16], small[:, 16:24]]
        nmax = [small[:, 24:25], small[:, 25:26]]
        nbias = [small[:, 26:27], small[:, 27:28]]
        rsum = [small[:, 28:29], small[:, 29:30]]
        rinv = [small[:, 30:31], small[:, 31:32]]
        lnr = small[:, 32:36]
        ksn = small[:, 36:38]

        def cols(l):
            return slice(0, T) if l == 0 else slice(S, T)

        def streams(l):
            return (0, 1) if l == 0 else (1,)

        def toks(l):
            return range(4) if l == 0 else range(2, 4)

        def tok(s):
            return slice(s * S, s * S + S)

        def hidden(g):
            return (oh, ol) if g % 2 == 0 else (bh, bl)

        def acts(step):
            return ACT_ENDS[AT[step]]

        def dves(step):
            return DVE_ENDS[AT[step]]

        def units(step):
            return UNIT_NO[step] + 1

        def auxes(step):
            return AUX_NO[step] + 1

        def bank(step):
            return aux[:, AUX_NO[step] % 2]

        block = es.enter_context(nc.Block())

        @block.sync
        def _(sp):
            for u in range(len(UNITS)):
                if u >= RAW:
                    sp.wait_ge(hi_made, u - RAW + 1)
                    sp.wait_ge(lo_made, u - RAW + 1)
                sp.dma_start(raw[:, u % RAW], a["wts"][u]).then_inc(raw_in[u % RAW], 16)

        @block.gpsimd
        def _(pool):
            pool.dma_start(cvec[:], a["ct"]).then_inc(vec_in, 16)
            pool.dma_start(vecs[:], a["vecs"]).then_inc(vec_in, 16)
            pool.dma_start(cons[:], a["cons"]).then_inc(vec_in, 16)
            pool.dma_start(fw1[:], a["fw1"]).then_inc(vec_in, 16)
            pool.dma_start(fw2[:], a["fw2"]).then_inc(vec_in, 16)
            pool.dma_start(bv[:], a["bv"]).then_inc(vec_in, 16)
            pool.dma_start(X, a["xt"]).then_inc(x_in, 16)
            for n, s in enumerate(SCHEDULE):
                if s[0] == "hprep":
                    l = s[1]
                    for cg in range(NG):
                        if cg == 0:
                            pool.wait_ge(dve_step_done, dves(("hb2", l, 0, NC - 1)))
                            if l:
                                pool.wait_ge(x_kept, 16)
                        else:
                            pool.wait_ge(dve_step_done, dves(("K0", l, cg - 1, 1)))
                        pool.dma_start(w3, a["fw3"][l, cg]).then_inc(filt_in, 16)
                        pool.dma_start(dec, a["dec"][cg]).then_inc(filt_in, 16)
                elif s[0] == "xback":
                    l = s[1]
                    pool.wait_ge(dve_step_done, dves(("PV", l, NH - 1, 1, 1)))
                    pool.dma_start(X, a["xt"] if l == 0 else x_kept_dram).then_inc(xback_in, 16)
                elif s[0] == "xout":
                    pool.wait_ge(act_step_done, acts(("lnx", s[1], 1, NC - 1)))
                    pool.dma_start(x_kept_dram, X).then_inc(x_kept, 16)
            pool.wait_ge(act_step_done, acts(("lnx", DEPTH - 1, 1, NC - 1)))
            pool.dma_start(out_dram, X[:, :, S:T]).then_inc(stored, 16)
            pool.wait_ge(stored, 16)

        @block.tensor
        def _(pe):
            mm = nc.tensor.matmul

            def wait_operands(s):
                kind, l = s[0], s[1]
                if kind == "ada":
                    pe.wait_ge(dve_step_done, dves(("silu",)))
                elif kind == "proj":
                    b = s[2]
                    last = {1: ("hsplit", l, NG - 1, 1), 2: ("S2", l, NG - 1, 1), 0: ("PV", l, NH - 1, 1, 1)}[b]
                    pe.wait_ge(dve_step_done, dves(last))
                elif kind == "out":
                    pe.wait_ge(dve_step_done, dves(("msplit", l, NG - 1)))
                elif kind == "mlp1":
                    pe.wait_ge(dve_step_done, dves(("hb2", l, 1, NC - 1)))
                elif kind == "mlp2":
                    pe.wait_ge(dve_step_done, dves(("msq", l, s[2], 3)))
                else:
                    pe.wait_ge(dve_step_done, dves(("hb2", l, 0, NC - 1)))

            def unit(s):
                kind, l = s[0], s[1]
                u = UNIT_NO[s]
                pe.wait_ge(lo_made, u + 1)
                if u >= 2:
                    before = UNITS[u - 2]
                    if before[0] in ACT_PART:
                        pe.wait_ge(act_step_done, acts(before))
                    if before[0] in DVE_PART:
                        pe.wait_ge(dve_step_done, dves(before))
                wait_operands(s)
                W = [w[:, u % 2].rearrange("p (k n) -> p k n", k=NC) for w in (wh, wl)]
                if kind == "v":
                    for t in range(4):
                        dst = gemm[:, 2 * (u % 2) + t // 2, (t % 2) * UC:(t % 2 + 1) * UC]
                        ts = slice(t * P, t * P + P)
                        mm(dst, ones[0:1, :], bv[0:1, l], start=True, stop=False)
                        for k in range(NC):
                            mm(dst, hl[:, k, ts], W[0][:, k], start=False, stop=False)
                            mm(dst, hh[:, k, ts], W[0][:, k], start=False, stop=False)
                            last = mm(dst, hh[:, k, ts], W[1][:, k], start=False, stop=(k == NC - 1))
                    last.then_inc(unit_summed, 1)
                    return
                if kind == "ada":
                    mh, ml, cs = sh, sl, slice(0, 2)
                elif kind == "proj":
                    mh, ml, cs = oh, ol, cols(l)
                elif kind == "mlp2":
                    mh, ml = hidden(s[2])
                    cs = cols(l)
                else:
                    mh, ml, cs = hh, hl, cols(l)
                if kind == "k":
                    cs = slice(0, T)
                for i in range(2):
                    dst = gemm[:, 2 * (u % 2) + i, cs]
                    ws = slice(i * P, i * P + P)
                    for k in range(NC):
                        mm(dst, W[1][:, k, ws], mh[:, k, cs], start=(k == 0), stop=False)
                        mm(dst, W[0][:, k, ws], mh[:, k, cs], start=False, stop=False)
                        last = mm(dst, W[0][:, k, ws], ml[:, k, cs], start=False, stop=(k == NC - 1))
                last.then_inc(unit_summed, 1)

            def aux_step(s):
                kind, l = s[0], s[1]
                n = AUX_NO[s]
                A = bank(s)
                if n >= 2:
                    before = AUXES[n - 2]
                    if before[0] in ACT_PART:
                        pe.wait_ge(act_step_done, acts(before))
                    if before[0] in DVE_PART:
                        pe.wait_ge(dve_step_done, dves(before))
                if kind == "f1":
                    pe.wait_ge(vec_in, 96)
                    last = mm(A[0:FH, 0, 0:S], fw1[:, l], con("emb", S, EMB), start=True, stop=True)
                elif kind == "f2":
                    pe.wait_ge(act_step_done, acts(("f1", l)))
                    last = mm(A[0:FH, 0, 0:S], fw2[:, l], fh1[:], start=True, stop=True)
                elif kind == "K0":
                    _, _, cg, o = s
                    pe.wait_ge(act_step_done, acts(("f2", l)))
                    pe.wait_ge(filt_in, 32 * (NG * l + cg + 1))
                    for par in range(2):
                        last = mm(A[:, par], fh2[:, par * P:par * P + P], w3[:, o], start=True, stop=True)
                elif kind == "KN":
                    _, _, cg, o = s
                    pe.wait_ge(act_step_done, acts(("K0", l, cg, o)))
                    sq = hy_y
                    for i in range(2):
                        for q in range(4):
                            last = mm(A[:, 0, i:i + 1], sq[:, q // 2, q % 2, i * P:i * P + P], ones[:, 0:1],
                                      start=(q == 0), stop=(q == 3))
                elif kind == "K1":
                    _, _, cg, o = s
                    pe.wait_ge(dve_step_done, dves(("K0", l, cg, o)))
                    for par in range(2):
                        for c in range(2):
                            last = mm(A[:, par, c * UC:(c + 1) * UC], fwd[:, c, par], hu[:, c, par],
                                      start=True, stop=True)
                elif kind == "T":
                    _, _, cg, st_, o = s
                    if o == 0:
                        pe.wait_ge(dve_step_done, dves(("hy", l, cg, 1)))
                    else:
                        pe.wait_ge(dve_step_done, dves(("I", l, cg, st_, 0)))
                    z = hyu[cg % 2][:, 2]
                    for par in range(2):
                        for i in range(2):
                            src = z[:, i, tok(st_)].rearrange("p (t a) -> p a t", a=2)[:, par]
                            last = nc.tensor.transpose(A[:, 0, par * UC + i * P:par * UC + (i + 1) * P], src, ident)
                elif kind == "F":
                    pe.wait_ge(act_step_done, acts(("T",) + s[1:]))
                    for par in range(2):
                        for c in range(2):
                            last = mm(A[:, par, c * UC:(c + 1) * UC], fwd[:, c, par], zt[:, par],
                                      start=True, stop=True)
                elif kind == "I":
                    pe.wait_ge(dve_step_done, dves(("F",) + s[1:]))
                    for i in range(2):
                        for par in range(2):
                            for c in range(2):
                                last = mm(A[:, 0, (2 * i + par) * P:(2 * i + par + 1) * P],
                                          hu[:, par, c, i * P:i * P + P], inv[:, c, par],
                                          start=(c == 0), stop=(c == 1))
                elif kind == "S1":
                    _, _, g, st_ = s
                    pe.wait_ge(act_step_done, acts(("fn", l, g)))
                    for t in range(2):
                        for k in range(2):
                            last = mm(A[:, t], pf[g % 2][:, k, st_ * S + t * P:st_ * S + (t + 1) * P], fcs[:, k],
                                      start=(k == 0), stop=(k == 1))
                elif kind == "S2":
                    _, _, g, st_ = s
                    pe.wait_ge(act_step_done, acts(("S1", l, g, st_)))
                    for i in range(2):
                        for t in range(2):
                            for c in range(2):
                                last = mm(A[:, 0, i * S:(i + 1) * S], xcs[st_][:, t, c, i * P:i * P + P],
                                          fcs[:, t, c], start=(t == 0 and c == 0), stop=(t == 1 and c == 1))
                elif kind in ("KR1", "QR"):
                    if kind == "QR":
                        j = s[2]
                        pe.wait_ge(act_step_done, acts(("q", l, j)))
                        r = toks(l)
                    else:
                        pe.wait_ge(act_step_done, acts(("k", l)))
                        r = range(4)
                    for i in range(2):
                        for t in r:
                            last = mm(A[:, 0, 4 * i + t:4 * i + t + 1], QSQ[:, i, t * P:t * P + P], ones[:, 0:1],
                                      start=True, stop=True)
                    if kind == "QR":
                        for i in range(2):
                            last = mm(A[:, 1, i * S:(i + 1) * S], swap, QG[j % 2][:, i, S:T], start=True, stop=True)
                elif kind == "KR2":
                    pe.wait_ge(dve_step_done, dves(("KR1", l)))
                    for i in range(2):
                        for t in range(4):
                            last = mm(A[:, i, t * P:t * P + P], ones, DG[:, 4 * i + t], start=True, stop=True)
                elif kind == "KR3":
                    pe.wait_ge(dve_step_done, dves(("KR2", l)))
                    for i in range(2):
                        last = mm(A[:, 0, i * S:(i + 1) * S], swap, K[:, i, S:T], start=True, stop=True)
                elif kind == "SC":
                    _, _, h, st_, qc = s
                    pe.wait_ge(dve_step_done, dves(("QR", l, h // 2)))
                    pe.wait_ge(dve_step_done, dves(("KR3", l)))
                    at = st_ * S + qc * P
                    keys = slice(0, T) if st_ else slice(0, S)
                    last = mm(A[:, 0, keys], QG[h // 2 % 2][:, h % 2, at:at + P], K[:, h // 4, keys],
                              start=True, stop=True)
                elif kind == "TP":
                    _, _, h, st_, qc = s
                    pe.wait_ge(dve_step_done, dves(("SN",) + s[1:]))
                    for kc in range(4 if st_ else 2):
                        last = nc.tensor.transpose(A[:, 0, kc * P:kc * P + P], PR[qc][:, kc * P:kc * P + P], ident)
                elif kind == "PV":
                    _, _, h, st_, qc = s
                    pe.wait_ge(act_step_done, acts(("TP",) + s[1:]))
                    pe.wait_ge(act_step_done, acts(("v", l)))
                    n = 4 if st_ else 2
                    for kc in range(n):
                        last = mm(A[:, 0, 0:P], V[:, kc, h // 4 * P:h // 4 * P + P], PT[qc][:, kc],
                                  start=(kc == 0), stop=(kc == n - 1))
                elif kind == "lnm":
                    which = s[2]
                    for c in range(NC):
                        pe.wait_ge(dve_step_done, dves(("mlp2", l, 3, c // 2) if which else ("out", l, c // 2)))
                        last = mm(A[:, 0, cols(l)], mean, X[:, c, cols(l)], start=(c == 0), stop=(c == NC - 1))
                elif kind == "lnv":
                    which = s[2]
                    for c in range(NC):
                        pe.wait_ge(act_step_done, acts(("lnsq", l, which, c)))
                        for t in toks(l):
                            last = mm(A[:, 0, t:t + 1], M[:, c, t * P:t * P + P], ones[:, 0:1],
                                      start=(c == 0 and t == toks(l)[0]), stop=(c == NC - 1),
                                      skip_group_check=True)
                elif kind == "lnb":
                    which = s[2]
                    pe.wait_ge(dve_step_done, dves(("lnv", l, which)))
                    for t in toks(l):
                        last = mm(A[:, 0, t * P:t * P + P], ones, st[:, 3, t * P:t * P + P], start=True, stop=True)
                last.then_inc(aux_summed, 1)

            for s in SCHEDULE:
                if s[0] in UNIT:
                    unit(s)
                elif s[0] in AUX:
                    aux_step(s)

        @block.scalar
        def _(act):
            act_fn = nc.scalar.activation
            done = {"chain": 0}

            def link(ins):
                ins.then_inc(act_chain, 1)
                done["chain"] += 1
                act.wait_ge(act_chain, done["chain"])

            def hi(u):
                act.wait_ge(raw_in[u % RAW], 16 * (u // RAW + 1))
                if u >= 2:
                    act.wait_ge(unit_summed, u - 1)
                    act.wait_ge(lo_made, u - 1)
                act_fn(wh[:, u % 2], raw[:, u % RAW], ACT.Copy).then_inc(hi_made, 1)

            def part(s):
                kind = s[0]
                l = s[1] if len(s) > 1 else 0
                cs = cols(l)
                last = None
                if kind in UNIT:
                    u = UNIT_NO[s]
                    act.wait_ge(unit_summed, units(s))
                    g = [gemm[:, 2 * (u % 2) + i] for i in range(2)]
                elif kind in AUX:
                    act.wait_ge(aux_summed, auxes(s))
                    A = bank(s)
                if kind == "silu":
                    act.wait_ge(vec_in, 96)
                    last = act_fn(csig[:], cvec[:], ACT.Sigmoid)
                elif kind == "ada":
                    j = s[2]
                    for i in range(2):
                        last = act_fn(mods[:, l, 2 * j + i], g[i][:, 0:2], ACT.Identity,
                                      bias=vec(l, "b_ada", 2 * j + i))
                elif kind == "hy":
                    _, _, cg, part_ = s
                    before = {(2): (cg - 1, 1), (0): (cg, 2), (1): (cg, 0)}[part_]
                    act.wait_ge(dve_step_done, dves(("hy", l) + before if before[0] >= 0 else ("hprep", l)))
                    for i in range(2):
                        b = vec(l, "b_in", OFF_HY // P + NC * part_ + 2 * cg + i)
                        n0, n1 = (0, 2) if l == 0 else (1, 2)
                        last = act_fn(pad[:, i, n0:n1, 1:S + 1],
                                      g[i][:, cs].rearrange("p (s t) -> p s t", t=S), ACT.Identity, bias=b)
                elif kind == "gate":
                    _, _, b, j = s
                    if j == 0:
                        act.wait_ge(dve_step_done, dves({1: ("hsplit", l, NG - 1, 1), 2: ("S2", l, NG - 1, 1),
                                          0: ("PV", l, NH - 1, 1, 1)}[b]))
                    for i in range(2):
                        last = act_fn(G[:, 2 * j + i, cs], g[i][:, cs], ACT.Sigmoid,
                                      bias=vec(l, "b_in", OFF_G // P + NC * b + 2 * j + i))
                elif kind == "fn":
                    gr = s[2]
                    if gr == 0:
                        act.wait_ge(dve_step_done, dves(("hsplit", l, NG - 1, 1)))
                    for i in range(2):
                        last = act_fn(pf[gr % 2][:, i, cs], g[i][:, cs], ACT.Identity,
                                      bias=vec(l, "b_in", OFF_FN // P + 2 * gr + i))
                elif kind in ("k", "q"):
                    if kind == "k":
                        c0, dst, gain, cs = OFF_K // P, K, vec(l, "k_gain"), slice(0, T)
                        act.wait_ge(dve_step_done, dves(("proj", l, 2, NG - 1)))
                        gb = NH
                    else:
                        j = s[2]
                        c0, dst, gain = 2 * j, QG[j % 2], vec(l, "q_gain")
                        gb = 2 * j
                        if j >= 2:
                            act.wait_ge(aux_summed, auxes(("SC", l, 2 * j - 3, 1, 1)))
                    for i in range(2):
                        act_fn(QSQ[:, i, cs], g[i][:, cs], ACT.Square,
                               bias=vec(l, "b_in", c0 + i)).then_inc(act_chain, 1)
                        done["chain"] += 1
                        last = act_fn(dst[:, i, cs], g[i][:, cs], ACT.Identity, scale=gain,
                                      bias=gainb[:, l, gb + i:gb + i + 1])
                    act.wait_ge(act_chain, done["chain"])
                elif kind == "v":
                    act.wait_ge(dve_step_done, dves(("proj", l, 2, NG - 1)))
                    for i in range(2):
                        last = act_fn(V[:, 2 * i:2 * i + 2], g[i].rearrange("p (t n) -> p t n", t=2), ACT.Copy)
                elif kind == "mlp1":
                    _, _, gr, j = s
                    act.wait_ge(dve_step_done, dves(SCHEDULE[AT[s] - 1]))
                    for i in range(2):
                        last = act_fn(st[:, i, cs], g[i][:, cs], ACT.Relu, bias=vec(l, "b_mlp1", 8 * gr + 2 * j + i))
                elif kind == "msq":
                    _, _, gr, j = s
                    if gr >= 2 and j == 0:
                        act.wait_ge(unit_summed, units(("mlp2", l, gr - 2, 3)))
                    if gr == 0 and j == 0:
                        act.wait_ge(unit_summed, units(("proj", l, 0, NG - 1)))
                    act.wait_ge(dve_step_done, dves(("mlp1", l, gr, j)))
                    for i in range(2):
                        last = act_fn(hidden(gr)[0][:, 2 * j + i, cs], st[:, 2 + i, cs], ACT.Copy)
                elif kind in ("f1", "f2"):
                    act.wait_ge(dve_step_done, dves(s))
                    last = act_fn((fh1 if kind == "f1" else fh2)[:], st[0:FH, 1, 0:S], ACT.Sin)
                elif kind == "K0":
                    act.wait_ge(dve_step_done, dves(s))
                    act_fn(hy_y[:, 0], hu[:, 0], ACT.Square).then_inc(act_chain, 1)
                    last = act_fn(hy_y[:, 1], hu[:, 1], ACT.Square)
                    done["chain"] += 1
                    act.wait_ge(act_chain, done["chain"])
                elif kind == "KN":
                    last = act_fn(ksn, A[:, 0, 0:2], ACT.Sqrt, scale=0.5, bias=con("epskern", 1))
                elif kind in ("K1", "F"):
                    last = act_fn(ec, A[:, 0], ACT.Copy)
                elif kind == "T":
                    last = act_fn(zt, A[:, 0].rearrange("p (a n) -> p a n", a=2), ACT.Copy)
                elif kind == "I":
                    _, _, cg, st_, o = s
                    for i in range(2):
                        last = act_fn(ht[:, 0, i].rearrange("p (t a) -> p a t", a=2),
                                      A[:, 0, i * UC:(i + 1) * UC].rearrange("p (a t) -> p a t", a=2),
                                      ACT.Identity, scale=ksc[:, o, i:i + 1])
                elif kind == "hsplit":
                    _, _, cg, st_ = s
                    act.wait_ge(dve_step_done, dves(("I", l, cg, st_, 1)))
                    if cg == 0 and st_ == streams(l)[0] and l:
                        act.wait_ge(unit_summed, units(("mlp2", l - 1, 2, 3)))
                    last = act_fn(oh[:, 2 * cg:2 * cg + 2, tok(st_)], hyu[cg % 2][:, 2, :, tok(st_)], ACT.Copy)
                elif kind == "S1":
                    _, _, gr, st_ = s
                    act_fn(xcs[st_][:, :, 0], A[:, :, 0:S], ACT.Copy, scale=1.0 / S).then_inc(act_chain, 1)
                    done["chain"] += 1
                    last = act_fn(xcs[st_][:, :, 1], A[:, :, S:T], ACT.Copy, scale=-1.0 / S)
                    act.wait_ge(act_chain, done["chain"])
                elif kind == "S2":
                    _, _, gr, st_ = s
                    if gr == 0 and st_ == streams(l)[0]:
                        act.wait_ge(unit_summed, units(("proj", l, 1, NG - 1)))
                    last = act_fn(oh[:, 2 * gr:2 * gr + 2, tok(st_)], A[:, 0].rearrange("p (i t) -> p i t", i=2),
                                  ACT.Copy)
                elif kind == "KR1":
                    last = act_fn(rk, A[:, 0, 0:8], ACT.Sqrt, scale=1.0 / HEAD, bias=con("epsrms", 1))
                elif kind == "QR":
                    j = s[2]
                    t0 = toks(l)[0]
                    last = act_fn(rq[j % 2].rearrange("p (i t) -> p i t", i=2)[:, :, t0:4],
                                  A[:, 0, 0:8].rearrange("p (i t) -> p i t", i=2)[:, :, t0:4],
                                  ACT.Sqrt, scale=1.0 / HEAD, bias=con("epsrms", 1))
                elif kind == "SC":
                    _, _, h, st_, qc = s
                    act.wait_ge(dve_step_done, dves(s))
                    keys = slice(0, T) if st_ else slice(0, S)
                    col = 4 * (h % 2) + 2 * st_ + qc
                    last = act_fn(PR[qc][:, keys], A[:, 0, keys], ACT.Exp, bias=nbias[qc],
                                  scale=rq[h // 2 % 2][:, col:col + 1], accum_out=rsum[qc])
                elif kind == "TP":
                    _, _, h, st_, qc = s
                    n = 4 if st_ else 2
                    last = act_fn(PT[qc][:, 0:n], A[:, 0, 0:n * P].rearrange("p (k q) -> p k q", k=n), ACT.Copy)
                elif kind == "PV":
                    _, _, h, st_, qc = s
                    if h == 0:
                        act.wait_ge(unit_summed, units(("proj", l, 2, NG - 1)))
                    at = st_ * S + qc * P
                    last = act_fn(oh[:, h, at:at + P], A[:, 0, 0:P], ACT.Copy)
                elif kind == "msplit":
                    _, _, j = s
                    if j == 0:
                        act.wait_ge(unit_summed, units(("gate", l, 0, NG - 1)))
                    act.wait_ge(dve_step_done, dves(("proj", l, 0, j)))
                    last = act_fn(hh[:, 2 * j:2 * j + 2, cs], M[:, 2 * j:2 * j + 2, cs], ACT.Copy)
                elif kind == "lnsq":
                    _, _, which, c = s
                    act.wait_ge(dve_step_done, dves(("lnd", l, which, c)))
                    last = act_fn(M[:, c, cs], X[:, c, cs], ACT.Square)
                elif kind == "lnv":
                    t0 = toks(l)[0]
                    last = act_fn(lnr[:, t0:4], A[:, 0, t0:4], ACT.Sqrt, scale=1.0 / D, bias=con("epsln", 1))
                elif kind == "lnx":
                    _, _, which, c = s
                    n = "ln2" if which else "ln1"
                    act.wait_ge(dve_step_done, dves(("lnn", l, which, c)))
                    last = act_fn(X[:, c, cs], X[:, c, cs], ACT.Identity, scale=vec(l, n + "_g", c),
                                  bias=vec(l, n + "_b", c))
                elif kind == "hb2":
                    _, _, which, c = s
                    if c == 0 and which:
                        act.wait_ge(unit_summed, units(("out", l, NG - 1)))
                    elif c == 0 and l:
                        act.wait_ge(unit_summed, units(("mlp1", l - 1, 3, 3)))
                    act.wait_ge(dve_step_done, dves(("hb1", l, which, c)))
                    full = slice(0, T) if not which else cs
                    last = act_fn(hh[:, c, full], st[:, c % 4, full], ACT.Copy)
                last.then_inc(act_step_done, 1)

            hi(0)
            hi(1)
            for s in SCHEDULE:
                if s[0] in UNIT:
                    u = UNIT_NO[s]
                    if u + 2 < len(UNITS):
                        hi(u + 2)
                if s[0] in ACT_PART:
                    part(s)

        @block.vector
        def _(dve):
            v = nc.vector
            done = {"chain": 0, "parts": 0}

            def link(ins):
                ins.then_inc(dve_chain, 1)
                done["chain"] += 1
                dve.wait_ge(dve_chain, done["chain"])

            def also(ins):
                ins.then_inc(dve_chain, 1)
                done["chain"] += 1

            def own(step=None):
                if done["chain"]:
                    dve.wait_ge(dve_chain, done["chain"])
                if done["parts"]:
                    dve.wait_ge(dve_step_done, done["parts"])

            def lo(u):
                dve.wait_ge(hi_made, u + 1)
                v.tensor_tensor(wl[:, u % 2], raw[:, u % RAW], wh[:, u % 2].bitcast(F32),
                                ALU.subtract).then_inc(lo_made, 1)

            def part(s):
                kind = s[0]
                l = s[1] if len(s) > 1 else 0
                cs = cols(l)
                if kind in UNIT:
                    u = UNIT_NO[s]
                    if kind in ACT_PART:
                        dve.wait_ge(act_step_done, acts(s))
                    dve.wait_ge(unit_summed, units(s))
                    g = [gemm[:, 2 * (u % 2) + i] for i in range(2)]
                elif kind in AUX:
                    dve.wait_ge(aux_summed, auxes(s))
                    A = bank(s)
                own()
                last = None
                if kind == "silu":
                    dve.wait_ge(act_step_done, acts(s))
                    link(v.tensor_tensor(csig[:], csig[:], cvec[:], ALU.mult))
                    link(v.tensor_copy(sh[:], csig[:]))
                    last = v.tensor_tensor(sl[:], csig[:], sh[:].bitcast(F32), ALU.subtract)
                elif kind == "coefA":
                    dve.wait_ge(act_step_done, acts(("ada", l, 7)))
                    for j in range(2):
                        b, n, gn = (VEC["b_in"], NH, "q_gain") if j == 0 else (VEC["b_in"] + OFF_K // P, NKV, "k_gain")
                        also(v.tensor_scalar(gainb[:, l, j * NH:j * NH + n], vecs[:, l, b:b + n], vec(l, gn), None,
                                             ALU.mult))
                    last = v.tensor_scalar(scale1[:, l, 0], mods[:, l, NC:2 * NC], 1.0, None, ALU.add)
                elif kind == "coefB":
                    dve.wait_ge(act_step_done, acts(("ada", l, 23)))
                    for m, n in ((2, "b_out"), (5, "b_mlp2")):
                        for x in range(2):
                            also(v.tensor_tensor(gateb[:, l, m // 3, :, x], mods[:, l, m * NC:(m + 1) * NC, x],
                                                 vecs[:, l, VEC[n]:VEC[n] + NC], ALU.mult))
                    last = v.tensor_scalar(scale1[:, l, 1], mods[:, l, 4 * NC:5 * NC], 1.0, None, ALU.add)
                elif kind == "hprep":
                    dve.wait_ge(dve_step_done, dves(("hb2", l, 0, NC - 1)))
                    if l:
                        dve.wait_ge(unit_summed, units(("mlp2", l - 1, 3, 3)))
                    also(v.memset(pad[:, :, :, 0:1], 0.0))
                    last = v.memset(pad[:, :, :, S + 1:S + 2], 0.0)
                elif kind == "hb1":
                    _, _, which, c = s
                    if which == 0 and l == 0 and c == 0:
                        dve.wait_ge(x_in, 16)
                    elif c == 0:
                        dve.wait_ge(act_step_done, acts(("lnx", l, 0, 0) if which else ("lnx", l - 1, 1, 0)))
                    if not (which == 0 and l == 0):
                        dve.wait_ge(act_step_done, acts(("lnx", l, 0, c) if which else ("lnx", l - 1, 1, c)))
                    if c >= 4:
                        dve.wait_ge(act_step_done, acts(("hb2", l, which, c - 4)))
                    ss = (0, 1) if which == 0 else streams(l)
                    for x in ss:
                        ins = v.tensor_scalar(st[:, c % 4, tok(x)], X[:, c, tok(x)], scale1[:, l, which, c, x:x + 1],
                                              mods[:, l, 3 * which * NC + c, x:x + 1], ALU.mult, ALU.add)
                        if x != ss[-1]:
                            also(ins)
                    last = ins
                elif kind == "hb2":
                    _, _, which, c = s
                    dve.wait_ge(act_step_done, acts(s))
                    full = slice(0, T) if not which else cs
                    last = v.tensor_tensor(hl[:, c, full], st[:, c % 4, full], hh[:, c, full].bitcast(F32),
                                           ALU.subtract)
                elif kind == "hy":
                    _, _, cg, part_ = s
                    u_ = hyu[cg % 2]
                    n0, n1 = (0, 2) if l == 0 else (1, 2)
                    src = lambda i, k: pad[:, i, n0:n1, k:k + S]
                    w = lambda i, k: vec(l, "conv_w", 3 * NC * k + NC * part_ + 2 * cg + i)
                    dst = lambda i: u_[:, part_, i, cs].rearrange("p (s t) -> p s t", t=S)
                    for i in range(2):
                        also(v.tensor_scalar(dst(i), src(i, 0), w(i, 0), vec(l, "conv_b", NC * part_ + 2 * cg + i),
                                             ALU.mult, ALU.add))
                    own()
                    for i in range(2):
                        also(v.scalar_tensor_tensor(out=dst(i), in0=src(i, 1), scalar=w(i, 1), in1=dst(i),
                                                    op0=ALU.mult, op1=ALU.add))
                    own()
                    for i in range(2):
                        last = v.scalar_tensor_tensor(out=dst(i), in0=src(i, 2), scalar=w(i, 2), in1=dst(i),
                                                      op0=ALU.mult, op1=ALU.add)
                        if i == 0:
                            also(last)
                elif kind == "proj":
                    _, _, b, j = s
                    dve.wait_ge(act_step_done, acts(("gate", l, b, j)))
                    for i in range(2):
                        c = 2 * j + i
                        if b == 1:
                            last = v.tensor_tensor(M[:, c, cs], g[i][:, cs], G[:, c, cs], ALU.mult)
                            if i == 0:
                                also(last)
                        else:
                            also(v.tensor_tensor(gtmp[:, i, cs], g[i][:, cs], G[:, c, cs], ALU.mult))
                    if b != 1:
                        own()
                        last = v.tensor_tensor(M[:, 2 * j:2 * j + 2, cs], M[:, 2 * j:2 * j + 2, cs], gtmp[:, :, cs],
                                               ALU.add)
                elif kind == "msplit":
                    _, _, j = s
                    dve.wait_ge(act_step_done, acts(s))
                    last = v.tensor_tensor(hl[:, 2 * j:2 * j + 2, cs], M[:, 2 * j:2 * j + 2, cs],
                                           hh[:, 2 * j:2 * j + 2, cs].bitcast(F32), ALU.subtract)
                elif kind == "out":
                    _, _, j = s
                    if j == 0:
                        dve.wait_ge(xback_in, 16 * (l + 1))
                    residual(l, 0, j, lambda i: g[i])
                    return
                elif kind == "mlp1":
                    dve.wait_ge(act_step_done, acts(s))
                    if AT[s] and SCHEDULE[AT[s] - 1][0] == "msq":
                        pass
                    last = v.tensor_tensor(st[:, 2:4, cs], st[:, 0:2, cs], st[:, 0:2, cs], ALU.mult)
                elif kind == "msq":
                    _, _, gr, j = s
                    dve.wait_ge(act_step_done, acts(s))
                    h, lo_ = hidden(gr)
                    last = v.tensor_tensor(lo_[:, 2 * j:2 * j + 2, cs], st[:, 2:4, cs],
                                           h[:, 2 * j:2 * j + 2, cs].bitcast(F32), ALU.subtract)
                elif kind == "mlp2":
                    _, _, gr, j = s
                    for i in range(2):
                        c = 2 * j + i
                        if gr == 0:
                            last = v.tensor_copy(M[:, c, cs], g[i][:, cs])
                        else:
                            last = v.tensor_tensor(M[:, c, cs], g[i][:, cs], M[:, c, cs], ALU.add)
                        if i == 0 or gr == 3:
                            also(last)
                    if gr == 3:
                        own()
                        residual(l, 1, j, lambda i: M[:, 2 * j + i])
                        return
                elif kind in ("f1", "f2"):
                    n = "1" if kind == "f1" else "2"
                    src = A[0:FH, 0, 0:S]
                    ar, rn = st[0:FH, 0, 0:S], st[0:FH, 1, 0:S]
                    if kind == "f1":
                        dve.wait_ge(dve_step_done, dves(("hb2", l, 0, NC - 1)))
                    link(v.tensor_scalar(ar, src, vec(l, "hy_b" + n, 0, FH), vec(l, "hy_freq" + n, 0, FH),
                                         ALU.add, ALU.mult))
                    link(v.tensor_scalar(rn, ar, 1.0 / TWO_PI, ROUND, ALU.mult, ALU.add))
                    link(v.tensor_scalar(rn, rn, ROUND, None, ALU.subtract))
                    link(v.scalar_tensor_tensor(out=ar, in0=rn, scalar=-PI_HI, in1=ar, op0=ALU.mult, op1=ALU.add))
                    link(v.scalar_tensor_tensor(out=ar, in0=rn, scalar=-PI_LO, in1=ar, op0=ALU.mult, op1=ALU.add))
                    last = v.tensor_scalar(rn, ar, BELOW_PI, -BELOW_PI, ALU.min, ALU.max)
                elif kind == "K0":
                    _, _, cg, o = s
                    dve.wait_ge(filt_in, 32 * (NG * l + cg + 1))
                    f, b = ht[:, 0], ht[:, 1]
                    also(v.tensor_tensor(f, A[:, :, 0:UC], dec, ALU.mult))
                    also(v.scalar_tensor_tensor(out=b[:, 0], in0=A[:, 0, UC:T], scalar=con("notfirst", 1),
                                                in1=dec[:, 0], op0=ALU.mult, op1=ALU.mult))
                    also(v.tensor_tensor(b[:, 1], A[:, 1, UC:T], dec[:, 1], ALU.mult))
                    own()
                    also(v.tensor_tensor(hu[:, 0], f, b, ALU.add))
                    last = v.tensor_tensor(hu[:, 1], f, b, ALU.subtract)
                elif kind == "KN":
                    _, _, cg, o = s
                    dve.wait_ge(act_step_done, acts(s))
                    link(v.reciprocal(ksn, ksn))
                    last = v.tensor_scalar(ksc[:, o], ksn, 1.0 / S, None, ALU.mult)
                elif kind in ("K1", "F"):
                    dve.wait_ge(act_step_done, acts(s))
                    U = kf[:, s[3]] if kind == "K1" else hu
                    flat = lambda x: x.rearrange("p c n -> p (c n)")
                    also(v.tensor_tensor(flat(U[:, 0]), ec, A[:, 1], ALU.add))
                    ins = v.tensor_tensor(flat(U[:, 1]), ec, A[:, 1], ALU.subtract)
                    if kind == "K1":
                        last = ins
                    else:
                        o = s[4]
                        also(ins)
                        own()
                        Kf = kf[:, o]
                        link(v.tensor_tensor(ht, U, Kf, ALU.mult))
                        link(v.tensor_tensor(hy_y[:, :, 0], ht[:, :, 0], ht[:, :, 1], ALU.subtract))
                        for c in range(2):
                            also(v.tensor_tensor(ht[:, :, c], U[:, :, c], Kf[:, :, 1 - c], ALU.mult))
                        own()
                        link(v.tensor_tensor(hy_y[:, :, 1], ht[:, :, 0], ht[:, :, 1], ALU.add))
                        also(v.tensor_tensor(U[:, 0], hy_y[:, 0], hy_y[:, 1], ALU.add))
                        last = v.tensor_tensor(U[:, 1], hy_y[:, 0], hy_y[:, 1], ALU.subtract)
                elif kind == "I":
                    _, _, cg, st_, o = s
                    dve.wait_ge(act_step_done, acts(s))
                    u_ = hyu[cg % 2]
                    for i in range(2):
                        also(v.scalar_tensor_tensor(out=ht[:, 1, i], in0=u_[:, 2, i, tok(st_)],
                                                    scalar=vec(l, "hy_skip", NC * o + 2 * cg + i), in1=ht[:, 0, i],
                                                    op0=ALU.mult, op1=ALU.add))
                    own()
                    last = v.tensor_tensor(u_[:, 2, :, tok(st_)], ht[:, 1], u_[:, o, :, tok(st_)], ALU.mult)
                elif kind == "hsplit":
                    _, _, cg, st_ = s
                    dve.wait_ge(act_step_done, acts(s))
                    last = v.tensor_tensor(ol[:, 2 * cg:2 * cg + 2, tok(st_)], hyu[cg % 2][:, 2, :, tok(st_)],
                                           oh[:, 2 * cg:2 * cg + 2, tok(st_)].bitcast(F32), ALU.subtract)
                elif kind == "S2":
                    _, _, gr, st_ = s
                    dve.wait_ge(act_step_done, acts(s))
                    last = v.tensor_tensor(ol[:, 2 * gr:2 * gr + 2, tok(st_)],
                                           A[:, 0].rearrange("p (i t) -> p i t", i=2),
                                           oh[:, 2 * gr:2 * gr + 2, tok(st_)].bitcast(F32), ALU.subtract)
                elif kind == "KR1":
                    dve.wait_ge(act_step_done, acts(s))
                    link(v.reciprocal(rk, rk))
                    for t in range(8):
                        last = v.tensor_scalar(DG[:, t], ident, rk[:, t:t + 1], None, ALU.mult)
                        if t < 7:
                            also(last)
                elif kind == "KR2":
                    last = v.tensor_tensor(K, K, A, ALU.mult)
                elif kind in ("KR3", "QR"):
                    X2 = K if kind == "KR3" else QG[s[2] % 2]
                    R_ = A[:, 0 if kind == "KR3" else 1].rearrange("p (i t) -> p i t", i=2)
                    if kind == "QR":
                        dve.wait_ge(act_step_done, acts(s))
                        t0 = toks(l)[0]
                        r = rq[s[2] % 2].rearrange("p (i t) -> p i t", i=2)[:, :, t0:4]
                        link(v.reciprocal(r, r))
                        also(v.tensor_scalar(r, r, ATTN_SCALE, None, ALU.mult))
                    for i in range(2):
                        also(v.tensor_tensor(RT[:, 0, i], X2[:, i, S:T], rope_c, ALU.mult))
                        also(v.tensor_tensor(RT[:, 1, i], R_[:, i], rope_s, ALU.mult))
                    own()
                    last = v.tensor_tensor(X2[:, :, S:T], RT[:, 0], RT[:, 1], ALU.add)
                elif kind == "SC":
                    _, _, h, st_, qc = s
                    keys = slice(0, T) if st_ else slice(0, S)
                    col = 4 * (h % 2) + 2 * st_ + qc
                    link(v.tensor_reduce(nmax[qc], A[:, 0, keys], AX.X, ALU.max))
                    last = v.tensor_scalar(nbias[qc], nmax[qc], rq[h // 2 % 2][:, col:col + 1], -1.0,
                                           ALU.mult, ALU.mult)
                elif kind == "SN":
                    _, _, h, st_, qc = s
                    dve.wait_ge(act_step_done, acts(("SC",) + s[1:]))
                    keys = slice(0, T) if st_ else slice(0, S)
                    link(v.reciprocal(rinv[qc], rsum[qc]))
                    last = v.tensor_scalar(PR[qc][:, keys], PR[qc][:, keys], rinv[qc], None, ALU.mult)
                elif kind == "PV":
                    _, _, h, st_, qc = s
                    dve.wait_ge(act_step_done, acts(s))
                    at = st_ * S + qc * P
                    last = v.tensor_tensor(ol[:, h, at:at + P], A[:, 0, 0:P], oh[:, h, at:at + P].bitcast(F32),
                                           ALU.subtract)
                elif kind == "lnm":
                    last = v.tensor_copy(st[:, 0, cs], A[:, 0, cs])
                elif kind == "lnd":
                    c = s[3]
                    last = v.tensor_tensor(X[:, c, cs], X[:, c, cs], st[:, 0, cs], ALU.subtract)
                elif kind == "lnv":
                    dve.wait_ge(act_step_done, acts(s))
                    t0 = toks(l)[0]
                    link(v.reciprocal(lnr[:, t0:4], lnr[:, t0:4]))
                    for t in toks(l):
                        last = v.tensor_scalar(st[:, 3, t * P:t * P + P], ident, lnr[:, t:t + 1], None, ALU.mult)
                        if t < 3:
                            also(last)
                elif kind == "lnb":
                    last = v.tensor_copy(st[:, 1, cs], A[:, 0, cs])
                elif kind == "lnn":
                    c = s[3]
                    dve.wait_ge(act_step_done, acts(("lnsq", l, s[2], c)))
                    last = v.tensor_tensor(X[:, c, cs], X[:, c, cs], st[:, 1, cs], ALU.mult)
                last.then_inc(dve_step_done, 1)
                done["parts"] += 1

            def residual(l, which, j, y):
                m = 5 if which else 2
                for i in range(2):
                    c = 2 * j + i
                    for x in streams(l):
                        also(v.tensor_scalar(st[:, i, tok(x)], y(i)[:, tok(x)], mods[:, l, m * NC + c, x:x + 1],
                                             gateb[:, l, which, c, x:x + 1], ALU.mult, ALU.add))
                own()
                cs = cols(l)
                v.scalar_tensor_tensor(out=X[:, 2 * j:2 * j + 2, cs], in0=X[:, 2 * j:2 * j + 2, cs], scalar=ALPHA,
                                       in1=st[:, 0:2, cs], op0=ALU.mult, op1=ALU.add).then_inc(dve_step_done, 1)
                done["parts"] += 1

            lo(0)
            lo(1)
            for s in SCHEDULE:
                if s[0] in UNIT:
                    u = UNIT_NO[s]
                    if u + 2 < len(UNITS):
                        lo(u + 2)
                if s[0] in DVE_PART:
                    part(s)



def constants():
    con = np.zeros((P, NCON), np.float64)

    def put(name, x):
        con[:x.shape[0], CON[name]:CON[name] + x.shape[1]] = x

    t = np.arange(S).reshape(P, 2).T
    ang = np.pi * (2 * np.arange(P)[None, None, :] + 1) * t[:, :, None] / T
    f = np.stack([np.cos(ang), np.sin(ang)])
    put("hy_fwd", f.transpose(2, 0, 1, 3).reshape(P, -1))
    put("hy_inv", f.transpose(3, 0, 1, 2).reshape(P, -1))
    w = 2 * np.pi * (np.outer(np.arange(S), np.arange(S)) % S) / S
    put("fnet", np.stack([np.cos(w), np.sin(w)], 1).reshape(2, P, 2, S).transpose(1, 0, 2, 3).reshape(P, -1))
    inv_freq = 10000.0 ** (-np.arange(32) * 2.0 / 64)
    pos = np.stack([np.arange(S) // GRID_W, np.arange(S) % GRID_W])
    p = np.arange(P)
    a = inv_freq[p % 32][:, None] * pos[p // 64]
    put("rope_cos", np.cos(a))
    put("rope_sin", np.sin(a) * np.where(p % 64 < 32, -1.0, 1.0)[:, None])
    put("swap", np.eye(P)[p ^ 32])
    put("ident", np.eye(P))
    put("ones", np.ones((P, P)))
    put("mean", np.full((P, P), 1.0 / D))
    tt = np.linspace(0.0, 1.0, S)
    ww = (2 * np.pi / S) * np.arange(S)
    ff = np.linspace(1e-4, BANDS - 1, BANDS)
    emb = np.concatenate([tt[None], np.cos(ff[:, None] * ww), -np.sin(ff[:, None] * ww)])
    put("emb", emb.reshape(EMB, P, 2).transpose(0, 2, 1).reshape(EMB, S))
    put("notfirst", (p > 0).astype(float)[:, None])
    for n, e in (("epsln", LN_EPS), ("epsrms", RMS_EPS), ("epskern", KERN_EPS)):
        put(n, np.full((P, 1), e))
    lo, hi = math.log(1e-2) / 0.3, math.log(1e-2) / 1.5
    deltas = np.abs(np.linspace(lo, hi, D))
    decay = np.exp(-tt[:, None] * deltas)
    decay = decay.reshape(P, 2, NG, UC).transpose(2, 0, 1, 3)
    return con.astype(np.float32), np.ascontiguousarray(decay.astype(np.float32))


def unit_source(w, s):
    kind, l = s[0], s[1]
    col = {"ada": lambda: 256 * s[2], "hy": lambda: OFF_HY + D * s[3] + UC * s[2],
           "gate": lambda: OFF_G + D * s[2] + UC * s[3], "fn": lambda: OFF_FN + UC * s[2],
           "k": lambda: OFF_K, "v": lambda: OFF_V, "q": lambda: UC * s[2], "out": lambda: UC * s[2],
           "proj": lambda: UC * s[3], "mlp1": lambda: D * s[2] + UC * s[3], "mlp2": lambda: UC * s[3]}[kind]()
    name = {"ada": "w_ada", "out": "w_out", "mlp1": "w_mlp1", "mlp2": "w_mlp2"}.get(kind, "w_in")
    if kind == "proj":
        name = ("w_att_o", "w_hy_o", "w_fn_o")[s[2]]
    rows = slice(D * s[2], D * s[2] + D) if kind == "mlp2" else slice(0, D)
    return w[name][l, rows, col:col + UC].reshape(NC, P, UC).transpose(1, 0, 2)


def kernel(**inputs):
    from concourse import bacc
    from concourse.bass_utils import run_bass_kernel_spmd

    w = {k: np.asarray(x) for k, x in inputs.items()}
    chunks = lambda x: x.reshape(-1, P).T
    wts = np.empty((len(UNITS), P, NC, UC), np.float32)
    for u, s in enumerate(UNITS):
        wts[u] = unit_source(w, s)
    vecs = np.zeros((P, DEPTH, NVEC), np.float32)
    for l in range(DEPTH):
        for name, at in VEC.items():
            x = w[name][l].reshape(-1)
            if x.size < P:
                vecs[:x.size, l, at] = x
            else:
                vecs[:, l, at:at + x.size // P] = chunks(x)
    tokens = np.concatenate([w["ctx"][0], w["x"][0]])
    con, decay = constants()
    arrays = {
        "wts": wts.reshape(len(UNITS), P, UW),
        "vecs": vecs,
        "cons": con,
        "dec": decay,
        "xt": np.ascontiguousarray(tokens.T.reshape(NC, P, T).transpose(1, 0, 2)),
        "ct": np.ascontiguousarray(np.stack([w["c_ctx"], w["c"][0]], -1).reshape(NC, P, 2).transpose(1, 0, 2)),
        "fw1": np.ascontiguousarray(w["hy_w1"].transpose(1, 0, 2)),
        "fw2": np.ascontiguousarray(w["hy_w2"].transpose(1, 0, 2)),
        "fw3": np.ascontiguousarray(w["hy_w3"].reshape(DEPTH, FH, 2, 2, NG, UC).transpose(0, 4, 1, 3, 2, 5))
        .reshape(DEPTH, NG, FH, 2, 2 * UC),
        "bv": np.ascontiguousarray(w["b_in"][None, :, OFF_V:OFF_HY]),
    }
    nc = bacc.Bacc("TRN2", target_bir_lowering=False, num_devices=1, dynamic_dma_scratch_size=8192)
    aps = {k: nc.dram_tensor("in_" + k, x.shape, F32, kind="ExternalInput").ap() for k, x in arrays.items()}
    out = nc.dram_tensor("out", (P, NC, S), F32, kind="ExternalOutput").ap()
    build_program(nc, aps, out)
    r = run_bass_kernel_spmd(nc, [{"in_" + k: x for k, x in arrays.items()}], core_ids=[0])
    y = np.asarray(r.results[0]["out"])
    return np.ascontiguousarray(y.transpose(2, 1, 0).reshape(1, S, D))
```

```python
import math
from contextlib import ExitStack

import numpy as np
import concourse.bass as bass
from concourse import mybir

F32 = mybir.dt.float32
F32R = mybir.dt.float32r
ALU = mybir.AluOpType
ACT = mybir.ActivationFunctionType
AX = mybir.AxisListType

P = 128
D = 1024
NC = D // P
S = 256
T = 2 * S
DEPTH = 2
HEAD = 128
NH = D // HEAD
NKV = 2
GRID_W = 64
FF = 4 * D
OFF_K = D
OFF_V = OFF_K + NKV * HEAD
OFF_HY = OFF_V + NKV * HEAD
OFF_FN = OFF_HY + 3 * D
OFF_G = OFF_FN + D
D_IN = OFF_G + 3 * D
UC = 256
UW = NC * UC
NG = D // UC
BANDS = 16
EMB = 1 + 2 * BANDS
FH = 64
ALPHA = (2 * DEPTH) ** 0.25
LN_EPS = 1e-6
RMS_EPS = 1e-6
KERN_EPS = 1e-6
ATTN_SCALE = HEAD ** -0.5
RAW = 3
TWO_PI = 2.0 * math.pi
PI_HI = 6.28125
PI_LO = TWO_PI - PI_HI
ROUND = 1.5 * 2.0 ** 23
BELOW_PI = 3.1415925

VEC = {}
_at = 0
for _name, _n in (("b_in", D_IN // P), ("b_ada", 6 * NC), ("b_mlp1", FF // P), ("b_mlp2", NC), ("b_out", NC),
                  ("ln1_g", NC), ("ln1_b", NC), ("ln2_g", NC), ("ln2_b", NC), ("conv_w", 9 * NC),
                  ("conv_b", 3 * NC), ("hy_skip", 2 * NC), ("q_gain", 1), ("k_gain", 1),
                  ("hy_b1", 1), ("hy_freq1", 1), ("hy_b2", 1), ("hy_freq2", 1)):
    VEC[_name] = _at
    _at += _n
NVEC = _at

CON = {}
_at = 0
for _name, _n in (("hy_fwd", 4 * P), ("hy_inv", 4 * P), ("fnet", 4 * S), ("rope_cos", S), ("rope_sin", S),
                  ("swap", P), ("ident", P), ("ones", P), ("notfirst", 1), ("epsln", 1), ("epsrms", 1), ("epskern", 1)):
    CON[_name] = _at
    _at += _n
NCON = _at



def halves(*units):
    out = []
    for u in units:
        out += [[u]] if u[0] == "ada" else [[("half", u)], [u]]
    return out


def woven(pieces, groups):
    out, pieces = [], list(pieces)
    for g in groups:
        out += g
        if pieces:
            out += pieces.pop(0)
    for p in pieces:
        out += p
    return out


def ada(l, js):
    out, js = [], list(js)
    for n, j in enumerate(js):
        out.append([("ada", l, j)] + ([("adaT", l, js[n - 1])] if n else []))
    if js:
        out.append([("adaT", l, js[-1])])
    return out


def hyena(l, fills):
    streams = (0, 1) if l == 0 else (1,)

    def units(cg):
        return halves(*[("hy", l, cg, part) for part in (2, 0, 1)])

    out = woven(units(0), [[], [("K0", l, 0, 0)], [("K1", l, 0, 0)], [("KN", l, 0, 0)]])
    for cg in range(NG):
        pieces = units(cg + 1) if cg + 1 < NG else halves(("gate", l, 1, 0), ("gate", l, 1, 1)) + fills
        for o in range(2):
            z = [[(k, l, cg, x, o) for k in "TFI"] for x in streams]
            nk = (l, cg, 1) if o == 0 else (l, cg + 1, 0)
            kk = [(k,) + nk for k in ("K0", "K1", "KN")] if nk[1] < NG else []
            split = [[("hsplit", l, cg, x)] if o else [] for x in streams]
            if len(z) == 2:
                groups = [[z[0][0], z[1][0]], [z[0][1]] + kk[0:1], [z[1][1], z[0][2]] + split[0],
                          kk[1:2] + [z[1][2]] + kk[2:3] + split[1]]
            else:
                groups = [[z[0][0]], [z[0][1]] + kk[0:1], [z[0][2]] + kk[1:2] + split[0], kk[2:3]]
            n = 3 if cg + 1 < NG else len(pieces) - len(pieces) // 2 * (1 - o)
            n = min(n, len(groups)) if o == 0 else len(pieces)
            out += woven(pieces[:n], groups)
            pieces = pieces[n:]
    return out


def fourier(l, fills):
    streams = (0, 1) if l == 0 else (1,)
    out = [("fn", l, 0), ("fn", l, 1), ("proj", l, 1, 0), ("gate", l, 1, 2), ("proj", l, 1, 1), ("gate", l, 1, 3)]
    out += [("S1", l, 0, x) for x in streams]
    out += [("proj", l, 1, 2), ("proj", l, 1, 3)]
    out += [("S2", l, 0, x) for x in streams]
    pieces = halves(("fn", l, 2)) + halves(("fn", l, 3)) + halves(("gate", l, 2, 0), ("gate", l, 2, 1)) + fills
    for g in range(1, NG):
        n = 2 if g + 1 < NG else len(pieces)
        out += woven(pieces[:n], [[("S1", l, g, x) for x in streams], [("S2", l, g, x) for x in streams]])
        pieces = pieces[n:]
    return out


def attention(l, fills):
    streams = (0, 1) if l == 0 else (1,)
    out = [("k", l), ("proj", l, 2, 0), ("KR1", l), ("v", l), ("gate", l, 2, 2), ("KR2", l), ("proj", l, 2, 1),
           ("KR3", l), ("q", l, 0), ("gate", l, 2, 3), ("QR", l, 0), ("proj", l, 2, 2), ("proj", l, 2, 3)]
    items = ITEMS[l]
    per = len(items) // 4
    groups = [[] for _ in range(len(items) + 3)]
    for n, it in enumerate(items):
        groups[n].append(("SC",) + it)
        groups[n + 1].append(("SN",) + it)
        groups[n + 2].append(("TP",) + it)
        groups[n + 3].append(("PV",) + it)
    pieces = []
    for j in range(4):
        if j < 3:
            q = halves(("q", l, j + 1))
            q[-1] = q[-1]
            own = q + [[("QR", l, j + 1)]]
        else:
            own = halves(("gate", l, 0, 0), ("gate", l, 0, 1))
        n = len(fills) // (4 - j)
        own = own[:2] + fills[:n] + own[2:] if j < 3 else own + fills[:n]
        fills = fills[n:]
        pieces.append(own)
    for j in range(4):
        mine = pieces[j]
        gr = groups[j * per:(j + 1) * per if j < 3 else None]
        for n, g in enumerate(gr):
            out += g
            upto = len(mine) * (n + 1) // len(gr)
            done = len(mine) * n // len(gr)
            for p in mine[done:upto]:
                out += p
    out.append(("xback", l))
    out += [("proj", l, 0, 0), ("gate", l, 0, 2), ("proj", l, 0, 1), ("gate", l, 0, 3), ("msplit", l, 0),
            ("msplit", l, 1), ("proj", l, 0, 2), ("msplit", l, 2), ("proj", l, 0, 3), ("msplit", l, 3)]
    return out


def norm(l, which, fills):
    groups = [[("lnm", l, which)], [("lnv", l, which)], [("lnb", l, which)]]
    out = groups[0]
    n = len(fills)
    for c in range(NC):
        out = out + [("lnd", l, which, c), ("lnsq", l, which, c)]
        if c % 2 and fills:
            out += fills.pop(0)
    out += groups[1]
    for _ in range(2):
        if fills:
            out += fills.pop(0)
    out += groups[2]
    for c in range(NC):
        out += [("lnn", l, which, c), ("lnx", l, which, c)]
        if fills:
            out += fills.pop(0)
    for f in fills:
        out += f
    return out


def modulated(l, which):
    out = [("hb1", l, which, 0)]
    for c in range(NC):
        if c + 1 < NC:
            out.append(("hb1", l, which, c + 1))
        out.append(("hb2", l, which, c))
    return out


def mlp(l):
    out = []

    def up(g):
        for j in range(4):
            out.append(("mlp1", l, g, j))
            out.append(("msq", l, g, j))

    def down(g):
        for j in range(4):
            out.append(("mlp2", l, g, j))

    up(0)
    up(1)
    down(0)
    up(2)
    down(1)
    up(3)
    down(2)
    down(3)
    return out


def schedule():
    out = [("silu",)]
    out += woven(ada(0, range(8)), [[("f1", 0)], [("f1", 1)], [("f2", 0)], [("f2", 1)]])
    out += [("coefA", 0)] + modulated(0, 0)
    for l in range(DEPTH):
        out.append(("hprep", l))
        out += hyena(l, ada(0, range(8, 12)) if l == 0 else [])
        out += fourier(l, [])
        out += attention(l, ada(0, range(12, 24)) if l == 0 else [])
        if l == 0:
            out.append(("coefB", 0))
        out += [("out", l, j) for j in range(NG)]
        out += norm(l, 0, ada(1, range(0, 12)) if l == 0 else [])
        if l == 0:
            out.append(("coefA", 1))
        out += modulated(l, 1)
        out += mlp(l)
        out += norm(l, 1, ada(1, range(12, 24)) if l == 0 else [])
        if l + 1 < DEPTH:
            out += [("coefB", 1), ("xout", l)] + modulated(l + 1, 0)
    return out


ITEMS = [[(l, h, x, qc) for h in range(NH) for x in ((0, 1) if l == 0 else (1,)) for qc in range(2)]
         for l in range(DEPTH)]
ITEM_NO = {it: n for its in ITEMS for n, it in enumerate(its)}
SCHEDULE = schedule()
UNIT = ("ada", "hy", "gate", "proj", "fn", "k", "v", "q", "out", "mlp1", "mlp2")
AUX = ("f1", "f2", "K0", "K1", "KN", "T", "F", "I", "S1", "S2", "KR1", "KR2", "KR3", "QR", "SC", "TP", "PV",
       "lnm", "lnv", "lnb", "adaT")
ACT_PART = ("silu", "ada", "adaT", "hy", "gate", "fn", "k", "v", "q", "mlp1", "f1", "f2", "K1", "KN", "T", "F", "I",
            "S1", "S2", "KR1", "QR", "SC", "TP", "PV", "lnv", "lnsq", "lnx", "hb2", "msplit", "msq", "hsplit")
DVE_PART = ("silu", "hy", "proj", "out", "mlp1", "mlp2", "f1", "f2", "K0", "K1", "KN", "F", "I", "S2", "KR1", "KR2",
            "KR3", "QR", "SC", "SN", "PV", "lnm", "lnd", "lnv", "lnb", "lnn", "hb1", "hb2", "msplit", "msq",
            "hsplit", "coefA", "coefB", "hprep")
AT = {s: n for n, s in enumerate(SCHEDULE)}
UNITS = [s for s in SCHEDULE if s[0] in UNIT]
UNIT_NO = {s: n for n, s in enumerate(UNITS)}
AUXES = [s for s in SCHEDULE if s[0] in AUX]
AUX_NO = {s: n for n, s in enumerate(AUXES)}
SPLITS = [s for s in UNITS if s[0] != "ada"]
SPLIT_NO = {s: n for n, s in enumerate(SPLITS)}
EC_NO = {s: n for n, s in enumerate([s for s in SCHEDULE if s[0] in ("K1", "F")])}
Z_NO = {s: n for k in "TFI" for n, s in enumerate([s for s in SCHEDULE if s[0] == k])}
ADA_NO = {s: n for k in ("ada", "adaT") for n, s in enumerate([s for s in SCHEDULE if s[0] == k])}
EC_STEPS, Z_I = list(EC_NO), [s for s in Z_NO if s[0] == "I"]
ADA_T = [s for s in ADA_NO if s[0] == "adaT"]


def ends(part):
    n, out = 0, []
    for s in SCHEDULE:
        n += s[0] in part
        out.append(n)
    return out


ACT_ENDS = ends(ACT_PART)
DVE_ENDS = ends(DVE_PART)
assert len(AT) == len(SCHEDULE)


def build_program(nc, a, out_dram):
    es = ExitStack()
    with es:
        def sb(name, shape, dt=F32):
            return es.enter_context(nc.sbuf_tensor(name, shape, dt))

        def sem(name):
            return es.enter_context(nc.semaphore(name))

        raw = sb("raw", [P, RAW, UW])
        wh = sb("wh", [P, 2, UW], F32R)
        wl = sb("wl", [P, 2, UW], F32R)
        hh = sb("hh", [P, NC, T], F32R)
        hl = sb("hl", [P, NC, T], F32R)
        oh = sb("oh", [P, NC, T], F32R)
        ol = sb("ol", [P, NC, T], F32R)
        xs = sb("xs", [P, NC * T])
        ms = sb("ms", [P, NC * T])
        st = sb("st", [P, 4, T])
        cons = sb("cons", [P, NCON])
        vecs = sb("vecs", [P, DEPTH, NVEC])
        mods = sb("mods", [P, DEPTH, 6 * NC, 2])
    

        scale1 = sb("scale1", [P, DEPTH, 2, NC, 2])
        gateb = sb("gateb", [P, DEPTH, 2, NC, 2])
        gainb = sb("gainb", [P, DEPTH, NH + NKV])
        cvec = sb("cvec", [P, NC, 2])
        csig = sb("csig", [P, NC, 2])
        fh2 = sb("fh2", [FH, DEPTH, S])
        arow = sb("arow", [2, 2, UC])
        hx = sb("hx", [P, 1536])
        ksc = sb("ksc", [P, 2, 2])
        small = sb("small", [P, 48])
        inner = ExitStack()
        s2 = inner.enter_context(nc.sbuf_tensor("s2", [P, 2 * NC * T], F32))
        inner.close()
        bh = sb("bh", [P, NC, T], F32R)
        bl = sb("bl", [P, NC, T], F32R)

        gemm = es.enter_context(nc.psum_tensor("gemm", [P, 4, T], F32))
        aux = es.enter_context(nc.psum_tensor("aux", [P, 2, 2, T], F32))

        raw_in = [sem(f"raw_in{i}") for i in range(RAW)]
        x_in = sem("x_in")
        vec_in = sem("vec_in")
        w3_in = [sem(f"w3_in{o}") for o in range(2)]
        dec_in = [sem(f"dec_in{n}") for n in range(2)]
        bv_in = sem("bv_in")
        xback_in = sem("xback_in")
        x_kept = sem("x_kept")
        hi_made = sem("hi_made")
        lo_made = sem("lo_made")
        unit_summed = sem("unit_summed")
        aux_summed = sem("aux_summed")
        act_step_done = sem("act_step_done")
        dve_step_done = sem("dve_step_done")
        act_chain = sem("act_chain")
        dve_chain = sem("dve_chain")
        stored = sem("stored")

        x_kept_dram = nc.dram_tensor("x_kept_dram", (P, NC, T), F32, kind="Internal").ap()

        X = xs[:, :].rearrange("p (c t) -> p c t", c=NC)
        M = ms[:, :].rearrange("p (c t) -> p c t", c=NC)

        def con(name, n, parts=P):
            return cons[0:parts, CON[name]:CON[name] + n]

        def vec(l, name, i=0, parts=P):
            return vecs[0:parts, l, VEC[name] + i:VEC[name] + i + 1]

        fwd = con("hy_fwd", 4 * P).rearrange("p (c a k) -> p c a k", c=2, a=2)
        inv = con("hy_inv", 4 * P).rearrange("p (c a k) -> p c a k", c=2, a=2)
        fcs = con("fnet", 4 * S).rearrange("p (k c n) -> p k c n", k=2, c=2)
        rope_c = con("rope_cos", S)
        rope_s = con("rope_sin", S)
        swap = con("swap", P)
        ident = con("ident", P)
        ones = con("ones", P)

        pad = s2[:, 0:1032].rearrange("p (i s t) -> p i s t", i=2, s=2)
        hyu = [s2[:, 1040 + 3072 * b:1040 + 3072 * (b + 1)].rearrange("p (x i t) -> p x i t", x=3, i=2) for b in (0, 1)]
        kf = xs[:, 0:2048].rearrange("p (o h c n) -> p o h c n", o=2, h=2, c=2)
        ztb = [xs[:, 2048 + 512 * b:2560 + 512 * b].rearrange("p (a n) -> p a n", a=2) for b in (0, 1)]
        ecb = [xs[:, 3072 + 512 * b:3584 + 512 * b] for b in (0, 1)]
        decb = [x.rearrange("p (a n) -> p a n", a=2) for x in (s2[:, 7184:7696], hx[:, 1024:1536])]
        stw = st[:, :, :].rearrange("p a t -> p (a t)")
        hub = [x.rearrange("p (h c n) -> p h c n", h=2, c=2) for x in (ms[:, 0:1024], stw[:, 0:1024])]
        y1b = [stw[:, 1024 + 512 * b:1536 + 512 * b].rearrange("p (i t) -> p i t", i=2) for b in (0, 1)]
        ksd = hx[:, 0:1024].rearrange("p (c a n) -> p c a n", c=2, a=2)
        ht = ms[:, 1024:2048].rearrange("p (h c n) -> p h c n", h=2, c=2)
        hy_y = ms[:, 2048:3072].rearrange("p (h c n) -> p h c n", h=2, c=2)
        w3 = ms[0:FH, 3072:4096].rearrange("p (o n) -> p o n", o=2)
        fw1 = s2[0:EMB, 0:2 * FH].rearrange("p (l n) -> p l n", l=2)
        fw2 = s2[0:FH, 128:128 + 2 * FH].rearrange("p (l n) -> p l n", l=2)
        emb = s2[0:EMB, 256:256 + S]
        fh1 = [s2[0:FH, 512 + S * l:512 + S * l + S] for l in range(DEPTH)]
        farg = [s2[0:FH, 1024 + S * n:1024 + S * n + S] for n in range(2)]
        def gates(b, j):
            at = (1040 if b == 1 else 5120) + 1024 * (j % 2)
            return s2[:, at:at + 1024].rearrange("p (i t) -> p i t", i=2)

        gtmp = hx[:, 0:1024].rearrange("p (i t) -> p i t", i=2)
        pf = [xs[:, 1024 * b:1024 * (b + 1)].rearrange("p (i t) -> p i t", i=2) for b in (0, 1)]
        xcs = [xs[:, 2048 + 1024 * b:3072 + 1024 * b].rearrange("p (t c n) -> p t c n", t=2, c=2) for b in (0, 1)]
        K = xs[:, 0:1024].rearrange("p (g t) -> p g t", g=2)
        V = xs[:, 1024:2048].rearrange("p (t n) -> p t n", t=4)
        PR = [xs[:, 2048:2560], xs[:, 2560:3072], s2[:, 7168:7680], s2[:, 7680:8192]]
        bv = hx[0:1, 1024:1024 + NKV * HEAD]
        PT = [xs[:, 3072 + 512 * b:3584 + 512 * b].rearrange("p (k q) -> p k q", k=4) for b in (0, 1)]
        QG = [s2[:, 1024 * b:1024 * (b + 1)].rearrange("p (i t) -> p i t", i=2) for b in (0, 1)]
        QSQ = s2[:, 2048:3072].rearrange("p (i t) -> p i t", i=2)
        RT = s2[:, 3072:4096].rearrange("p (k i t) -> p k i t", k=2, i=2)
        DG = s2[:, 4096:5120].rearrange("p (k t) -> p k t", k=8)
        rk = small[:, 0:8]
        rq = [small[:, 8:16], small[:, 16:24]]
        nmax, nbias, rsum, rinv = [[small[:, 24 + 4 * k + n:25 + 4 * k + n] for n in range(4)] for k in range(4)]
        lnr = small[:, 40:44]
        ksn = small[:, 44:46]

        def cols(l):
            return slice(0, T) if l == 0 else slice(S, T)

        def streams(l):
            return (0, 1) if l == 0 else (1,)

        def toks(l):
            return range(4) if l == 0 else range(2, 4)

        def tok(s):
            return slice(s * S, s * S + S)

        def hidden(g):
            return (oh, ol) if g % 2 == 0 else (bh, bl)

        def acts(step):
            return ACT_ENDS[AT[step]]

        def dves(step):
            return DVE_ENDS[AT[step]]

        def units(step):
            return UNIT_NO[step] + 1

        def auxes(step):
            return AUX_NO[step] + 1

        def bank(step):
            return aux[:, AUX_NO[step] % 2]

        block = es.enter_context(nc.Block())

        @block.sync
        def _(sp):
            for u in range(len(UNITS)):
                if u >= RAW:
                    if UNITS[u - RAW] in SPLIT_NO:
                        sp.wait_ge(hi_made, SPLIT_NO[UNITS[u - RAW]] + 1)
                        sp.wait_ge(lo_made, SPLIT_NO[UNITS[u - RAW]] + 1)
                    else:
                        sp.wait_ge(unit_summed, u - RAW + 1)
                sp.dma_start(raw[:, u % RAW], a["wts"][u]).then_inc(raw_in[u % RAW], 16)

        @block.gpsimd
        def _(pool):
            pool.dma_start(cvec[:], a["ct"]).then_inc(vec_in, 16)
            pool.dma_start(vecs[:], a["vecs"]).then_inc(vec_in, 16)
            pool.dma_start(cons[:], a["cons"]).then_inc(vec_in, 16)
            pool.dma_start(fw1, a["fw1"]).then_inc(vec_in, 16)
            pool.dma_start(fw2, a["fw2"]).then_inc(vec_in, 16)
            pool.dma_start(emb, a["emb"]).then_inc(vec_in, 16)
            pool.dma_start(X, a["xt"]).then_inc(x_in, 16)
            for n, s in enumerate(SCHEDULE):
                if s[0] == "half" and s[1][0] == "hy" and s[1][2:] == (0, 2):
                    l = s[1][1]
                    pool.wait_ge(dve_step_done, dves(("hb2", l, 0, NC - 1)))
                    if l:
                        pool.wait_ge(x_kept, 16)
                    for cg in range(NG):
                        if cg >= 2:
                            pool.wait_ge(dve_step_done, dves(("K0", l, cg - 2, 1)))
                        pool.dma_start(decb[cg % 2], a["dec"][cg]).then_inc(dec_in[cg % 2], 16)
                        for o in range(2):
                            if cg:
                                pool.wait_ge(aux_summed, auxes(("K0", l, cg - 1, o)))
                            pool.dma_start(w3[:, o], a["fw3"][l, cg, o]).then_inc(w3_in[o], 16)
                    pool.wait_ge(aux_summed, auxes(("KN", l, NG - 1, 1)))
                    pool.wait_ge(dve_step_done, dves(("K0", l, NG - 1, 1)))
                    pool.dma_start(bv, a["bv"][:, l]).then_inc(bv_in, 16)
                elif s[0] == "xback":
                    l = s[1]
                    pool.wait_ge(dve_step_done, dves(("PV", l, NH - 1, 1, 1)))
                    pool.dma_start(X, a["xt"] if l == 0 else x_kept_dram).then_inc(xback_in, 16)
                elif s[0] == "xout":
                    pool.wait_ge(act_step_done, acts(("lnx", s[1], 1, NC - 1)))
                    pool.dma_start(x_kept_dram, X).then_inc(x_kept, 16)
            pool.wait_ge(act_step_done, acts(("lnx", DEPTH - 1, 1, NC - 1)))
            pool.dma_start(out_dram, X[:, :, S:T]).then_inc(stored, 16)
            pool.wait_ge(stored, 16)

        @block.tensor
        def _(pe):
            mm = nc.tensor.matmul

            def wait_operands(s, k):
                kind, l = s[0], s[1]
                x = 1
                if kind == "proj" and s[2] == 1:
                    pe.wait_ge(dve_step_done, dves(("hsplit", l, k // 2, x)))
                elif kind == "proj" and s[2] == 2:
                    pe.wait_ge(dve_step_done, dves(("S2", l, k // 2, x)))
                elif kind == "proj":
                    pe.wait_ge(dve_step_done, dves(("PV", l, k, x, 1)))
                elif kind == "out":
                    pe.wait_ge(dve_step_done, dves(("msplit", l, k // 2)))
                elif kind == "mlp1":
                    pe.wait_ge(dve_step_done, dves(("hb2", l, 1, k)))
                elif kind == "mlp2":
                    pe.wait_ge(dve_step_done, dves(("msq", l, s[2], k // 2)))
                else:
                    pe.wait_ge(dve_step_done, dves(("hb2", l, 0, k)))

            def open_unit(s):
                u = UNIT_NO[s]
                if s in SPLIT_NO:
                    pe.wait_ge(lo_made, SPLIT_NO[s] + 1)
                else:
                    pe.wait_ge(raw_in[u % RAW], 16 * (u // RAW + 1))
                if u >= 2:
                    before = UNITS[u - 2]
                    if before[0] in ACT_PART:
                        pe.wait_ge(act_step_done, acts(before))
                    if before[0] in DVE_PART:
                        pe.wait_ge(dve_step_done, dves(before))

            def ada_unit(s):
                u = UNIT_NO[s]
                open_unit(s)
                pe.wait_ge(dve_step_done, dves(("silu",)))
                w = raw[:, u % RAW].rearrange("p (k n) -> p k n", k=NC)
                for k in range(NC):
                    last = mm(gemm[0:2, 2 * (u % 2), 0:UC], csig[:, k], w[:, k], start=(k == 0), stop=(k == NC - 1))
                last.then_inc(unit_summed, 1)

            def v_unit(s):
                l = s[1]
                u, n = UNIT_NO[s], SPLIT_NO[s]
                open_unit(s)
                pe.wait_ge(bv_in, 16 * (l + 1))
                WH, WL = [w[:, n % 2].rearrange("p (k n) -> p k n", k=NC) for w in (wh, wl)]
                for t in range(4):
                    dst = gemm[:, 2 * (u % 2) + t // 2, (t % 2) * UC:(t % 2 + 1) * UC]
                    ts = slice(t * P, t * P + P)
                    mm(dst, ones[0:1, :], bv, start=True, stop=False)
                    for k in range(NC):
                        mm(dst, hl[:, k, ts], WH[:, k], start=False, stop=False)
                        mm(dst, hh[:, k, ts], WH[:, k], start=False, stop=False)
                        last = mm(dst, hh[:, k, ts], WL[:, k], start=False, stop=(k == NC - 1))
                last.then_inc(unit_summed, 1)

            def chunk(s, i):
                kind, l = s[0], s[1]
                u, n = UNIT_NO[s], SPLIT_NO[s]
                if i == 0:
                    open_unit(s)
                WH, WL = [w[:, n % 2].rearrange("p (k n) -> p k n", k=NC) for w in (wh, wl)]
                first = s[-1] == 0 if kind != "hy" else s[2:] == (0, 2)
                mh, ml, cs = hh, hl, cols(l)
                if kind == "proj":
                    mh, ml = oh, ol
                elif kind == "mlp2":
                    mh, ml = hidden(s[2])
                elif kind == "k":
                    cs = slice(0, T)
                dst = gemm[:, 2 * (u % 2) + i, cs]
                ws = slice(i * P, i * P + P)
                if i == 0 and not first:
                    wait_operands(s, NC - 1)
                for k in range(NC):
                    if i == 0 and first:
                        wait_operands(s, k)
                    mm(dst, WL[:, k, ws], mh[:, k, cs], start=(k == 0), stop=False)
                    mm(dst, WH[:, k, ws], mh[:, k, cs], start=False, stop=False)
                    last = mm(dst, WH[:, k, ws], ml[:, k, cs], start=False, stop=(k == NC - 1))
                if i:
                    last.then_inc(unit_summed, 1)

            def aux_step(s):
                kind, l = s[0], s[1]
                n = AUX_NO[s]
                A = bank(s)
                if n >= 2:
                    before = AUXES[n - 2]
                    if before[0] in ACT_PART:
                        pe.wait_ge(act_step_done, acts(before))
                    if before[0] in DVE_PART:
                        pe.wait_ge(dve_step_done, dves(before))
                if kind == "adaT":
                    pe.wait_ge(act_step_done, acts(("ada",) + s[1:]))
                    pe.wait_ge(vec_in, 96)
                    for i in range(2):
                        last = mm(A[:, 0, 2 * i:2 * i + 2], arow[:, ADA_NO[s] % 2, i * P:i * P + P], ident[0:2, 0:2],
                                  start=True, stop=True)
                elif kind == "f1":
                    pe.wait_ge(vec_in, 96)
                    last = mm(A[0:FH, 0, 0:S], fw1[:, l], emb, start=True, stop=True)
                elif kind == "f2":
                    pe.wait_ge(act_step_done, acts(("f1", l)))
                    last = mm(A[0:FH, 0, 0:S], fw2[:, l], fh1[l], start=True, stop=True)
                elif kind == "K0":
                    _, _, cg, o = s
                    pe.wait_ge(act_step_done, acts(("f2", l)))
                    pe.wait_ge(w3_in[o], 16 * (NG * l + cg + 1))
                    for par in range(2):
                        last = mm(A[:, par], fh2[:, l, par * P:par * P + P], w3[:, o], start=True, stop=True)
                elif kind == "KN":
                    _, _, cg, o = s
                    pe.wait_ge(act_step_done, acts(("K1", l, cg, o)))
                    for i in range(2):
                        for q in range(4):
                            last = mm(A[:, 0, i:i + 1], ksd[:, q // 2, q % 2, i * P:i * P + P], ones[:, 0:1],
                                      start=(q == 0), stop=(q == 3))
                elif kind == "K1":
                    _, _, cg, o = s
                    pe.wait_ge(dve_step_done, dves(("K0", l, cg, o)))
                    for par in range(2):
                        for c in range(2):
                            last = mm(A[:, par, c * UC:(c + 1) * UC], fwd[:, c, par], ksd[:, c, par],
                                      start=True, stop=True)
                elif kind == "T":
                    _, _, cg, st_, o = s
                    if o == 0:
                        pe.wait_ge(dve_step_done, dves(("hy", l, cg, 2)))
                    else:
                        pe.wait_ge(dve_step_done, dves(("I", l, cg, st_, 0)))
                    z = hyu[cg % 2][:, 2]
                    for par in range(2):
                        for i in range(2):
                            src = z[:, i, tok(st_)].rearrange("p (t a) -> p a t", a=2)[:, par]
                            last = nc.tensor.transpose(A[:, 0, par * UC + i * P:par * UC + (i + 1) * P], src, ident)
                elif kind == "F":
                    pe.wait_ge(act_step_done, acts(("T",) + s[1:]))
                    for par in range(2):
                        for c in range(2):
                            last = mm(A[:, par, c * UC:(c + 1) * UC], fwd[:, c, par], ztb[Z_NO[s] % 2][:, par],
                                      start=True, stop=True)
                elif kind == "I":
                    pe.wait_ge(dve_step_done, dves(("F",) + s[1:]))
                    for i in range(2):
                        for par in range(2):
                            for c in range(2):
                                last = mm(A[:, 0, (2 * i + par) * P:(2 * i + par + 1) * P],
                                          hub[Z_NO[s] % 2][:, par, c, i * P:i * P + P], inv[:, c, par],
                                          start=(c == 0), stop=(c == 1))
                elif kind == "S1":
                    _, _, g, st_ = s
                    pe.wait_ge(act_step_done, acts(("fn", l, g)))
                    for t in range(2):
                        for k in range(2):
                            last = mm(A[:, t], pf[g % 2][:, k, st_ * S + t * P:st_ * S + (t + 1) * P], fcs[:, k],
                                      start=(k == 0), stop=(k == 1))
                elif kind == "S2":
                    _, _, g, st_ = s
                    pe.wait_ge(act_step_done, acts(("S1", l, g, st_)))
                    for i in range(2):
                        for t in range(2):
                            for c in range(2):
                                last = mm(A[:, 0, i * S:(i + 1) * S], xcs[st_][:, t, c, i * P:i * P + P],
                                          fcs[:, t, c], start=(t == 0 and c == 0), stop=(t == 1 and c == 1))
                elif kind in ("KR1", "QR"):
                    if kind == "QR":
                        j = s[2]
                        pe.wait_ge(act_step_done, acts(("q", l, j)))
                        r = toks(l)
                    else:
                        pe.wait_ge(act_step_done, acts(("k", l)))
                        r = range(4)
                    for i in range(2):
                        for t in r:
                            last = mm(A[:, 0, 4 * i + t:4 * i + t + 1], QSQ[:, i, t * P:t * P + P], ones[:, 0:1],
                                      start=True, stop=True)
                    if kind == "QR":
                        for i in range(2):
                            last = mm(A[:, 1, i * S:(i + 1) * S], swap, QG[j % 2][:, i, S:T], start=True, stop=True)
                elif kind == "KR2":
                    pe.wait_ge(dve_step_done, dves(("KR1", l)))
                    for i in range(2):
                        for t in range(4):
                            last = mm(A[:, i, t * P:t * P + P], ones, DG[:, 4 * i + t], start=True, stop=True)
                elif kind == "KR3":
                    pe.wait_ge(dve_step_done, dves(("KR2", l)))
                    for i in range(2):
                        last = mm(A[:, 0, i * S:(i + 1) * S], swap, K[:, i, S:T], start=True, stop=True)
                elif kind == "SC":
                    _, _, h, st_, qc = s
                    pe.wait_ge(dve_step_done, dves(("QR", l, h // 2)))
                    pe.wait_ge(dve_step_done, dves(("KR3", l)))
                    at = st_ * S + qc * P
                    keys = slice(0, T) if st_ else slice(0, S)
                    last = mm(A[:, 0, keys], QG[h // 2 % 2][:, h % 2, at:at + P], K[:, h // 4, keys],
                              start=True, stop=True)
                elif kind == "TP":
                    _, _, h, st_, qc = s
                    pe.wait_ge(dve_step_done, dves(("SN",) + s[1:]))
                    for kc in range(4 if st_ else 2):
                        last = nc.tensor.transpose(A[:, 0, kc * P:kc * P + P], PR[ITEM_NO[s[1:]] % 4][:, kc * P:kc * P + P], ident)
                elif kind == "PV":
                    _, _, h, st_, qc = s
                    pe.wait_ge(act_step_done, acts(("TP",) + s[1:]))
                    pe.wait_ge(act_step_done, acts(("v", l)))
                    n = 4 if st_ else 2
                    for kc in range(n):
                        last = mm(A[:, 0, 0:P], V[:, kc, h // 4 * P:h // 4 * P + P], PT[ITEM_NO[s[1:]] % 2][:, kc],
                                  start=(kc == 0), stop=(kc == n - 1))
                elif kind == "lnm":
                    which = s[2]
                    for c in range(NC):
                        pe.wait_ge(dve_step_done, dves(("mlp2", l, 3, c // 2) if which else ("out", l, c // 2)))
                        last = mm(A[:, 0, cols(l)], ones, X[:, c, cols(l)], start=(c == 0), stop=(c == NC - 1))
                elif kind == "lnv":
                    which = s[2]
                    for c in range(NC):
                        pe.wait_ge(act_step_done, acts(("lnsq", l, which, c)))
                        for t in toks(l):
                            last = mm(A[:, 0, t:t + 1], M[:, c, t * P:t * P + P], ones[:, 0:1],
                                      start=(c == 0 and t == toks(l)[0]), stop=(c == NC - 1),
                                      skip_group_check=True)
                elif kind == "lnb":
                    which = s[2]
                    pe.wait_ge(dve_step_done, dves(("lnv", l, which)))
                    for t in toks(l):
                        last = mm(A[:, 0, t * P:t * P + P], ones, st[:, 3, t * P:t * P + P], start=True, stop=True)
                last.then_inc(aux_summed, 1)

            for n, s in enumerate(SCHEDULE):
                if s[0] == "half":
                    chunk(s[1], 0)
                elif s[0] == "ada":
                    ada_unit(s)
                elif s[0] == "v":
                    v_unit(s)
                elif s[0] in UNIT:
                    if ("half", s) not in AT:
                        chunk(s, 0)
                    chunk(s, 1)
                elif s[0] in AUX:
                    aux_step(s)

        @block.scalar
        def _(act):
            act_fn = nc.scalar.activation
            done = {"chain": 0}

            def link(ins):
                ins.then_inc(act_chain, 1)
                done["chain"] += 1
                act.wait_ge(act_chain, done["chain"])

            def hi(s):
                u, n = UNIT_NO[s], SPLIT_NO[s]
                act.wait_ge(raw_in[u % RAW], 16 * (u // RAW + 1))
                if n >= 2:
                    act.wait_ge(unit_summed, units(SPLITS[n - 2]))
                    act.wait_ge(lo_made, n - 1)
                act_fn(wh[:, n % 2], raw[:, u % RAW], ACT.Copy).then_inc(hi_made, 1)

            def part(s):
                kind = s[0]
                l = s[1] if len(s) > 1 else 0
                cs = cols(l)
                last = None
                if kind in UNIT:
                    u = UNIT_NO[s]
                    act.wait_ge(unit_summed, units(s))
                    g = [gemm[:, 2 * (u % 2) + i] for i in range(2)]
                elif kind in AUX:
                    act.wait_ge(aux_summed, auxes(s))
                    A = bank(s)
                if kind == "silu":
                    act.wait_ge(vec_in, 96)
                    last = act_fn(csig[:], cvec[:], ACT.Sigmoid)
                elif kind == "ada":
                    n = ADA_NO[s]
                    if n >= 2:
                        act.wait_ge(aux_summed, auxes(ADA_T[n - 2]))
                    last = act_fn(arow[:, n % 2], g[0][0:2, 0:UC], ACT.Copy)
                elif kind == "adaT":
                    j = s[2]
                    for i in range(2):
                        last = act_fn(mods[:, l, 2 * j + i], A[:, 0, 2 * i:2 * i + 2], ACT.Identity,
                                      bias=vec(l, "b_ada", 2 * j + i))
                        if i == 0:
                            last.then_inc(act_chain, 1)
                            done["chain"] += 1
                    act.wait_ge(act_chain, done["chain"])
                elif kind == "hy":
                    _, _, cg, part_ = s
                    before = {(2): (cg - 1, 1), (0): (cg, 2), (1): (cg, 0)}[part_]
                    act.wait_ge(dve_step_done, dves(("hy", l) + before if before[0] >= 0 else ("hprep", l)))
                    for i in range(2):
                        b = vec(l, "b_in", OFF_HY // P + NC * part_ + 2 * cg + i)
                        n0, n1 = (0, 2) if l == 0 else (1, 2)
                        last = act_fn(pad[:, i, n0:n1, 1:S + 1],
                                      g[i][:, cs].rearrange("p (s t) -> p s t", t=S), ACT.Identity, bias=b)
                elif kind == "gate":
                    _, _, b, j = s
                    if j >= 2:
                        act.wait_ge(dve_step_done, dves(("proj", l, b, j - 2)))
                    elif b == 1:
                        act.wait_ge(dve_step_done, dves(("hsplit", l, NG - 2, 1)))
                    elif b == 2:
                        act.wait_ge(dve_step_done, dves(("hsplit", l, NG - 1, 1)))
                    else:
                        act.wait_ge(dve_step_done, dves(("proj", l, 2, NG - 1)))
                    G = gates(b, j)
                    for i in range(2):
                        last = act_fn(G[:, i, cs], g[i][:, cs], ACT.Sigmoid,
                                      bias=vec(l, "b_in", OFF_G // P + NC * b + 2 * j + i))
                elif kind == "fn":
                    gr = s[2]
                    if gr == 0:
                        act.wait_ge(dve_step_done, dves(("hsplit", l, NG - 1, 1)))
                    for i in range(2):
                        last = act_fn(pf[gr % 2][:, i, cs], g[i][:, cs], ACT.Identity,
                                      bias=vec(l, "b_in", OFF_FN // P + 2 * gr + i))
                elif kind in ("k", "q"):
                    if kind == "k":
                        c0, dst, gain, cs = OFF_K // P, K, vec(l, "k_gain"), slice(0, T)
                        act.wait_ge(aux_summed, auxes(("S2", l, NG - 1, 1)))
                        gb = NH
                    else:
                        j = s[2]
                        c0, dst, gain = 2 * j, QG[j % 2], vec(l, "q_gain")
                        gb = 2 * j
                        if j >= 2:
                            act.wait_ge(aux_summed, auxes(("SC", l, 2 * j - 3, 1, 1)))
                    for i in range(2):
                        act_fn(QSQ[:, i, cs], g[i][:, cs], ACT.Square,
                               bias=vec(l, "b_in", c0 + i)).then_inc(act_chain, 1)
                        done["chain"] += 1
                        last = act_fn(dst[:, i, cs], g[i][:, cs], ACT.Identity, scale=gain,
                                      bias=gainb[:, l, gb + i:gb + i + 1])
                    act.wait_ge(act_chain, done["chain"])
                elif kind == "v":
                    for i in range(2):
                        last = act_fn(V[:, 2 * i:2 * i + 2], g[i].rearrange("p (t n) -> p t n", t=2), ACT.Copy)
                elif kind == "mlp1":
                    _, _, gr, j = s
                    act.wait_ge(dve_step_done, dves(SCHEDULE[AT[s] - 1]))
                    for i in range(2):
                        last = act_fn(st[:, i, cs], g[i][:, cs], ACT.Relu, bias=vec(l, "b_mlp1", 8 * gr + 2 * j + i))
                elif kind == "msq":
                    _, _, gr, j = s
                    if gr >= 2 and j == 0:
                        act.wait_ge(unit_summed, units(("mlp2", l, gr - 2, 3)))
                    if gr == 0 and j == 0:
                        act.wait_ge(unit_summed, units(("proj", l, 0, NG - 1)))
                    act.wait_ge(dve_step_done, dves(("mlp1", l, gr, j)))
                    for i in range(2):
                        last = act_fn(hidden(gr)[0][:, 2 * j + i, cs], st[:, 2 + i, cs], ACT.Copy)
                elif kind in ("f1", "f2"):
                    act.wait_ge(dve_step_done, dves(s))
                    last = act_fn(fh1[l] if kind == "f1" else fh2[:, l], farg[1], ACT.Sin)
                elif kind == "KN":
                    last = act_fn(ksn, A[:, 0, 0:2], ACT.Sqrt, scale=0.5, bias=con("epskern", 1))
                elif kind in ("K1", "F"):
                    n = EC_NO[s]
                    if n >= 2:
                        act.wait_ge(dve_step_done, dves(EC_STEPS[n - 2]))
                    last = act_fn(ecb[n % 2], A[:, 0], ACT.Copy)
                    if kind == "K1":
                        last.then_inc(act_chain, 1)
                        done["chain"] += 1
                        last = act_fn(ksd, ksd, ACT.Square)
                        act.wait_ge(act_chain, done["chain"])
                elif kind == "T":
                    last = act_fn(ztb[Z_NO[s] % 2], A[:, 0].rearrange("p (a n) -> p a n", a=2), ACT.Copy)
                elif kind == "I":
                    _, _, cg, st_, o = s
                    n = Z_NO[s]
                    if n >= 2:
                        act.wait_ge(dve_step_done, dves(Z_I[n - 2]))
                    for i in range(2):
                        last = act_fn(y1b[n % 2][:, i].rearrange("p (t a) -> p a t", a=2),
                                      A[:, 0, i * UC:(i + 1) * UC].rearrange("p (a t) -> p a t", a=2),
                                      ACT.Identity, scale=ksc[:, o, i:i + 1])
                elif kind == "hsplit":
                    _, _, cg, st_ = s
                    act.wait_ge(dve_step_done, dves(("I", l, cg, st_, 1)))
                    if cg == 0 and st_ == streams(l)[0] and l:
                        act.wait_ge(unit_summed, units(("mlp2", l - 1, 2, 3)))
                    last = act_fn(oh[:, 2 * cg:2 * cg + 2, tok(st_)], hyu[cg % 2][:, 2, :, tok(st_)], ACT.Copy)
                elif kind == "S1":
                    _, _, gr, st_ = s
                    act_fn(xcs[st_][:, :, 0], A[:, :, 0:S], ACT.Copy, scale=1.0 / S).then_inc(act_chain, 1)
                    done["chain"] += 1
                    last = act_fn(xcs[st_][:, :, 1], A[:, :, S:T], ACT.Copy, scale=-1.0 / S)
                    act.wait_ge(act_chain, done["chain"])
                elif kind == "S2":
                    _, _, gr, st_ = s
                    if gr == 0 and st_ == streams(l)[0]:
                        act.wait_ge(unit_summed, units(("proj", l, 1, NG - 1)))
                    last = act_fn(oh[:, 2 * gr:2 * gr + 2, tok(st_)], A[:, 0].rearrange("p (i t) -> p i t", i=2),
                                  ACT.Copy)
                elif kind == "KR1":
                    last = act_fn(rk, A[:, 0, 0:8], ACT.Sqrt, scale=1.0 / HEAD, bias=con("epsrms", 1))
                elif kind == "QR":
                    j = s[2]
                    t0 = toks(l)[0]
                    last = act_fn(rq[j % 2].rearrange("p (i t) -> p i t", i=2)[:, :, t0:4],
                                  A[:, 0, 0:8].rearrange("p (i t) -> p i t", i=2)[:, :, t0:4],
                                  ACT.Sqrt, scale=1.0 / HEAD, bias=con("epsrms", 1))
                elif kind == "SC":
                    _, _, h, st_, qc = s
                    act.wait_ge(dve_step_done, dves(s))
                    keys = slice(0, T) if st_ else slice(0, S)
                    col = 4 * (h % 2) + 2 * st_ + qc
                    n = ITEM_NO[s[1:]] % 4
                    last = act_fn(PR[n][:, keys], A[:, 0, keys], ACT.Exp, bias=nbias[n],
                                  scale=rq[h // 2 % 2][:, col:col + 1], accum_out=rsum[n])
                elif kind == "TP":
                    _, _, h, st_, qc = s
                    n = 4 if st_ else 2
                    last = act_fn(PT[ITEM_NO[s[1:]] % 2][:, 0:n], A[:, 0, 0:n * P].rearrange("p (k q) -> p k q", k=n), ACT.Copy)
                elif kind == "PV":
                    _, _, h, st_, qc = s
                    if h == 0:
                        act.wait_ge(unit_summed, units(("proj", l, 2, NG - 1)))
                    at = st_ * S + qc * P
                    last = act_fn(oh[:, h, at:at + P], A[:, 0, 0:P], ACT.Copy)
                elif kind == "msplit":
                    _, _, j = s
                    if j == 0:
                        act.wait_ge(unit_summed, units(("gate", l, 0, NG - 1)))
                    act.wait_ge(dve_step_done, dves(("proj", l, 0, j)))
                    last = act_fn(hh[:, 2 * j:2 * j + 2, cs], M[:, 2 * j:2 * j + 2, cs], ACT.Copy)
                elif kind == "lnsq":
                    _, _, which, c = s
                    act.wait_ge(dve_step_done, dves(("lnd", l, which, c)))
                    last = act_fn(M[:, c, cs], X[:, c, cs], ACT.Square)
                elif kind == "lnv":
                    t0 = toks(l)[0]
                    last = act_fn(lnr[:, t0:4], A[:, 0, t0:4], ACT.Sqrt, scale=1.0 / D, bias=con("epsln", 1))
                elif kind == "lnx":
                    _, _, which, c = s
                    n = "ln2" if which else "ln1"
                    act.wait_ge(dve_step_done, dves(("lnn", l, which, c)))
                    last = act_fn(X[:, c, cs], X[:, c, cs], ACT.Identity, scale=vec(l, n + "_g", c),
                                  bias=vec(l, n + "_b", c))
                elif kind == "hb2":
                    _, _, which, c = s
                    if c == 0 and which:
                        act.wait_ge(unit_summed, units(("out", l, NG - 1)))
                    elif c == 0 and l:
                        act.wait_ge(unit_summed, units(("mlp1", l - 1, 3, 3)))
                    act.wait_ge(dve_step_done, dves(("hb1", l, which, c)))
                    full = slice(0, T) if not which else cs
                    last = act_fn(hh[:, c, full], st[:, c % 4, full], ACT.Copy)
                last.then_inc(act_step_done, 1)

            for s in SCHEDULE:
                if s[0] in UNIT and UNIT_NO[s] + 2 < len(UNITS):
                    ahead = UNITS[UNIT_NO[s] + 2]
                    if ahead in SPLIT_NO:
                        hi(ahead)
                if s[0] in ACT_PART:
                    part(s)

        @block.vector
        def _(dve):
            v = nc.vector
            done = {"chain": 0, "parts": 0}

            def link(ins):
                ins.then_inc(dve_chain, 1)
                done["chain"] += 1
                dve.wait_ge(dve_chain, done["chain"])

            def also(ins):
                ins.then_inc(dve_chain, 1)
                done["chain"] += 1

            def own(step=None):
                if done["chain"]:
                    dve.wait_ge(dve_chain, done["chain"])
                if done["parts"]:
                    dve.wait_ge(dve_step_done, done["parts"])

            def lo(s):
                u, n = UNIT_NO[s], SPLIT_NO[s]
                dve.wait_ge(hi_made, n + 1)
                v.tensor_tensor(wl[:, n % 2], raw[:, u % RAW], wh[:, n % 2].bitcast(F32),
                                ALU.subtract).then_inc(lo_made, 1)

            def part(s):
                kind = s[0]
                l = s[1] if len(s) > 1 else 0
                cs = cols(l)
                if kind in UNIT:
                    u = UNIT_NO[s]
                    if kind in ACT_PART:
                        dve.wait_ge(act_step_done, acts(s))
                    dve.wait_ge(unit_summed, units(s))
                    g = [gemm[:, 2 * (u % 2) + i] for i in range(2)]
                elif kind in AUX:
                    dve.wait_ge(aux_summed, auxes(s))
                    A = bank(s)
                own()
                last = None
                if kind == "silu":
                    dve.wait_ge(act_step_done, acts(s))
                    last = v.tensor_tensor(csig[:], csig[:], cvec[:], ALU.mult)
                elif kind == "coefA":
                    dve.wait_ge(act_step_done, acts(("adaT", l, 7)))
                    for j in range(2):
                        b, n, gn = (VEC["b_in"], NH, "q_gain") if j == 0 else (VEC["b_in"] + OFF_K // P, NKV, "k_gain")
                        also(v.tensor_scalar(gainb[:, l, j * NH:j * NH + n], vecs[:, l, b:b + n], vec(l, gn), None,
                                             ALU.mult))
                    last = v.tensor_scalar(scale1[:, l, 0], mods[:, l, NC:2 * NC], 1.0, None, ALU.add)
                elif kind == "coefB":
                    dve.wait_ge(act_step_done, acts(("adaT", l, 23)))
                    for m, n in ((2, "b_out"), (5, "b_mlp2")):
                        for x in range(2):
                            also(v.tensor_tensor(gateb[:, l, m // 3, :, x], mods[:, l, m * NC:(m + 1) * NC, x],
                                                 vecs[:, l, VEC[n]:VEC[n] + NC], ALU.mult))
                    last = v.tensor_scalar(scale1[:, l, 1], mods[:, l, 4 * NC:5 * NC], 1.0, None, ALU.add)
                elif kind == "hprep":
                    if l == 0:
                        dve.wait_ge(act_step_done, acts(("f2", 1)))
                        dve.wait_ge(aux_summed, auxes(("f2", 1)))
                    else:
                        dve.wait_ge(unit_summed, units(("mlp2", l - 1, 3, 3)))
                    also(v.memset(pad[:, :, :, 0:1], 0.0))
                    last = v.memset(pad[:, :, :, S + 1:S + 2], 0.0)
                elif kind == "hb1":
                    _, _, which, c = s
                    if which == 0 and l == 0 and c == 0:
                        dve.wait_ge(x_in, 16)
                    elif c == 0:
                        dve.wait_ge(act_step_done, acts(("lnx", l, 0, 0) if which else ("lnx", l - 1, 1, 0)))
                    if not (which == 0 and l == 0):
                        dve.wait_ge(act_step_done, acts(("lnx", l, 0, c) if which else ("lnx", l - 1, 1, c)))
                    if c >= 4:
                        dve.wait_ge(act_step_done, acts(("hb2", l, which, c - 4)))
                    ss = (0, 1) if which == 0 else streams(l)
                    for x in ss:
                        ins = v.tensor_scalar(st[:, c % 4, tok(x)], X[:, c, tok(x)], scale1[:, l, which, c, x:x + 1],
                                              mods[:, l, 3 * which * NC + c, x:x + 1], ALU.mult, ALU.add)
                        if x != ss[-1]:
                            also(ins)
                    last = ins
                elif kind == "hb2":
                    _, _, which, c = s
                    dve.wait_ge(act_step_done, acts(s))
                    full = slice(0, T) if not which else cs
                    last = v.tensor_tensor(hl[:, c, full], st[:, c % 4, full], hh[:, c, full].bitcast(F32),
                                           ALU.subtract)
                elif kind == "hy":
                    _, _, cg, part_ = s
                    u_ = hyu[cg % 2]
                    n0, n1 = (0, 2) if l == 0 else (1, 2)
                    src = lambda i, k: pad[:, i, n0:n1, k:k + S]
                    w = lambda i, k: vec(l, "conv_w", 3 * NC * k + NC * part_ + 2 * cg + i)
                    dst = lambda i: u_[:, part_, i, cs].rearrange("p (s t) -> p s t", t=S)
                    for i in range(2):
                        also(v.tensor_scalar(dst(i), src(i, 0), w(i, 0), vec(l, "conv_b", NC * part_ + 2 * cg + i),
                                             ALU.mult, ALU.add))
                    own()
                    for i in range(2):
                        also(v.scalar_tensor_tensor(out=dst(i), in0=src(i, 1), scalar=w(i, 1), in1=dst(i),
                                                    op0=ALU.mult, op1=ALU.add))
                    own()
                    for i in range(2):
                        last = v.scalar_tensor_tensor(out=dst(i), in0=src(i, 2), scalar=w(i, 2), in1=dst(i),
                                                      op0=ALU.mult, op1=ALU.add)
                        if i == 0:
                            also(last)
                elif kind == "proj":
                    _, _, b, j = s
                    dve.wait_ge(act_step_done, acts(("gate", l, b, j)))
                    G = gates(b, j)
                    for i in range(2):
                        c = 2 * j + i
                        if b == 1:
                            last = v.tensor_tensor(M[:, c, cs], g[i][:, cs], G[:, i, cs], ALU.mult)
                            if i == 0:
                                also(last)
                        else:
                            also(v.tensor_tensor(gtmp[:, i, cs], g[i][:, cs], G[:, i, cs], ALU.mult))
                    if b != 1:
                        own()
                        last = v.tensor_tensor(M[:, 2 * j:2 * j + 2, cs], M[:, 2 * j:2 * j + 2, cs], gtmp[:, :, cs],
                                               ALU.add)
                elif kind == "msplit":
                    _, _, j = s
                    dve.wait_ge(act_step_done, acts(s))
                    last = v.tensor_tensor(hl[:, 2 * j:2 * j + 2, cs], M[:, 2 * j:2 * j + 2, cs],
                                           hh[:, 2 * j:2 * j + 2, cs].bitcast(F32), ALU.subtract)
                elif kind == "out":
                    _, _, j = s
                    if j == 0:
                        dve.wait_ge(xback_in, 16 * (l + 1))
                    residual(l, 0, j, lambda i: g[i])
                    return
                elif kind == "mlp1":
                    dve.wait_ge(act_step_done, acts(s))
                    if AT[s] and SCHEDULE[AT[s] - 1][0] == "msq":
                        pass
                    last = v.tensor_tensor(st[:, 2:4, cs], st[:, 0:2, cs], st[:, 0:2, cs], ALU.mult)
                elif kind == "msq":
                    _, _, gr, j = s
                    dve.wait_ge(act_step_done, acts(s))
                    h, lo_ = hidden(gr)
                    last = v.tensor_tensor(lo_[:, 2 * j:2 * j + 2, cs], st[:, 2:4, cs],
                                           h[:, 2 * j:2 * j + 2, cs].bitcast(F32), ALU.subtract)
                elif kind == "mlp2":
                    _, _, gr, j = s
                    for i in range(2):
                        c = 2 * j + i
                        if gr == 0:
                            last = v.tensor_copy(M[:, c, cs], g[i][:, cs])
                        else:
                            last = v.tensor_tensor(M[:, c, cs], g[i][:, cs], M[:, c, cs], ALU.add)
                        if i == 0 or gr == 3:
                            also(last)
                    if gr == 3:
                        own()
                        residual(l, 1, j, lambda i: M[:, 2 * j + i])
                        return
                elif kind in ("f1", "f2"):
                    n = "1" if kind == "f1" else "2"
                    src = A[0:FH, 0, 0:S]
                    ar, rn = farg
                    if (kind, l) != ("f1", 0):
                        dve.wait_ge(act_step_done, acts(("f1", 0) if (kind, l) == ("f1", 1) else ("f1", 1) if l == 0 else ("f2", 0)))
                    link(v.tensor_scalar(ar, src, vec(l, "hy_b" + n, 0, FH), vec(l, "hy_freq" + n, 0, FH),
                                         ALU.add, ALU.mult))
                    link(v.tensor_scalar(rn, ar, 1.0 / TWO_PI, ROUND, ALU.mult, ALU.add))
                    link(v.tensor_scalar(rn, rn, ROUND, None, ALU.subtract))
                    link(v.scalar_tensor_tensor(out=ar, in0=rn, scalar=-PI_HI, in1=ar, op0=ALU.mult, op1=ALU.add))
                    link(v.scalar_tensor_tensor(out=ar, in0=rn, scalar=-PI_LO, in1=ar, op0=ALU.mult, op1=ALU.add))
                    last = v.tensor_scalar(rn, ar, BELOW_PI, -BELOW_PI, ALU.min, ALU.max)
                elif kind == "K0":
                    _, _, cg, o = s
                    dve.wait_ge(dec_in[cg % 2], 16 * (NG // 2 * l + cg // 2 + 1))
                    dec = decb[cg % 2]
                    f, b = ht[:, 0], ht[:, 1]
                    also(v.tensor_tensor(f, A[:, :, 0:UC], dec, ALU.mult))
                    also(v.scalar_tensor_tensor(out=b[:, 0], in0=A[:, 0, UC:T], scalar=con("notfirst", 1),
                                                in1=dec[:, 0], op0=ALU.mult, op1=ALU.mult))
                    also(v.tensor_tensor(b[:, 1], A[:, 1, UC:T], dec[:, 1], ALU.mult))
                    own()
                    also(v.tensor_tensor(ksd[:, 0], f, b, ALU.add))
                    last = v.tensor_tensor(ksd[:, 1], f, b, ALU.subtract)
                elif kind == "KN":
                    _, _, cg, o = s
                    dve.wait_ge(act_step_done, acts(s))
                    link(v.reciprocal(ksn, ksn))
                    last = v.tensor_scalar(ksc[:, o], ksn, 1.0 / S, None, ALU.mult)
                elif kind in ("K1", "F"):
                    dve.wait_ge(act_step_done, acts(s))
                    U = kf[:, s[3]] if kind == "K1" else hub[Z_NO[s] % 2]
                    ec = ecb[EC_NO[s] % 2]
                    flat = lambda x: x.rearrange("p c n -> p (c n)")
                    also(v.tensor_tensor(flat(U[:, 0]), ec, A[:, 1], ALU.add))
                    ins = v.tensor_tensor(flat(U[:, 1]), ec, A[:, 1], ALU.subtract)
                    if kind == "K1":
                        last = ins
                    else:
                        o = s[4]
                        also(ins)
                        own()
                        Kf = kf[:, o]
                        link(v.tensor_tensor(ht, U, Kf, ALU.mult))
                        link(v.tensor_tensor(hy_y[:, :, 0], ht[:, :, 0], ht[:, :, 1], ALU.subtract))
                        for c in range(2):
                            also(v.tensor_tensor(ht[:, :, c], U[:, :, c], Kf[:, :, 1 - c], ALU.mult))
                        own()
                        link(v.tensor_tensor(hy_y[:, :, 1], ht[:, :, 0], ht[:, :, 1], ALU.add))
                        also(v.tensor_tensor(U[:, 0], hy_y[:, 0], hy_y[:, 1], ALU.add))
                        last = v.tensor_tensor(U[:, 1], hy_y[:, 0], hy_y[:, 1], ALU.subtract)
                elif kind == "I":
                    _, _, cg, st_, o = s
                    dve.wait_ge(act_step_done, acts(s))
                    u_ = hyu[cg % 2]
                    y1 = y1b[Z_NO[s] % 2]
                    for i in range(2):
                        also(v.scalar_tensor_tensor(out=y1[:, i], in0=u_[:, 2, i, tok(st_)],
                                                    scalar=vec(l, "hy_skip", NC * o + 2 * cg + i), in1=y1[:, i],
                                                    op0=ALU.mult, op1=ALU.add))
                    own()
                    last = v.tensor_tensor(u_[:, 2, :, tok(st_)], y1, u_[:, o, :, tok(st_)], ALU.mult)
                elif kind == "hsplit":
                    _, _, cg, st_ = s
                    dve.wait_ge(act_step_done, acts(s))
                    last = v.tensor_tensor(ol[:, 2 * cg:2 * cg + 2, tok(st_)], hyu[cg % 2][:, 2, :, tok(st_)],
                                           oh[:, 2 * cg:2 * cg + 2, tok(st_)].bitcast(F32), ALU.subtract)
                elif kind == "S2":
                    _, _, gr, st_ = s
                    dve.wait_ge(act_step_done, acts(s))
                    last = v.tensor_tensor(ol[:, 2 * gr:2 * gr + 2, tok(st_)],
                                           A[:, 0].rearrange("p (i t) -> p i t", i=2),
                                           oh[:, 2 * gr:2 * gr + 2, tok(st_)].bitcast(F32), ALU.subtract)
                elif kind == "KR1":
                    dve.wait_ge(act_step_done, acts(s))
                    link(v.reciprocal(rk, rk))
                    for t in range(8):
                        last = v.tensor_scalar(DG[:, t], ident, rk[:, t:t + 1], None, ALU.mult)
                        if t < 7:
                            also(last)
                elif kind == "KR2":
                    last = v.tensor_tensor(K, K, A, ALU.mult)
                elif kind in ("KR3", "QR"):
                    X2 = K if kind == "KR3" else QG[s[2] % 2]
                    R_ = A[:, 0 if kind == "KR3" else 1].rearrange("p (i t) -> p i t", i=2)
                    if kind == "QR":
                        dve.wait_ge(act_step_done, acts(s))
                        t0 = toks(l)[0]
                        r = rq[s[2] % 2].rearrange("p (i t) -> p i t", i=2)[:, :, t0:4]
                        link(v.reciprocal(r, r))
                        also(v.tensor_scalar(r, r, ATTN_SCALE, None, ALU.mult))
                    for i in range(2):
                        also(v.tensor_tensor(RT[:, 0, i], X2[:, i, S:T], rope_c, ALU.mult))
                        also(v.tensor_tensor(RT[:, 1, i], R_[:, i], rope_s, ALU.mult))
                    own()
                    last = v.tensor_tensor(X2[:, :, S:T], RT[:, 0], RT[:, 1], ALU.add)
                elif kind == "SC":
                    _, _, h, st_, qc = s
                    keys = slice(0, T) if st_ else slice(0, S)
                    col = 4 * (h % 2) + 2 * st_ + qc
                    n = ITEM_NO[s[1:]] % 4
                    link(v.tensor_reduce(nmax[n], A[:, 0, keys], AX.X, ALU.max))
                    last = v.tensor_scalar(nbias[n], nmax[n], rq[h // 2 % 2][:, col:col + 1], -1.0,
                                           ALU.mult, ALU.mult)
                elif kind == "SN":
                    _, _, h, st_, qc = s
                    dve.wait_ge(act_step_done, acts(("SC",) + s[1:]))
                    keys = slice(0, T) if st_ else slice(0, S)
                    n = ITEM_NO[s[1:]] % 4
                    link(v.reciprocal(rinv[n], rsum[n]))
                    last = v.tensor_scalar(PR[n][:, keys], PR[n][:, keys], rinv[n], None, ALU.mult)
                elif kind == "PV":
                    _, _, h, st_, qc = s
                    dve.wait_ge(act_step_done, acts(s))
                    at = st_ * S + qc * P
                    last = v.tensor_tensor(ol[:, h, at:at + P], A[:, 0, 0:P], oh[:, h, at:at + P].bitcast(F32),
                                           ALU.subtract)
                elif kind == "lnm":
                    last = v.tensor_scalar(st[:, 0, cs], A[:, 0, cs], 1.0 / D, None, ALU.mult)
                elif kind == "lnd":
                    c = s[3]
                    last = v.tensor_tensor(X[:, c, cs], X[:, c, cs], st[:, 0, cs], ALU.subtract)
                elif kind == "lnv":
                    dve.wait_ge(act_step_done, acts(s))
                    t0 = toks(l)[0]
                    link(v.reciprocal(lnr[:, t0:4], lnr[:, t0:4]))
                    for t in toks(l):
                        last = v.tensor_scalar(st[:, 3, t * P:t * P + P], ident, lnr[:, t:t + 1], None, ALU.mult)
                        if t < 3:
                            also(last)
                elif kind == "lnb":
                    last = v.tensor_copy(st[:, 1, cs], A[:, 0, cs])
                elif kind == "lnn":
                    c = s[3]
                    dve.wait_ge(act_step_done, acts(("lnsq", l, s[2], c)))
                    last = v.tensor_tensor(X[:, c, cs], X[:, c, cs], st[:, 1, cs], ALU.mult)
                last.then_inc(dve_step_done, 1)
                done["parts"] += 1

            def residual(l, which, j, y):
                m = 5 if which else 2
                for i in range(2):
                    c = 2 * j + i
                    for x in streams(l):
                        also(v.tensor_scalar(st[:, i, tok(x)], y(i)[:, tok(x)], mods[:, l, m * NC + c, x:x + 1],
                                             gateb[:, l, which, c, x:x + 1], ALU.mult, ALU.add))
                own()
                cs = cols(l)
                v.scalar_tensor_tensor(out=X[:, 2 * j:2 * j + 2, cs], in0=X[:, 2 * j:2 * j + 2, cs], scalar=ALPHA,
                                       in1=st[:, 0:2, cs], op0=ALU.mult, op1=ALU.add).then_inc(dve_step_done, 1)
                done["parts"] += 1

            for s in SCHEDULE:
                if s[0] in UNIT and UNIT_NO[s] + 2 < len(UNITS):
                    ahead = UNITS[UNIT_NO[s] + 2]
                    if ahead in SPLIT_NO:
                        lo(ahead)
                if s[0] in DVE_PART:
                    part(s)



def constants():
    con = np.zeros((P, NCON), np.float64)

    def put(name, x):
        con[:x.shape[0], CON[name]:CON[name] + x.shape[1]] = x

    t = np.arange(S).reshape(P, 2).T
    ang = np.pi * (2 * np.arange(P)[None, None, :] + 1) * t[:, :, None] / T
    f = np.stack([np.cos(ang), np.sin(ang)])
    put("hy_fwd", f.transpose(2, 0, 1, 3).reshape(P, -1))
    put("hy_inv", f.transpose(3, 0, 1, 2).reshape(P, -1))
    w = 2 * np.pi * (np.outer(np.arange(S), np.arange(S)) % S) / S
    put("fnet", np.stack([np.cos(w), np.sin(w)], 1).reshape(2, P, 2, S).transpose(1, 0, 2, 3).reshape(P, -1))
    inv_freq = 10000.0 ** (-np.arange(32) * 2.0 / 64)
    pos = np.stack([np.arange(S) // GRID_W, np.arange(S) % GRID_W])
    p = np.arange(P)
    a = inv_freq[p % 32][:, None] * pos[p // 64]
    put("rope_cos", np.cos(a))
    put("rope_sin", np.sin(a) * np.where(p % 64 < 32, -1.0, 1.0)[:, None])
    put("swap", np.eye(P)[p ^ 32])
    put("ident", np.eye(P))
    put("ones", np.ones((P, P)))
    tt = np.linspace(0.0, 1.0, S)
    ww = (2 * np.pi / S) * np.arange(S)
    ff = np.linspace(1e-4, BANDS - 1, BANDS)
    emb = np.concatenate([tt[None], np.cos(ff[:, None] * ww), -np.sin(ff[:, None] * ww)])
    emb = np.ascontiguousarray(emb.reshape(EMB, P, 2).transpose(0, 2, 1).reshape(EMB, S).astype(np.float32))
    put("notfirst", (p > 0).astype(float)[:, None])
    for n, e in (("epsln", LN_EPS), ("epsrms", RMS_EPS), ("epskern", KERN_EPS)):
        put(n, np.full((P, 1), e))
    lo, hi = math.log(1e-2) / 0.3, math.log(1e-2) / 1.5
    deltas = np.abs(np.linspace(lo, hi, D))
    decay = np.exp(-tt[:, None] * deltas)
    decay = decay.reshape(P, 2, NG, UC).transpose(2, 0, 1, 3)
    return con.astype(np.float32), emb, np.ascontiguousarray(decay.astype(np.float32))


def unit_source(w, s):
    kind, l = s[0], s[1]
    col = {"ada": lambda: 256 * s[2], "hy": lambda: OFF_HY + D * s[3] + UC * s[2],
           "gate": lambda: OFF_G + D * s[2] + UC * s[3], "fn": lambda: OFF_FN + UC * s[2],
           "k": lambda: OFF_K, "v": lambda: OFF_V, "q": lambda: UC * s[2], "out": lambda: UC * s[2],
           "proj": lambda: UC * s[3], "mlp1": lambda: D * s[2] + UC * s[3], "mlp2": lambda: UC * s[3]}[kind]()
    name = {"ada": "w_ada", "out": "w_out", "mlp1": "w_mlp1", "mlp2": "w_mlp2"}.get(kind, "w_in")
    if kind == "proj":
        name = ("w_att_o", "w_hy_o", "w_fn_o")[s[2]]
    rows = slice(D * s[2], D * s[2] + D) if kind == "mlp2" else slice(0, D)
    return w[name][l, rows, col:col + UC].reshape(NC, P, UC).transpose(1, 0, 2)


def kernel(**inputs):
    from concourse import bacc
    from concourse.bass_utils import run_bass_kernel_spmd

    w = {k: np.asarray(x) for k, x in inputs.items()}
    chunks = lambda x: x.reshape(-1, P).T
    wts = np.empty((len(UNITS), P, NC, UC), np.float32)
    for u, s in enumerate(UNITS):
        wts[u] = unit_source(w, s)
    vecs = np.zeros((P, DEPTH, NVEC), np.float32)
    for l in range(DEPTH):
        for name, at in VEC.items():
            x = w[name][l].reshape(-1)
            if x.size < P:
                vecs[:x.size, l, at] = x
            else:
                vecs[:, l, at:at + x.size // P] = chunks(x)
    tokens = np.concatenate([w["ctx"][0], w["x"][0]])
    con, emb, decay = constants()
    arrays = {
        "wts": wts.reshape(len(UNITS), P, UW),
        "vecs": vecs,
        "cons": con,
        "dec": decay,
        "emb": emb,
        "xt": np.ascontiguousarray(tokens.T.reshape(NC, P, T).transpose(1, 0, 2)),
        "ct": np.ascontiguousarray(np.stack([w["c_ctx"], w["c"][0]], -1).reshape(NC, P, 2).transpose(1, 0, 2)),
        "fw1": np.ascontiguousarray(w["hy_w1"].transpose(1, 0, 2)),
        "fw2": np.ascontiguousarray(w["hy_w2"].transpose(1, 0, 2)),
        "fw3": np.ascontiguousarray(w["hy_w3"].reshape(DEPTH, FH, 2, 2, NG, UC).transpose(0, 4, 3, 1, 2, 5))
        .reshape(DEPTH, NG, 2, FH, 2 * UC),
        "bv": np.ascontiguousarray(w["b_in"][None, :, OFF_V:OFF_HY]),
    }
    nc = bacc.Bacc("TRN2", target_bir_lowering=False, num_devices=1, dynamic_dma_scratch_size=4096)
    aps = {k: nc.dram_tensor("in_" + k, x.shape, F32, kind="ExternalInput").ap() for k, x in arrays.items()}
    out = nc.dram_tensor("out", (P, NC, S), F32, kind="ExternalOutput").ap()
    build_program(nc, aps, out)
    r = run_bass_kernel_spmd(nc, [{"in_" + k: x for k, x in arrays.items()}], core_ids=[0])
    y = np.asarray(r.results[0]["out"])
    return np.ascontiguousarray(y.transpose(2, 1, 0).reshape(1, S, D))
```

```python
import math
from contextlib import ExitStack

import numpy as np
import concourse.bass as bass
from concourse import mybir

F32 = mybir.dt.float32
F32R = mybir.dt.float32r
ALU = mybir.AluOpType
ACT = mybir.ActivationFunctionType
AX = mybir.AxisListType

P = 128
D = 1024
NC = D // P
S = 256
T = 2 * S
DEPTH = 2
HEAD = 128
NH = D // HEAD
NKV = 2
GRID_W = 64
FF = 4 * D
OFF_K = D
OFF_V = OFF_K + NKV * HEAD
OFF_HY = OFF_V + NKV * HEAD
OFF_FN = OFF_HY + 3 * D
OFF_G = OFF_FN + D
D_IN = OFF_G + 3 * D
UC = 256
UW = NC * UC
NG = D // UC
BANDS = 16
EMB = 1 + 2 * BANDS
FH = 64
ALPHA = (2 * DEPTH) ** 0.25
LN_EPS = 1e-6
RMS_EPS = 1e-6
KERN_EPS = 1e-6
ATTN_SCALE = HEAD ** -0.5
RAW = 3
TWO_PI = 2.0 * math.pi
PI_HI = 6.28125
PI_LO = TWO_PI - PI_HI
ROUND = 1.5 * 2.0 ** 23
BELOW_PI = 3.1415925

NF = P + 1
VEC = {}
_at = 0
for _name, _n in (("b_in", D_IN // P), ("b_ada", 6 * NC), ("b_mlp1", FF // P), ("b_mlp2", NC), ("b_out", NC),
                  ("ln1_g", NC), ("ln1_b", NC), ("ln2_g", NC), ("ln2_b", NC), ("conv_w", 9 * NC),
                  ("conv_b", 3 * NC), ("hy_skip", 2 * NC), ("q_gain", 1), ("k_gain", 1),
                  ("hy_b1", 1), ("hy_freq1", 1), ("hy_b2", 1), ("hy_freq2", 1)):
    VEC[_name] = _at
    _at += _n
NVEC = _at

CON = {}
_at = 0
for _name, _n in (("hy_fwd", 4 * P), ("hy_inv", 4 * P), ("fnet", 4 * S), ("rope_cos", S), ("rope_sin", S),
                  ("swap", P), ("ident", P), ("ones", P), ("notfirst", 1), ("epsln", 1), ("epsrms", 1), ("epskern", 1)):
    CON[_name] = _at
    _at += _n
NCON = _at



def halves(*units):
    out = []
    for u in units:
        out += [[u]] if u[0] == "ada" else [[("half", u)], [u]]
    return out


def woven(pieces, groups):
    out = []
    for n, g in enumerate(groups):
        out += g
        for p in pieces[len(pieces) * n // len(groups):len(pieces) * (n + 1) // len(groups)]:
            out += p
    return out


def ada(l, js):
    out, js = [], list(js)
    for n, j in enumerate(js):
        out.append([("ada", l, j)] + ([("adaT", l, js[n - 1])] if n else []))
    if js:
        out.append([("adaT", l, js[-1])])
    return out


def filters(l, cg, o):
    return [[(k, l, cg, o)] for k in ("K0", "K1", "KN")]


def hyena(l, fills):
    streams = (0, 1) if l == 0 else (1,)
    fills = list(fills)

    def units(cg):
        return [("hy", l, cg, part) for part in (2, 0, 1)]

    first = units(0)
    out = [first[0]] + ([("adaT", 1, 23)] if l else []) + [first[1]] + woven(halves(*first[2:]), [[]] + (filters(l, 0, 0) if l else [[]]))
    gates = {0: [], 1: [], 2: [], 3: [0, 1]} if l == 0 else {0: [0], 1: [1], 2: [], 3: [2, 3]}
    norm = []
    for cg in range(NG):
        pieces = halves(*(units(cg + 1) if cg + 1 < NG else []), *[("gate", l, 1, j) for j in gates[cg]])
        n = HY_FILLS[l][cg]
        mine, fills = fills[:n], fills[n:]
        both = []
        for m in range(max(len(pieces), len(mine))):
            both += pieces[m:m + 1] + mine[m:m + 1]
        for o in range(2):
            z = [[(k, l, cg, x, o) for k in "TFI"] for x in streams]
            nk = (l, cg, 1) if o == 0 else (l, cg + 1, 0)
            kk = filters(*nk) if nk[1] < NG and nk != (0, 0, 1) else [[], [], []]
            split = [[("hsplit", l, cg, x)] if o else [] for x in streams]
            if len(z) == 2:
                groups = [[z[0][0], z[1][0]], [z[0][1]], kk[0], [z[1][1]], [z[0][2]] + split[0], kk[1], [z[1][2]],
                          kk[2] + split[1]]
            else:
                groups = [[z[0][0]] + norm, [z[0][1]], kk[0], [z[0][2]] + split[0], [], kk[1]]
                norm = kk[2]
            half = len(both) // 2
            out += woven(both[half * o:half * (o + 1) if o == 0 else None], groups)
    assert not fills
    return out


def fourier(l):
    streams = (0, 1) if l == 0 else (1,)
    more = [("gate", l, 1, 2)] if l == 0 else []
    last = [("gate", l, 1, 3)] if l == 0 else []
    out = [("fn", l, 0), ("fn", l, 1), ("proj", l, 1, 0)] + more + [("proj", l, 1, 1)] + last
    out += [("S1", l, 0, x) for x in streams]
    out += [("proj", l, 1, 2), ("proj", l, 1, 3)]
    out += [("S2", l, 0, x) for x in streams]
    late = halves(("gate", l, 2, 1))
    pieces = [halves(("fn", l, 2), ("gate", l, 2, 0)), halves(("fn", l, 3)) + late[:1], late[1:]]
    for g in range(1, NG):
        groups = [[(k, l, g, x)] for k in ("S1", "S2") for x in streams]
        groups = [groups[0] + groups[1], groups[2] + groups[3]] if l == 0 else groups
        out += woven(pieces[g - 1], groups)
    return out


def attention(l, fills):
    out = [("k", l), ("proj", l, 2, 0), ("KR1", l), ("v", l), ("gate", l, 2, 2), ("KR2", l), ("proj", l, 2, 1),
           ("KR3", l), ("q", l, 0), ("gate", l, 2, 3), ("QR", l, 0), ("proj", l, 2, 2), ("proj", l, 2, 3)]
    items = ITEMS[l]
    per = len(items) // 4
    groups = [[] for _ in range(len(items) + 3)]
    for n, it in enumerate(items):
        groups[n].append(("SC",) + it)
        groups[n + 1].append(("SN",) + it)
        groups[n + 2].append(("TP",) + it)
        groups[n + 3].append(("PV",) + it)
    fills = list(fills)
    for j in range(4):
        if j < 3:
            mine = halves(("q", l, j + 1)) + [[("QR", l, j + 1)]]
        else:
            mine = halves(("gate", l, 0, 0), ("gate", l, 0, 1))
        n = len(fills) // (4 - j)
        mine, fills = (mine[:2] + fills[:n] + mine[2:] if j < 3 else mine + fills[:n]), fills[n:]
        gr = groups[j * per:(j + 1) * per] if j < 3 else groups[j * per:]
        if j < 3 and l:
            out += mine[0] + gr[0] + mine[1] + gr[1] + mine[2]
            out += woven(mine[3:], gr[2:])
        else:
            out += woven(mine, gr)
    out.append(("xback", l))
    out += [("proj", l, 0, 0), ("gate", l, 0, 2), ("proj", l, 0, 1), ("gate", l, 0, 3), ("msplit", l, 0),
            ("msplit", l, 1), ("proj", l, 0, 2), ("msplit", l, 2), ("proj", l, 0, 3), ("msplit", l, 3)]
    return out


def closing(l, which, j=None):
    u = [("mlp2", l, 3, j) if which else ("out", l, j) for j in range(4)]
    at = (l, which)
    out = [u[0], u[1], ("lnp",) + at, ("lnd",) + at + (0,), ("lnd",) + at + (1,)]
    if l == 0:
        out += [("lnsq",) + at + (0,), ("lnsq",) + at + (1,), ("lnf",) + at + (1,), u[2],
                ("lnd",) + at + (2,), ("lnsq",) + at + (2,), ("lnf",) + at + (2,), u[3]]
    else:
        out += [u[2], ("lnsq",) + at + (0,), ("lnsq",) + at + (1,), ("lnd",) + at + (2,), ("lnsq",) + at + (2,), u[3]]
    out += [("lnd",) + at + (3,), ("lnsq",) + at + (3,), ("lnm",) + at, ("lnr",) + at]
    if j is not None:
        out.append(("ada", 1, j))
    if at == (DEPTH - 1, 1):
        for c in range(NC):
            out += [("lnn",) + at + (c,), ("lnx",) + at + (c,)]
        return out
    to = (l, 1) if which == 0 else (l + 1, 0)
    for c in range(NC + 1):
        if c < NC:
            out.append(("lnn",) + at + (c,))
        if c:
            out.append(("hb2",) + to + (c - 1,))
        if c < NC:
            out.append(("hn",) + to + (c,))
    out += [("lnx",) + at + (c,) for c in range(NC)]
    if j is not None:
        CLOSING_ADA.append(("ada", 1, j))
    return out


def modulated(l, which):
    out = [("hb1", l, which, 0)]
    for c in range(NC):
        if c + 1 < NC:
            out.append(("hb1", l, which, c + 1))
        out.append(("hb2", l, which, c))
    return out


def mlp(l):
    out = []

    def up(g):
        for j in range(4):
            out.append(("mlp1", l, g, j))
            out.append(("msq", l, g, j))

    def down(g):
        for j in range(4):
            out.append(("mlp2", l, g, j))

    up(0)
    up(1)
    down(0)
    up(2)
    down(1)
    up(3)
    down(2)
    return out


CLOSING_ADA = []
HY0, AT0, HY1 = 7, 11, 19
HY_FILLS = ((6, 6, 6, 7), (1, 2, 2, 4))


def schedule():
    out = [("silu",)]
    out += woven([x for p in zip(ada(0, range(8)) + [[]]) for x in p],
                 [[], [], [("f1", 0)], [("f1", 1)], [("f2", 0)], [("f2", 1)]] + filters(0, 0, 0) + filters(0, 0, 1))
    out += [("coefA", 0)] + modulated(0, 0)
    for l in range(DEPTH):
        out.append(("hprep", l))
        out += hyena(l, ada(0, range(8, 24)) + ada(1, range(HY0)) if l == 0 else ada(1, range(AT0, HY1)))
        out += fourier(l)
        out += attention(l, ada(1, range(HY0, AT0)) if l == 0 else ada(1, range(HY1, 22)))
        out.append(("coefB", l))
        if l == 0:
            out.append(("coefA", 1))
        out += closing(l, 0, 22 if l == 0 else None)
        m = mlp(l)
        out += m[:1] + ([("adaT", 1, 22)] if l == 0 else []) + m[1:]
        out += closing(l, 1, 23 if l == 0 else None)
    return out


ITEMS = [[(l, h, x, qc) for h in range(NH) for x in ((0, 1) if l == 0 else (1,)) for qc in range(2)]
         for l in range(DEPTH)]
ITEM_NO = {it: n for its in ITEMS for n, it in enumerate(its)}
SCHEDULE = schedule()
UNIT = ("ada", "hy", "gate", "proj", "fn", "k", "v", "q", "out", "mlp1", "mlp2")
AUX = ("f1", "f2", "K0", "K1", "KN", "T", "F", "I", "S1", "S2", "KR1", "KR2", "KR3", "QR", "SC", "TP", "PV",
       "lnp", "lnm", "adaT")
ACT_PART = ("silu", "ada", "adaT", "hy", "gate", "fn", "k", "v", "q", "mlp1", "f1", "f2", "K1", "KN", "T", "F", "I",
            "S1", "S2", "KR1", "QR", "SC", "TP", "PV", "lnm", "lnr", "lnsq", "lnx", "hn", "hb2", "msplit", "msq", "hsplit")
DVE_PART = ("silu", "hy", "proj", "out", "mlp1", "mlp2", "f1", "f2", "K0", "K1", "KN", "F", "I", "S2", "KR1", "KR2",
            "KR3", "QR", "SC", "SN", "PV", "lnp", "lnd", "lnf", "lnm", "lnr", "lnn", "hb1", "hb2", "msplit", "msq",
            "hsplit", "coefA", "coefB", "hprep")
FROM_OTHERS = ("hb2", "S2", "PV", "hsplit", "msq", "hy", "F", "I", "K1", "KR2", "SC", "SN", "K0", "QR", "KR3", "KR1", "mlp1", "lnp", "lnm", "lnr")
AT = {s: n for n, s in enumerate(SCHEDULE)}
UNITS = [s for s in SCHEDULE if s[0] in UNIT]
UNIT_NO = {s: n for n, s in enumerate(UNITS)}
AUXES = [s for s in SCHEDULE if s[0] in AUX]
AUX_NO = {s: n for n, s in enumerate(AUXES)}
PAIR = ("K0", "K1", "F", "S1", "KR2", "QR", "lnm")


def placed():
    user, where, before = [None] * 4, {}, {}
    for s in AUXES:
        sizes = [(b, b + 1) for b in (0, 2)] if s[0] in PAIR else [(b,) for b in range(4)]
        where[s] = min(sizes, key=lambda bs: max(-1 if user[b] is None else AUX_NO[user[b]] for b in bs))
        before[s] = sorted({user[b] for b in where[s]} - {None}, key=AUX_NO.get)
        for b in where[s]:
            user[b] = s
    return where, before


BANKS, BANK_BEFORE = placed()
OPENERS = {s: UNITS[UNIT_NO[s] + 1] for s in UNITS
           if s[0] == "hy" and s[2:] == (0, 2) or s[0] == "mlp1" and s[2:] == (0, 0)}
SPLITS = [s for s in UNITS if s[0] != "ada"]
SPLIT_NO = {s: n for n, s in enumerate(SPLITS)}
AHEAD = {s: UNITS[n + 2] for n, s in enumerate(UNITS[:-2])}
for _s in CLOSING_ADA:
    _n = UNIT_NO[_s]
    AHEAD[UNITS[_n - 2]], AHEAD[UNITS[_n - 1]] = UNITS[_n + 1], UNITS[_n + 2]
    del AHEAD[_s]
EC_NO = {s: n for n, s in enumerate([s for s in SCHEDULE if s[0] in ("K1", "F")])}
Z_NO = {s: n for k in "TFI" for n, s in enumerate([s for s in SCHEDULE if s[0] == k])}
ADA_NO = {s: n for k in ("ada", "adaT") for n, s in enumerate([s for s in SCHEDULE if s[0] == k])}
EC_STEPS, Z_I = list(EC_NO), [s for s in Z_NO if s[0] == "I"]
ADA_T = [s for s in ADA_NO if s[0] == "adaT"]


def ends(part):
    n, out = 0, []
    for s in SCHEDULE:
        n += s[0] in part
        out.append(n)
    return out


ACT_ENDS = ends(ACT_PART)
DVE_ENDS = ends(DVE_PART)
assert len(AT) == len(SCHEDULE)


def build_program(nc, a, out_dram):
    es = ExitStack()
    with es:
        def sb(name, shape, dt=F32):
            return es.enter_context(nc.sbuf_tensor(name, shape, dt))

        def sem(name):
            return es.enter_context(nc.semaphore(name))

        raw = sb("raw", [P, RAW, UW])
        wh = sb("wh", [P, 2, UW], F32R)
        wl = sb("wl", [P, 2, UW], F32R)
        hh = sb("hh", [P, NC, T], F32R)
        hl = sb("hl", [P, NC, T], F32R)
        oh = sb("oh", [P, NC, T], F32R)
        ol = sb("ol", [P, NC, T], F32R)
        xs = sb("xs", [P, NC * T])
        ms = sb("ms", [P, NC * T])
        st = sb("st", [P, 4, T])
        cons = sb("cons", [P, NCON])
        vecs = sb("vecs", [P, DEPTH, NVEC])
        mods = sb("mods", [P, DEPTH, 6 * NC, 2])
        scale1 = sb("scale1", [P, DEPTH, 2, NC, 2])
        gateb = sb("gateb", [P, DEPTH, 2, NC, 2])
        gainb = sb("gainb", [P, DEPTH, NH + NKV])
        convb = sb("convb", [P, DEPTH, 3 * NC])
        cvec = sb("cvec", [P, NC, 2])
        fold = sb("fold", [P, NC])
        csig = sb("csig", [P, NC, 2])
        fh2 = sb("fh2", [FH, DEPTH, S])
        arow = sb("arow", [2, 2, UC])
        hx = sb("hx", [P, 1536])
        ksc = sb("ksc", [P, 2, 2])
        small = sb("small", [P, 48])
        inner = ExitStack()
        s2 = inner.enter_context(nc.sbuf_tensor("s2", [P, 2 * NC * T], F32))
        inner.close()
        bh = sb("bh", [P, NC, T], F32R)
        bl = sb("bl", [P, NC, T], F32R)

        gemm = es.enter_context(nc.psum_tensor("gemm", [P, 4, T], F32))
        aux = es.enter_context(nc.psum_tensor("aux", [P, 4, T], F32))

        raw_in = [sem(f"raw_in{i}") for i in range(RAW)]
        x_in = sem("x_in")
        c_in = sem("c_in")
        vec_in = sem("vec_in")
        w3_in = [sem(f"w3_in{o}") for o in range(2)]
        dec_in = [sem(f"dec_in{n}") for n in range(2)]
        bv_in = sem("bv_in")
        xback_in = sem("xback_in")
        x_kept = sem("x_kept")
        hi_made = sem("hi_made")
        lo_made = sem("lo_made")
        unit_summed = sem("unit_summed")
        aux_summed = sem("aux_summed")
        act_step_done = sem("act_step_done")
        dve_step_done = sem("dve_step_done")
        act_chain = sem("act_chain")
        dve_chain = sem("dve_chain")
        stored = sem("stored")

        x_kept_dram = nc.dram_tensor("x_kept_dram", (P, NC, S), F32, kind="Internal").ap()

        X = xs[:, :].rearrange("p (c t) -> p c t", c=NC)
        M = ms[:, :].rearrange("p (c t) -> p c t", c=NC)

        def con(name, n, parts=P):
            return cons[0:parts, CON[name]:CON[name] + n]

        def vec(l, name, i=0, parts=P):
            return vecs[0:parts, l, VEC[name] + i:VEC[name] + i + 1]

        fwd = con("hy_fwd", 4 * P).rearrange("p (c a k) -> p c a k", c=2, a=2)
        inv = con("hy_inv", 4 * P).rearrange("p (c a k) -> p c a k", c=2, a=2)
        fcs = con("fnet", 4 * S).rearrange("p (k c n) -> p k c n", k=2, c=2)
        rope_c = con("rope_cos", S)
        rope_s = con("rope_sin", S)
        swap = con("swap", P)
        ident = con("ident", P)
        ones = con("ones", P)

        XI = s2[:, 2048:2048 + NC * T].rearrange("p (c t) -> p c t", c=NC)

        pad = s2[:, 0:1032].rearrange("p (i s t) -> p i s t", i=2, s=2)
        hyu = [s2[:, 1040 + 3072 * b:1040 + 3072 * (b + 1)].rearrange("p (x i t) -> p x i t", x=3, i=2) for b in (0, 1)]
        kf = xs[:, 0:2048].rearrange("p (o h c n) -> p o h c n", o=2, h=2, c=2)
        ztb = [xs[:, 2048 + 512 * b:2560 + 512 * b].rearrange("p (a n) -> p a n", a=2) for b in (0, 1)]
        ecb = [xs[:, 3072 + 512 * b:3584 + 512 * b] for b in (0, 1)]
        decb = [x.rearrange("p (a n) -> p a n", a=2) for x in (s2[:, 7184:7696], hx[:, 1024:1536])]
        stw = st[:, :, :].rearrange("p a t -> p (a t)")
        hub = [x.rearrange("p (h c n) -> p h c n", h=2, c=2) for x in (ms[:, 0:1024], stw[:, 0:1024])]
        y1b = [stw[:, 1024 + 512 * b:1536 + 512 * b].rearrange("p (i t) -> p i t", i=2) for b in (0, 1)]
        ksd = hx[:, 0:1024].rearrange("p (c a n) -> p c a n", c=2, a=2)
        ht = ms[:, 1024:2048].rearrange("p (h c n) -> p h c n", h=2, c=2)
        hy_y = ms[:, 2048:3072].rearrange("p (h c n) -> p h c n", h=2, c=2)
        w3 = ms[0:FH, 3072:4096].rearrange("p (o n) -> p o n", o=2)
        fw1 = s2[0:EMB, 0:2 * FH].rearrange("p (l n) -> p l n", l=2)
        fw2 = s2[0:FH, 128:128 + 2 * FH].rearrange("p (l n) -> p l n", l=2)
        emb = s2[0:EMB, 256:256 + S]
        fh1 = [s2[0:FH, 512 + S * l:512 + S * l + S] for l in range(DEPTH)]
        farg = [s2[0:FH, 1024 + S * n:1024 + S * n + S] for n in range(2)]
        def gates(l, b, j):
            at = (1040 if b == 1 else 5120) + 1024 * (j % 2)
            if b == 1 and l:
                at = 1040 + 1024 * j - S
            return s2[:, at:at + 1024].rearrange("p (i t) -> p i t", i=2)

        gtmp = hx[:, 0:1024].rearrange("p (i t) -> p i t", i=2)
        pf = [xs[:, 1024 * b:1024 * (b + 1)].rearrange("p (i t) -> p i t", i=2) for b in (0, 1)]
        xcs = [xs[:, 2048 + 1024 * b:3072 + 1024 * b].rearrange("p (t c n) -> p t c n", t=2, c=4) for b in (0, 1)]
        K = xs[:, 0:1024].rearrange("p (g t) -> p g t", g=2)
        V = xs[:, 1024:2048].rearrange("p (t n) -> p t n", t=4)
        PR = [xs[:, 2048:2560], xs[:, 2560:3072], s2[:, 7168:7680], s2[:, 7680:8192]]
        bv = hx[0:1, 1024:1024 + NKV * HEAD]
        PT = [xs[:, 3072 + 512 * b:3584 + 512 * b].rearrange("p (k q) -> p k q", k=4) for b in (0, 1)]
        QG = [s2[:, 1024 * b:1024 * (b + 1)].rearrange("p (i t) -> p i t", i=2) for b in (0, 1)]
        QSQ = s2[:, 2048:3072].rearrange("p (i t) -> p i t", i=2)
        RT = s2[:, 3072:4096].rearrange("p (k i t) -> p k i t", k=2, i=2)
        DG = s2[:, 4096:5120].rearrange("p (k t) -> p k t", k=8)
        rk = small[:, 0:8]
        rq = [small[:, 8:16], small[:, 16:24]]
        nmax, nbias, rsum, rinv = [[small[:, 24 + 4 * k + n:25 + 4 * k + n] for n in range(4)] for k in range(4)]
        warm = small[:, 40:41]
        ksn = small[:, 44:46]

        pairs = hx[:, 0:1024].rearrange("p (i t) -> p i t", i=2)
        ln_mean, ln_off, ln_rstd = st[:, 2], st[:, 0], st[:, 3]

        def hbuf(l, which, c):
            if (l, which) == (0, 0):
                return st[:, c % 4]
            return (st[:, 1], st[:, 2], pairs[:, 0], pairs[:, 1])[c % 4]

        def cols(l):
            return slice(0, T) if l == 0 else slice(S, T)

        def streams(l):
            return (0, 1) if l == 0 else (1,)

        def toks(l):
            return range(4) if l == 0 else range(2, 4)

        def tok(s):
            return slice(s * S, s * S + S)

        def hidden(g):
            return (oh, ol) if g % 2 == 0 else (bh, bl)

        def acts(step):
            return ACT_ENDS[AT[step]]

        def dves(step):
            return DVE_ENDS[AT[step]]

        def units(step):
            return UNIT_NO[step] + 1

        def auxes(step):
            return AUX_NO[step] + 1

        def bank(step):
            return aux[:, BANKS[step][0]:BANKS[step][-1] + 1]

        block = es.enter_context(nc.Block())

        @block.sync
        def _(sp):
            for u in range(len(UNITS)):
                if u >= RAW:
                    if UNITS[u - RAW] in SPLIT_NO:
                        sp.wait_ge(hi_made, SPLIT_NO[UNITS[u - RAW]] + 1)
                        sp.wait_ge(lo_made, SPLIT_NO[UNITS[u - RAW]] + 1)
                    else:
                        sp.wait_ge(unit_summed, u - RAW + 1)
                sp.dma_start(raw[:, u % RAW], a["wts"][u]).then_inc(raw_in[u % RAW], 16)

        @block.gpsimd
        def _(pool):
            pool.dma_start(cvec[:], a["ct"]).then_inc(c_in, 16)
            pool.dma_start(vecs[:], a["vecs"]).then_inc(vec_in, 16)
            pool.dma_start(cons[:], a["cons"]).then_inc(vec_in, 16)
            pool.dma_start(fw1, a["fw1"]).then_inc(vec_in, 16)
            pool.dma_start(fw2, a["fw2"]).then_inc(vec_in, 16)
            pool.dma_start(emb, a["emb"]).then_inc(vec_in, 16)
            pool.dma_start(XI, a["xt"]).then_inc(x_in, 16)
            for n, s in enumerate(SCHEDULE):
                if s[0] == "f2" and s[1] == 1 or s[0] == "hprep" and s[1]:
                    l = 0 if s[0] == "f2" else s[1]
                    if l:
                        pool.wait_ge(aux_summed, auxes(("lnm", l - 1, 1)))
                    for cg in range(NG):
                        if cg >= 2:
                            pool.wait_ge(dve_step_done, dves(("K0", l, cg - 2, 1)))
                        pool.dma_start(decb[cg % 2], a["dec"][cg]).then_inc(dec_in[cg % 2], 16)
                        for o in range(2):
                            if cg:
                                pool.wait_ge(aux_summed, auxes(("K0", l, cg - 1, o)))
                            pool.dma_start(w3[:, o], a["fw3"][l, cg, o]).then_inc(w3_in[o], 16)
                        if l and cg == 0:
                            pool.wait_ge(act_step_done, acts(("lnx", l - 1, 1, NC - 1)))
                            pool.dma_start(x_kept_dram, X[:, :, S:T]).then_inc(x_kept, 16)
                    pool.wait_ge(aux_summed, auxes(("KN", l, NG - 1, 1)))
                    pool.wait_ge(dve_step_done, dves(("K0", l, NG - 1, 1)))
                    pool.dma_start(bv, a["bv"][:, l]).then_inc(bv_in, 16)
                elif s[0] == "xback":
                    l = s[1]
                    pool.wait_ge(dve_step_done, dves(("PV", l, NH - 1, 1, 1)))
                    if l == 0:
                        pool.dma_start(X, a["xt"]).then_inc(xback_in, 16)
                    else:
                        pool.dma_start(X[:, :, S:T], x_kept_dram).then_inc(xback_in, 16)
            for c in range(1, NC, 2):
                pool.wait_ge(act_step_done, acts(("lnx", DEPTH - 1, 1, c)))
                pool.dma_start(out_dram[:, c - 1:c + 1], X[:, c - 1:c + 1, S:T]).then_inc(stored, 16)
            pool.wait_ge(stored, 16 * (NC // 2))

        @block.tensor
        def _(pe):
            mm = nc.tensor.matmul

            def wait_operands(s, k):
                kind, l = s[0], s[1]
                x = 1
                if kind == "proj" and s[2] == 1:
                    pe.wait_ge(dve_step_done, dves(("hsplit", l, k // 2, x)))
                elif kind == "proj" and s[2] == 2:
                    pe.wait_ge(dve_step_done, dves(("S2", l, k // 2, x)))
                elif kind == "proj":
                    pe.wait_ge(dve_step_done, dves(("PV", l, k, x, 1)))
                elif kind == "out":
                    pe.wait_ge(dve_step_done, dves(("msplit", l, k // 2)))
                elif kind == "mlp1":
                    pe.wait_ge(dve_step_done, dves(("hb2", l, 1, k)))
                elif kind == "mlp2":
                    pe.wait_ge(dve_step_done, dves(("msq", l, s[2], k // 2)))
                else:
                    pe.wait_ge(dve_step_done, dves(("hb2", l, 0, k)))

            def open_unit(s):
                u = UNIT_NO[s]
                if s in SPLIT_NO:
                    pe.wait_ge(lo_made, SPLIT_NO[s] + 1)
                else:
                    pe.wait_ge(raw_in[u % RAW], 16 * (u // RAW + 1))
                if u >= 2:
                    before = UNITS[u - 2]
                    if before[0] in ACT_PART:
                        pe.wait_ge(act_step_done, acts(before))
                    if before[0] in DVE_PART:
                        pe.wait_ge(dve_step_done, dves(before))

            def ada_unit(s):
                u = UNIT_NO[s]
                open_unit(s)
                pe.wait_ge(dve_step_done, dves(("silu",)))
                w = raw[:, u % RAW].rearrange("p (k n) -> p k n", k=NC)
                for k in range(NC):
                    last = mm(gemm[0:2, 2 * (u % 2), 0:UC], csig[:, k], w[:, k], start=(k == 0), stop=(k == NC - 1))
                last.then_inc(unit_summed, 1)

            def v_unit(s):
                l = s[1]
                u, n = UNIT_NO[s], SPLIT_NO[s]
                open_unit(s)
                pe.wait_ge(bv_in, 16 * (l + 1))
                WH, WL = [w[:, n % 2].rearrange("p (k n) -> p k n", k=NC) for w in (wh, wl)]
                for t in range(4):
                    dst = gemm[:, 2 * (u % 2) + t // 2, (t % 2) * UC:(t % 2 + 1) * UC]
                    ts = slice(t * P, t * P + P)
                    mm(dst, ones[0:1, :], bv, start=True, stop=False)
                    for k in range(NC):
                        mm(dst, hl[:, k, ts], WH[:, k], start=False, stop=False)
                        mm(dst, hh[:, k, ts], WH[:, k], start=False, stop=False)
                        last = mm(dst, hh[:, k, ts], WL[:, k], start=False, stop=(k == NC - 1))
                last.then_inc(unit_summed, 1)

            def chunk(s, i):
                kind, l = s[0], s[1]
                u, n = UNIT_NO[s], SPLIT_NO[s]
                if i == 0:
                    open_unit(s)
                first = opens(s)
                mh, ml, cs = hh, hl, cols(l)
                if kind == "proj":
                    mh, ml = oh, ol
                elif kind == "mlp2":
                    mh, ml = hidden(s[2])
                elif kind == "k":
                    cs = slice(0, T)
                if first:
                    both = s in OPENERS
                    if both:
                        open_unit(OPENERS[s])
                    order = [(x, k) for k in range(NC) for x in ((0, 1, 2) if both else (0, 1))]
                    if not both:
                        order = [(x, k) for ks in (range(NC - 2), range(NC - 2, NC)) for x in range(2) for k in ks]
                else:
                    order = [(i, k) for k in range(NC)]
                    if i == 0:
                        wait_operands(s, NC - 1)
                for x, k in order:
                    v_, c = x // 2, x % 2
                    WH, WL = [w[:, (n + v_) % 2].rearrange("p (k n) -> p k n", k=NC) for w in (wh, wl)]
                    dst = gemm[:, 2 * ((u + v_) % 2) + c, cs]
                    ws = slice(c * P, c * P + P)
                    if first and x == 0:
                        wait_operands(s, k)
                    mm(dst, WL[:, k, ws], mh[:, k, cs], start=(k == 0), stop=False)
                    mm(dst, WH[:, k, ws], mh[:, k, cs], start=False, stop=False)
                    last = mm(dst, WH[:, k, ws], ml[:, k, cs], start=False, stop=(k == NC - 1))
                    if first and (x, k) == (1, NC - 1):
                        last.then_inc(unit_summed, 1)
                if i:
                    last.then_inc(unit_summed, 1)

            def opens(s):
                return s[2:] == (0, 2) if s[0] == "hy" else s[0] in ("proj", "out", "mlp1", "mlp2") and s[-1] == 0

            def aux_step(s):
                kind, l = s[0], s[1]
                A = bank(s)
                for before in BANK_BEFORE[s]:
                    if before[0] in ACT_PART:
                        pe.wait_ge(act_step_done, acts(before))
                    if before[0] in DVE_PART:
                        pe.wait_ge(dve_step_done, dves(before))
                if kind == "adaT":
                    pe.wait_ge(act_step_done, acts(("ada",) + s[1:]))
                    pe.wait_ge(vec_in, 80)
                    for i in range(2):
                        last = mm(A[:, 0, 2 * i:2 * i + 2], arow[:, ADA_NO[s] % 2, i * P:i * P + P], ident[0:2, 0:2],
                                  start=True, stop=True)
                elif kind == "f1":
                    pe.wait_ge(vec_in, 80)
                    last = mm(A[0:FH, 0, 0:S], fw1[:, l], emb, start=True, stop=True)
                elif kind == "f2":
                    pe.wait_ge(act_step_done, acts(("f1", l)))
                    last = mm(A[0:FH, 0, 0:S], fw2[:, l], fh1[l], start=True, stop=True)
                elif kind == "K0":
                    _, _, cg, o = s
                    pe.wait_ge(act_step_done, acts(("f2", l)))
                    pe.wait_ge(w3_in[o], 16 * (NG * l + cg + 1))
                    for par in range(2):
                        last = mm(A[:, par], fh2[:, l, par * P:par * P + P], w3[:, o], start=True, stop=True)
                elif kind == "KN":
                    _, _, cg, o = s
                    pe.wait_ge(act_step_done, acts(("K1", l, cg, o)))
                    for i in range(2):
                        for q in range(4):
                            last = mm(A[:, 0, i:i + 1], ksd[:, q // 2, q % 2, i * P:i * P + P], ones[:, 0:1],
                                      start=(q == 0), stop=(q == 3))
                elif kind == "K1":
                    _, _, cg, o = s
                    pe.wait_ge(dve_step_done, dves(("K0", l, cg, o)))
                    for par in range(2):
                        for c in range(2):
                            last = mm(A[:, par, c * UC:(c + 1) * UC], fwd[:, c, par], ksd[:, c, par],
                                      start=True, stop=True)
                elif kind == "T":
                    _, _, cg, st_, o = s
                    if o == 0:
                        pe.wait_ge(dve_step_done, dves(("hy", l, cg, 2)))
                    else:
                        pe.wait_ge(dve_step_done, dves(("I", l, cg, st_, 0)))
                    z = hyu[cg % 2][:, 2]
                    for par in range(2):
                        for i in range(2):
                            src = z[:, i, tok(st_)].rearrange("p (t a) -> p a t", a=2)[:, par]
                            last = nc.tensor.transpose(A[:, 0, par * UC + i * P:par * UC + (i + 1) * P], src, ident)
                elif kind == "F":
                    pe.wait_ge(act_step_done, acts(("T",) + s[1:]))
                    for par in range(2):
                        for c in range(2):
                            last = mm(A[:, par, c * UC:(c + 1) * UC], fwd[:, c, par], ztb[Z_NO[s] % 2][:, par],
                                      start=True, stop=True)
                elif kind == "I":
                    pe.wait_ge(dve_step_done, dves(("F",) + s[1:]))
                    for i in range(2):
                        for par in range(2):
                            for c in range(2):
                                last = mm(A[:, 0, (2 * i + par) * P:(2 * i + par + 1) * P],
                                          hub[Z_NO[s] % 2][:, par, c, i * P:i * P + P], inv[:, c, par],
                                          start=(c == 0), stop=(c == 1))
                elif kind == "S1":
                    _, _, g, st_ = s
                    pe.wait_ge(act_step_done, acts(("fn", l, g)))
                    for t in range(2):
                        for c in range(2):
                            for k in range(2):
                                last = mm(A[:, t, c * NF:(c + 1) * NF],
                                          pf[g % 2][:, k, st_ * S + t * P:st_ * S + (t + 1) * P],
                                          fcs[:, k, c, 0:NF], start=(k == 0), stop=(k == 1))
                elif kind == "S2":
                    _, _, g, st_ = s
                    pe.wait_ge(act_step_done, acts(("S1", l, g, st_)))
                    for i in range(2):
                        for t in range(2):
                            for c in range(2):
                                last = mm(A[:, 0, i * S:(i + 1) * S], xcs[st_][:, t, 2 * c + i],
                                          fcs[:, t, c], start=(t == 0 and c == 0), stop=(t == 1 and c == 1))
                elif kind in ("KR1", "QR"):
                    if kind == "QR":
                        j = s[2]
                        pe.wait_ge(act_step_done, acts(("q", l, j)))
                        r = toks(l)
                    else:
                        pe.wait_ge(act_step_done, acts(("k", l)))
                        r = range(4)
                    for i in range(2):
                        for t in r:
                            last = mm(A[:, 0, 4 * i + t:4 * i + t + 1], QSQ[:, i, t * P:t * P + P], ones[:, 0:1],
                                      start=True, stop=True)
                    if kind == "QR":
                        for i in range(2):
                            last = mm(A[:, 1, i * S:(i + 1) * S], swap, QG[j % 2][:, i, S:T], start=True, stop=True)
                elif kind == "KR2":
                    pe.wait_ge(dve_step_done, dves(("KR1", l)))
                    for i in range(2):
                        for t in range(4):
                            last = mm(A[:, i, t * P:t * P + P], ones, DG[:, 4 * i + t], start=True, stop=True)
                elif kind == "KR3":
                    pe.wait_ge(dve_step_done, dves(("KR2", l)))
                    for i in range(2):
                        last = mm(A[:, 0, i * S:(i + 1) * S], swap, K[:, i, S:T], start=True, stop=True)
                elif kind == "SC":
                    _, _, h, st_, qc = s
                    pe.wait_ge(dve_step_done, dves(("QR", l, h // 2)))
                    pe.wait_ge(dve_step_done, dves(("KR3", l)))
                    at = st_ * S + qc * P
                    keys = slice(0, T) if st_ else slice(0, S)
                    last = mm(A[:, 0, keys], QG[h // 2 % 2][:, h % 2, at:at + P], K[:, h // 4, keys],
                              start=True, stop=True)
                elif kind == "TP":
                    _, _, h, st_, qc = s
                    pe.wait_ge(dve_step_done, dves(("SN",) + s[1:]))
                    for kc in range(4 if st_ else 2):
                        last = nc.tensor.transpose(A[:, 0, kc * P:kc * P + P], PR[ITEM_NO[s[1:]] % 4][:, kc * P:kc * P + P], ident)
                elif kind == "PV":
                    _, _, h, st_, qc = s
                    pe.wait_ge(act_step_done, acts(("TP",) + s[1:]))
                    pe.wait_ge(act_step_done, acts(("v", l)))
                    n = 4 if st_ else 2
                    for kc in range(n):
                        last = mm(A[:, 0, 0:P], V[:, kc, h // 4 * P:h // 4 * P + P], PT[ITEM_NO[s[1:]] % 2][:, kc],
                                  start=(kc == 0), stop=(kc == n - 1))
                elif kind == "lnp":
                    which = s[2]
                    pe.wait_ge(dve_step_done, dves(("mlp2", l, 3, 0) if which else ("out", l, 0)))
                    for c in range(2):
                        last = mm(A[:, 0, cols(l)], ones, X[:, c, cols(l)], start=(c == 0), stop=(c == 1))
                elif kind == "lnm":
                    at, cs = s[1:], cols(l)
                    if l == 0:
                        pe.wait_ge(dve_step_done, dves(("lnf",) + at + (2,)))
                        for i in range(2):
                            mm(A[:, 0, cs], ones, pairs[:, i, cs], start=(i == 0), stop=False)
                            mm(A[:, 1, cs], ones, M[:, i, cs], start=(i == 0), stop=False)
                    else:
                        for c in range(6):
                            pe.wait_ge(act_step_done, acts(("lnsq",) + at + (c // 2,)))
                            mm(A[:, 1, cs], ones, M[:, c, cs], start=(c == 0), stop=False)
                            if c >= 2:
                                mm(A[:, 0, cs], ones, X[:, c, cs], start=(c == 2), stop=False)
                    pe.wait_ge(dve_step_done, dves(("lnd",) + at + (3,)))
                    for c in (6, 7):
                        mm(A[:, 0, cs], ones, X[:, c, cs], start=False, stop=(c == 7))
                    pe.wait_ge(act_step_done, acts(("lnsq",) + at + (3,)))
                    for c in (6, 7):
                        last = mm(A[:, 1, cs], ones, M[:, c, cs], start=False, stop=(c == 7))
                last.then_inc(aux_summed, 1)

            for n, s in enumerate(SCHEDULE):
                if s[0] == "half":
                    chunk(s[1], 0)
                elif s[0] == "ada":
                    ada_unit(s)
                elif s[0] == "v":
                    v_unit(s)
                elif s[0] in UNIT:
                    if ("half", s) not in AT and s not in OPENERS.values():
                        chunk(s, 0)
                    if not opens(s):
                        chunk(s, 1)
                elif s[0] in AUX:
                    aux_step(s)

        @block.scalar
        def _(act):
            act_fn = nc.scalar.activation
            done = {"chain": 0}

            def hi(s):
                u, n = UNIT_NO[s], SPLIT_NO[s]
                act.wait_ge(raw_in[u % RAW], 16 * (u // RAW + 1))
                if n >= 2:
                    act.wait_ge(unit_summed, units(SPLITS[n - 2]))
                    act.wait_ge(lo_made, n - 1)
                act_fn(wh[:, n % 2], raw[:, u % RAW], ACT.Copy).then_inc(hi_made, 1)

            def part(s):
                kind = s[0]
                l = s[1] if len(s) > 1 else 0
                cs = cols(l)
                last = None
                if kind in UNIT:
                    u = UNIT_NO[s]
                    act.wait_ge(unit_summed, units(s))
                    g = [gemm[:, 2 * (u % 2) + i] for i in range(2)]
                elif kind in AUX:
                    act.wait_ge(aux_summed, auxes(s))
                    A = bank(s)
                if kind == "silu":
                    act.wait_ge(c_in, 16)
                    last = act_fn(csig[:], cvec[:], ACT.Sigmoid)
                elif kind == "ada":
                    n = ADA_NO[s]
                    if n >= 2:
                        act.wait_ge(aux_summed, auxes(ADA_T[n - 2]))
                    last = act_fn(arow[:, n % 2], g[0][0:2, 0:UC], ACT.Copy)
                elif kind == "adaT":
                    j = s[2]
                    act.wait_ge(vec_in, 80)
                    for i in range(2):
                        last = act_fn(mods[:, l, 2 * j + i], A[:, 0, 2 * i:2 * i + 2], ACT.Identity,
                                      bias=vec(l, "b_ada", 2 * j + i))
                        if i == 0:
                            last.then_inc(act_chain, 1)
                            done["chain"] += 1
                    act.wait_ge(act_chain, done["chain"])
                elif kind == "hy":
                    _, _, cg, part_ = s
                    before = {(2): (cg - 1, 1), (0): (cg, 2), (1): (cg, 0)}[part_]
                    act.wait_ge(dve_step_done, dves(("hy", l) + before if before[0] >= 0 else ("hprep", l)))
                    n0, n1 = (0, 2) if l == 0 else (1, 2)
                    for i in range(2):
                        c = NC * part_ + 2 * cg + i
                        act_fn(hyu[cg % 2][:, part_, i, cs], g[i][:, cs], ACT.Identity,
                               scale=vec(l, "conv_w", 3 * NC + c), bias=convb[:, l, c:c + 1]).then_inc(act_chain, 1)
                        last = act_fn(pad[:, i, n0:n1, 1:S + 1],
                                      g[i][:, cs].rearrange("p (s t) -> p s t", t=S), ACT.Identity,
                                      bias=vec(l, "b_in", OFF_HY // P + c))
                    done["chain"] += 2
                    act.wait_ge(act_chain, done["chain"])
                elif kind == "gate":
                    _, _, b, j = s
                    if b == 1 and l:
                        act.wait_ge(dve_step_done, dves(("hprep", l)))
                    elif j >= 2:
                        act.wait_ge(dve_step_done, dves(("proj", l, b, j - 2)))
                    elif b == 1:
                        act.wait_ge(dve_step_done, dves(("hsplit", l, NG - 2, 1)))
                    elif b == 2:
                        act.wait_ge(dve_step_done, dves(("hsplit", l, NG - 1, 1)))
                    else:
                        act.wait_ge(dve_step_done, dves(("proj", l, 2, NG - 1)))
                    G = gates(l, b, j)
                    for i in range(2):
                        last = act_fn(G[:, i, cs], g[i][:, cs], ACT.Sigmoid,
                                      bias=vec(l, "b_in", OFF_G // P + NC * b + 2 * j + i))
                elif kind == "fn":
                    gr = s[2]
                    if gr == 0:
                        act.wait_ge(dve_step_done, dves(("hsplit", l, NG - 1, 1)))
                    for i in range(2):
                        last = act_fn(pf[gr % 2][:, i, cs], g[i][:, cs], ACT.Identity,
                                      bias=vec(l, "b_in", OFF_FN // P + 2 * gr + i))
                elif kind in ("k", "q"):
                    if kind == "k":
                        c0, dst, gain, cs = OFF_K // P, K, vec(l, "k_gain"), slice(0, T)
                        act.wait_ge(aux_summed, auxes(("S2", l, NG - 1, 1)))
                        gb = NH
                    else:
                        j = s[2]
                        c0, dst, gain = 2 * j, QG[j % 2], vec(l, "q_gain")
                        gb = 2 * j
                        if j >= 2:
                            act.wait_ge(aux_summed, auxes(("SC", l, 2 * j - 3, 1, 1)))
                    for i in range(2):
                        act_fn(QSQ[:, i, cs], g[i][:, cs], ACT.Square,
                               bias=vec(l, "b_in", c0 + i)).then_inc(act_chain, 1)
                        done["chain"] += 1
                        last = act_fn(dst[:, i, cs], g[i][:, cs], ACT.Identity, scale=gain,
                                      bias=gainb[:, l, gb + i:gb + i + 1])
                    act.wait_ge(act_chain, done["chain"])
                elif kind == "v":
                    for i in range(2):
                        last = act_fn(V[:, 2 * i:2 * i + 2], g[i].rearrange("p (t n) -> p t n", t=2), ACT.Copy)
                elif kind == "mlp1":
                    _, _, gr, j = s
                    act.wait_ge(dve_step_done, dves(SCHEDULE[AT[s] - 1]))
                    for i in range(2):
                        last = act_fn(st[:, i, cs], g[i][:, cs], ACT.Relu, bias=vec(l, "b_mlp1", 8 * gr + 2 * j + i))
                elif kind == "msq":
                    _, _, gr, j = s
                    if gr >= 2 and j == 0:
                        act.wait_ge(unit_summed, units(("mlp2", l, gr - 2, 3)))
                    if gr == 0 and j == 0:
                        act.wait_ge(unit_summed, units(("proj", l, 0, NG - 1)))
                    act.wait_ge(dve_step_done, dves(("mlp1", l, gr, j)))
                    for i in range(2):
                        last = act_fn(hidden(gr)[0][:, 2 * j + i, cs], st[:, 2 + i, cs], ACT.Copy)
                elif kind in ("f1", "f2"):
                    act.wait_ge(dve_step_done, dves(s))
                    last = act_fn(fh1[l] if kind == "f1" else fh2[:, l], farg[1], ACT.Sin)
                elif kind == "KN":
                    last = act_fn(ksn, A[:, 0, 0:2], ACT.Sqrt, scale=0.5, bias=con("epskern", 1))
                elif kind in ("K1", "F"):
                    n = EC_NO[s]
                    if n >= 2:
                        act.wait_ge(dve_step_done, dves(EC_STEPS[n - 2]))
                    if s == ("K1", 1, 0, 0):
                        act.wait_ge(x_kept, 16)
                    last = act_fn(ecb[n % 2], A[:, 0], ACT.Copy)
                    if kind == "K1":
                        last.then_inc(act_chain, 1)
                        done["chain"] += 1
                        last = act_fn(ksd, ksd, ACT.Square)
                        act.wait_ge(act_chain, done["chain"])
                elif kind == "T":
                    last = act_fn(ztb[Z_NO[s] % 2], A[:, 0].rearrange("p (a n) -> p a n", a=2), ACT.Copy)
                elif kind == "I":
                    _, _, cg, st_, o = s
                    n = Z_NO[s]
                    if n >= 2:
                        act.wait_ge(dve_step_done, dves(Z_I[n - 2]))
                    act.wait_ge(dve_step_done, dves(("KN", l, cg, o)))
                    for i in range(2):
                        last = act_fn(y1b[n % 2][:, i].rearrange("p (t a) -> p a t", a=2),
                                      A[:, 0, i * UC:(i + 1) * UC].rearrange("p (a t) -> p a t", a=2),
                                      ACT.Identity, scale=ksc[:, o, i:i + 1])
                elif kind == "hsplit":
                    _, _, cg, st_ = s
                    act.wait_ge(dve_step_done, dves(("I", l, cg, st_, 1)))
                    if cg == 0 and st_ == streams(l)[0] and l:
                        act.wait_ge(unit_summed, units(("mlp2", l - 1, 2, 3)))
                    last = act_fn(oh[:, 2 * cg:2 * cg + 2, tok(st_)], hyu[cg % 2][:, 2, :, tok(st_)], ACT.Copy)
                elif kind == "S1":
                    _, _, gr, st_ = s
                    for i in range(2):
                        act_fn(xcs[st_][:, :, i], A[:, :, i:P + i], ACT.Copy, scale=1.0 / S).then_inc(act_chain, 1)
                    done["chain"] += 3
                    act_fn(xcs[st_][:, :, 2], A[:, :, NF:NF + P], ACT.Copy, scale=-1.0 / S).then_inc(act_chain, 1)
                    last = act_fn(xcs[st_][:, :, 3], A[:, :, NF + 1:NF + 1 + P], ACT.Copy, scale=1.0 / S)
                    act.wait_ge(act_chain, done["chain"])
                elif kind == "S2":
                    _, _, gr, st_ = s
                    if gr == 0 and st_ == streams(l)[0]:
                        act.wait_ge(unit_summed, units(("proj", l, 1, NG - 1)))
                    last = act_fn(oh[:, 2 * gr:2 * gr + 2, tok(st_)], A[:, 0].rearrange("p (i t) -> p i t", i=2),
                                  ACT.Copy)
                elif kind == "KR1":
                    last = act_fn(rk, A[:, 0, 0:8], ACT.Sqrt, scale=1.0 / HEAD, bias=con("epsrms", 1))
                elif kind == "QR":
                    j = s[2]
                    t0 = toks(l)[0]
                    last = act_fn(rq[j % 2].rearrange("p (i t) -> p i t", i=2)[:, :, t0:4],
                                  A[:, 0, 0:8].rearrange("p (i t) -> p i t", i=2)[:, :, t0:4],
                                  ACT.Sqrt, scale=1.0 / HEAD, bias=con("epsrms", 1))
                elif kind == "SC":
                    _, _, h, st_, qc = s
                    act.wait_ge(dve_step_done, dves(s))
                    keys = slice(0, T) if st_ else slice(0, S)
                    col = 4 * (h % 2) + 2 * st_ + qc
                    n = ITEM_NO[s[1:]] % 4
                    last = act_fn(PR[n][:, keys], A[:, 0, keys], ACT.Exp, bias=nbias[n],
                                  scale=rq[h // 2 % 2][:, col:col + 1], accum_out=rsum[n])
                elif kind == "TP":
                    _, _, h, st_, qc = s
                    n = 4 if st_ else 2
                    last = act_fn(PT[ITEM_NO[s[1:]] % 2][:, 0:n], A[:, 0, 0:n * P].rearrange("p (k q) -> p k q", k=n), ACT.Copy)
                elif kind == "PV":
                    _, _, h, st_, qc = s
                    if h == 0:
                        act.wait_ge(unit_summed, units(("proj", l, 2, NG - 1)))
                    at = st_ * S + qc * P
                    last = act_fn(oh[:, h, at:at + P], A[:, 0, 0:P], ACT.Copy)
                elif kind == "msplit":
                    _, _, j = s
                    if j == 0:
                        act.wait_ge(unit_summed, units(("gate", l, 0, NG - 1)))
                    act.wait_ge(dve_step_done, dves(("proj", l, 0, j)))
                    last = act_fn(hh[:, 2 * j:2 * j + 2, cs], M[:, 2 * j:2 * j + 2, cs], ACT.Copy)
                elif kind == "lnsq":
                    q = s[3]
                    if q == 0:
                        act_fn(warm, con("epsln", 1), ACT.Sqrt)
                    act.wait_ge(dve_step_done, dves(("lnd",) + s[1:]))
                    last = act_fn(M[:, 2 * q:2 * q + 2, cs], X[:, 2 * q:2 * q + 2, cs], ACT.Square)
                elif kind == "lnm":
                    last = act_fn(st[:, 1, cs], A[:, 0, cs], ACT.Square, scale=1.0 / D)
                elif kind == "lnr":
                    act.wait_ge(dve_step_done, dves(("lnm",) + s[1:]))
                    last = act_fn(ln_rstd[:, cs], ln_rstd[:, cs], ACT.Sqrt, bias=con("epsln", 1))
                elif kind == "lnx":
                    _, _, which, c = s
                    n = "ln2" if which else "ln1"
                    if (l, which) == (DEPTH - 1, 1):
                        act.wait_ge(dve_step_done, dves(("lnn", l, which, c)))
                    cs = slice(S, T) if which else cs
                    last = act_fn(X[:, c, cs], X[:, c, cs], ACT.Identity, scale=vec(l, n + "_g", c),
                                  bias=vec(l, n + "_b", c))
                elif kind == "hn":
                    _, _, which, c = s
                    act.wait_ge(dve_step_done, dves(("lnn", l, 0, c) if which else ("lnn", l - 1, 1, c)))
                    if c >= 4:
                        act.wait_ge(dve_step_done, dves(("hb2", l, which, c - 4)))
                    for x in (streams(l) if which else (0, 1)):
                        if x == 1 and (not which or l == 0):
                            last.then_inc(act_chain, 1)
                            done["chain"] += 1
                        last = act_fn(hbuf(l, which, c)[:, tok(x)], X[:, c, tok(x)], ACT.Identity,
                                      scale=scale1[:, l, which, c, x:x + 1],
                                      bias=mods[:, l, 3 * which * NC + c, x:x + 1])
                elif kind == "hb2":
                    _, _, which, c = s
                    if c == 0 and which:
                        act.wait_ge(unit_summed, units(("out", l, NG - 1)))
                    elif c == 0 and l:
                        act.wait_ge(unit_summed, units(("mlp1", l - 1, 3, 3)))
                    if (l, which) == (0, 0):
                        act.wait_ge(dve_step_done, dves(("hb1", l, which, c)))
                    else:
                        act.wait_ge(act_step_done, acts(("hn", l, which, c)))
                        act.wait_ge(act_chain, done["chain"])
                    full = slice(0, T) if not which else cs
                    last = act_fn(hh[:, c, full], hbuf(l, which, c)[:, full], ACT.Copy)
                last.then_inc(act_step_done, 1)

            for s in SCHEDULE:
                if s in AHEAD:
                    ahead = AHEAD[s]
                    if ahead in SPLIT_NO:
                        hi(ahead)
                if s[0] in ACT_PART:
                    part(s)

        @block.vector
        def _(dve):
            v = nc.vector
            done = {"chain": 0, "parts": 0}

            def link(ins):
                ins.then_inc(dve_chain, 1)
                done["chain"] += 1
                dve.wait_ge(dve_chain, done["chain"])

            def also(ins):
                ins.then_inc(dve_chain, 1)
                done["chain"] += 1

            def own():
                if done["chain"]:
                    dve.wait_ge(dve_chain, done["chain"])
                if done["parts"]:
                    dve.wait_ge(dve_step_done, done["parts"])

            def lo(s):
                u, n = UNIT_NO[s], SPLIT_NO[s]
                dve.wait_ge(hi_made, n + 1)
                v.tensor_tensor(wl[:, n % 2], raw[:, u % RAW], wh[:, n % 2].bitcast(F32),
                                ALU.subtract).then_inc(lo_made, 1)

            def with_norm(l, which, ln, n):
                g, b = [vecs[:, ln, VEC[n + k]:VEC[n + k] + NC] for k in ("_g", "_b")]
                for x in range(2):
                    own()
                    scale, shift = scale1[:, l, which, :, x], mods[:, l, 3 * which * NC:3 * which * NC + NC, x]
                    link(v.tensor_tensor(fold[:], scale, b, ALU.mult))
                    also(v.tensor_tensor(shift, shift, fold[:], ALU.add))
                    last = v.tensor_tensor(scale, scale, g, ALU.mult)
                    if x == 0:
                        also(last)
                return last

            def part(s):
                kind = s[0]
                l = s[1] if len(s) > 1 else 0
                cs = cols(l)
                if kind in UNIT:
                    u = UNIT_NO[s]
                    if kind in ACT_PART:
                        dve.wait_ge(act_step_done, acts(s))
                    dve.wait_ge(unit_summed, units(s))
                    g = [gemm[:, 2 * (u % 2) + i] for i in range(2)]
                elif kind in AUX:
                    dve.wait_ge(aux_summed, auxes(s))
                    A = bank(s)
                if kind not in FROM_OTHERS and not (kind == "lnn" and s[3] % 2):
                    own()
                last = None
                if kind == "silu":
                    dve.wait_ge(act_step_done, acts(s))
                    last = v.tensor_tensor(csig[:], csig[:], cvec[:], ALU.mult)
                elif kind == "coefA":
                    dve.wait_ge(act_step_done, acts(("adaT", l, 7)))
                    for j in range(2):
                        b, n, gn = (VEC["b_in"], NH, "q_gain") if j == 0 else (VEC["b_in"] + OFF_K // P, NKV, "k_gain")
                        also(v.tensor_scalar(gainb[:, l, j * NH:j * NH + n], vecs[:, l, b:b + n], vec(l, gn), None,
                                             ALU.mult))
                    b = VEC["b_in"] + OFF_HY // P
                    also(v.tensor_tensor(convb[:, l], vecs[:, l, b:b + 3 * NC],
                                         vecs[:, l, VEC["conv_w"] + 3 * NC:VEC["conv_w"] + 6 * NC], ALU.mult))
                    own()
                    also(v.tensor_tensor(convb[:, l], convb[:, l],
                                         vecs[:, l, VEC["conv_b"]:VEC["conv_b"] + 3 * NC], ALU.add))
                    last = v.tensor_scalar(scale1[:, l, 0], mods[:, l, NC:2 * NC], 1.0, None, ALU.add)
                    if l:
                        also(last)
                        last = with_norm(l, 0, l - 1, "ln2")
                elif kind == "coefB":
                    dve.wait_ge(act_step_done, acts(("adaT", l, 23)))
                    for m, n in ((2, "b_out"), (5, "b_mlp2")):
                        for x in range(2):
                            also(v.tensor_tensor(gateb[:, l, m // 3, :, x], mods[:, l, m * NC:(m + 1) * NC, x],
                                                 vecs[:, l, VEC[n]:VEC[n] + NC], ALU.mult))
                    also(v.tensor_scalar(scale1[:, l, 1], mods[:, l, 4 * NC:5 * NC], 1.0, None, ALU.add))
                    last = with_norm(l, 1, l, "ln1")
                elif kind == "hprep":
                    if l == 0:
                        dve.wait_ge(act_step_done, acts(("f2", 1)))
                        dve.wait_ge(aux_summed, auxes(("f2", 1)))
                    else:
                        dve.wait_ge(unit_summed, units(("mlp2", l - 1, 3, 3)))
                    also(v.memset(pad[:, :, :, 0:1], 0.0))
                    last = v.memset(pad[:, :, :, S + 1:S + 2], 0.0)
                elif kind == "hb1":
                    _, _, which, c = s
                    if c == 0:
                        dve.wait_ge(x_in, 16)
                    if c >= 4:
                        dve.wait_ge(act_step_done, acts(("hb2", l, which, c - 4)))
                    for x in range(2):
                        last = v.tensor_scalar(hbuf(l, which, c)[:, tok(x)], XI[:, c, tok(x)],
                                               scale1[:, l, which, c, x:x + 1], mods[:, l, c, x:x + 1],
                                               ALU.mult, ALU.add)
                        if x == 0:
                            also(last)
                elif kind == "hb2":
                    _, _, which, c = s
                    dve.wait_ge(act_step_done, acts(s))
                    full = slice(0, T) if not which else cs
                    last = v.tensor_tensor(hl[:, c, full], hbuf(l, which, c)[:, full], hh[:, c, full].bitcast(F32),
                                           ALU.subtract)
                elif kind == "hy":
                    _, _, cg, part_ = s
                    u_ = hyu[cg % 2]
                    n0, n1 = (0, 2) if l == 0 else (1, 2)
                    src = lambda i, k: pad[:, i, n0:n1, k:k + S]
                    w = lambda i, k: vec(l, "conv_w", 3 * NC * k + NC * part_ + 2 * cg + i)
                    dst = lambda i: u_[:, part_, i, cs].rearrange("p (s t) -> p s t", t=S)
                    for i in range(2):
                        also(v.scalar_tensor_tensor(out=dst(i), in0=src(i, 0), scalar=w(i, 0), in1=dst(i),
                                                    op0=ALU.mult, op1=ALU.add))
                    own()
                    for i in range(2):
                        last = v.scalar_tensor_tensor(out=dst(i), in0=src(i, 2), scalar=w(i, 2), in1=dst(i),
                                                      op0=ALU.mult, op1=ALU.add)
                        if i == 0:
                            also(last)
                elif kind == "proj":
                    _, _, b, j = s
                    dve.wait_ge(act_step_done, acts(("gate", l, b, j)))
                    G = gates(l, b, j)
                    for i in range(2):
                        c = 2 * j + i
                        if b == 1:
                            last = v.tensor_tensor(M[:, c, cs], g[i][:, cs], G[:, i, cs], ALU.mult)
                            if i == 0:
                                also(last)
                        else:
                            also(v.tensor_tensor(gtmp[:, i, cs], g[i][:, cs], G[:, i, cs], ALU.mult))
                    if b != 1:
                        own()
                        last = v.tensor_tensor(M[:, 2 * j:2 * j + 2, cs], M[:, 2 * j:2 * j + 2, cs], gtmp[:, :, cs],
                                               ALU.add)
                elif kind == "msplit":
                    _, _, j = s
                    dve.wait_ge(act_step_done, acts(s))
                    last = v.tensor_tensor(hl[:, 2 * j:2 * j + 2, cs], M[:, 2 * j:2 * j + 2, cs],
                                           hh[:, 2 * j:2 * j + 2, cs].bitcast(F32), ALU.subtract)
                elif kind == "out":
                    _, _, j = s
                    if j == 0:
                        dve.wait_ge(xback_in, 16 * (l + 1))
                    residual(l, 0, j, lambda i: g[i])
                    return
                elif kind == "mlp1":
                    dve.wait_ge(act_step_done, acts(s))
                    last = v.tensor_tensor(st[:, 2:4, cs], st[:, 0:2, cs], st[:, 0:2, cs], ALU.mult)
                elif kind == "msq":
                    _, _, gr, j = s
                    dve.wait_ge(act_step_done, acts(s))
                    h, lo_ = hidden(gr)
                    last = v.tensor_tensor(lo_[:, 2 * j:2 * j + 2, cs], st[:, 2:4, cs],
                                           h[:, 2 * j:2 * j + 2, cs].bitcast(F32), ALU.subtract)
                elif kind == "mlp2":
                    _, _, gr, j = s
                    for i in range(2):
                        c = 2 * j + i
                        if gr == 0:
                            last = v.tensor_copy(M[:, c, cs], g[i][:, cs])
                        else:
                            last = v.tensor_tensor(M[:, c, cs], g[i][:, cs], M[:, c, cs], ALU.add)
                        if i == 0 or gr == 3:
                            also(last)
                    if gr == 3:
                        if j == 0:
                            dve.wait_ge(act_step_done, acts(("lnx", l, 0, NC - 1)))
                        own()
                        residual(l, 1, j, lambda i: M[:, 2 * j + i])
                        return
                elif kind in ("f1", "f2"):
                    n = "1" if kind == "f1" else "2"
                    src = A[0:FH, 0, 0:S]
                    ar, rn = farg
                    if (kind, l) != ("f1", 0):
                        dve.wait_ge(act_step_done, acts(("f1", 0) if (kind, l) == ("f1", 1) else ("f1", 1) if l == 0 else ("f2", 0)))
                    link(v.tensor_scalar(ar, src, vec(l, "hy_b" + n, 0, FH), vec(l, "hy_freq" + n, 0, FH),
                                         ALU.add, ALU.mult))
                    link(v.tensor_scalar(rn, ar, 1.0 / TWO_PI, ROUND, ALU.mult, ALU.add))
                    link(v.tensor_scalar(rn, rn, ROUND, None, ALU.subtract))
                    link(v.scalar_tensor_tensor(out=ar, in0=rn, scalar=-PI_HI, in1=ar, op0=ALU.mult, op1=ALU.add))
                    link(v.scalar_tensor_tensor(out=ar, in0=rn, scalar=-PI_LO, in1=ar, op0=ALU.mult, op1=ALU.add))
                    last = v.tensor_scalar(rn, ar, BELOW_PI, -BELOW_PI, ALU.min, ALU.max)
                elif kind == "K0":
                    _, _, cg, o = s
                    dve.wait_ge(dec_in[cg % 2], 16 * (NG // 2 * l + cg // 2 + 1))
                    dec = decb[cg % 2]
                    f, b = ht[:, 0], ht[:, 1]
                    also(v.tensor_tensor(f, A[:, :, 0:UC], dec, ALU.mult))
                    also(v.scalar_tensor_tensor(out=b[:, 0], in0=A[:, 0, UC:T], scalar=con("notfirst", 1),
                                                in1=dec[:, 0], op0=ALU.mult, op1=ALU.mult))
                    also(v.tensor_tensor(b[:, 1], A[:, 1, UC:T], dec[:, 1], ALU.mult))
                    own()
                    also(v.tensor_tensor(ksd[:, 0], f, b, ALU.add))
                    last = v.tensor_tensor(ksd[:, 1], f, b, ALU.subtract)
                elif kind == "KN":
                    _, _, cg, o = s
                    dve.wait_ge(act_step_done, acts(s))
                    link(v.reciprocal(ksn, ksn))
                    last = v.tensor_scalar(ksc[:, o], ksn, 1.0 / S, None, ALU.mult)
                elif kind in ("K1", "F"):
                    dve.wait_ge(act_step_done, acts(s))
                    U = kf[:, s[3]] if kind == "K1" else hub[Z_NO[s] % 2]
                    ec = ecb[EC_NO[s] % 2]
                    flat = lambda x: x.rearrange("p c n -> p (c n)")
                    also(v.tensor_tensor(flat(U[:, 0]), ec, A[:, 1], ALU.add))
                    ins = v.tensor_tensor(flat(U[:, 1]), ec, A[:, 1], ALU.subtract)
                    if kind == "K1":
                        last = ins
                    else:
                        o = s[4]
                        also(ins)
                        own()
                        Kf = kf[:, o]
                        link(v.tensor_tensor(ht, U, Kf, ALU.mult))
                        link(v.tensor_tensor(hy_y[:, :, 0], ht[:, :, 0], ht[:, :, 1], ALU.subtract))
                        for c in range(2):
                            also(v.tensor_tensor(ht[:, :, c], U[:, :, c], Kf[:, :, 1 - c], ALU.mult))
                        own()
                        link(v.tensor_tensor(hy_y[:, :, 1], ht[:, :, 0], ht[:, :, 1], ALU.add))
                        also(v.tensor_tensor(U[:, 0], hy_y[:, 0], hy_y[:, 1], ALU.add))
                        last = v.tensor_tensor(U[:, 1], hy_y[:, 0], hy_y[:, 1], ALU.subtract)
                elif kind == "I":
                    _, _, cg, st_, o = s
                    dve.wait_ge(act_step_done, acts(s))
                    u_ = hyu[cg % 2]
                    y1 = y1b[Z_NO[s] % 2]
                    for i in range(2):
                        also(v.scalar_tensor_tensor(out=y1[:, i], in0=u_[:, 2, i, tok(st_)],
                                                    scalar=vec(l, "hy_skip", NC * o + 2 * cg + i), in1=y1[:, i],
                                                    op0=ALU.mult, op1=ALU.add))
                    own()
                    last = v.tensor_tensor(u_[:, 2, :, tok(st_)], y1, u_[:, o, :, tok(st_)], ALU.mult)
                elif kind == "hsplit":
                    _, _, cg, st_ = s
                    dve.wait_ge(act_step_done, acts(s))
                    last = v.tensor_tensor(ol[:, 2 * cg:2 * cg + 2, tok(st_)], hyu[cg % 2][:, 2, :, tok(st_)],
                                           oh[:, 2 * cg:2 * cg + 2, tok(st_)].bitcast(F32), ALU.subtract)
                elif kind == "S2":
                    _, _, gr, st_ = s
                    dve.wait_ge(act_step_done, acts(s))
                    last = v.tensor_tensor(ol[:, 2 * gr:2 * gr + 2, tok(st_)],
                                           A[:, 0].rearrange("p (i t) -> p i t", i=2),
                                           oh[:, 2 * gr:2 * gr + 2, tok(st_)].bitcast(F32), ALU.subtract)
                elif kind == "KR1":
                    dve.wait_ge(act_step_done, acts(s))
                    link(v.reciprocal(rk, rk))
                    for t in range(8):
                        last = v.tensor_scalar(DG[:, t], ident, rk[:, t:t + 1], None, ALU.mult)
                        if t < 7:
                            also(last)
                elif kind == "KR2":
                    last = v.tensor_tensor(K, K, A, ALU.mult)
                elif kind in ("KR3", "QR"):
                    X2 = K if kind == "KR3" else QG[s[2] % 2]
                    R_ = A[:, 0 if kind == "KR3" else 1].rearrange("p (i t) -> p i t", i=2)
                    if kind == "QR":
                        dve.wait_ge(act_step_done, acts(s))
                        t0 = toks(l)[0]
                        r = rq[s[2] % 2].rearrange("p (i t) -> p i t", i=2)[:, :, t0:4]
                        link(v.reciprocal(r, r))
                        also(v.tensor_scalar(r, r, ATTN_SCALE, None, ALU.mult))
                    for i in range(2):
                        also(v.tensor_tensor(RT[:, 0, i], X2[:, i, S:T], rope_c, ALU.mult))
                        also(v.tensor_tensor(RT[:, 1, i], R_[:, i], rope_s, ALU.mult))
                    own()
                    last = v.tensor_tensor(X2[:, :, S:T], RT[:, 0], RT[:, 1], ALU.add)
                elif kind == "SC":
                    _, _, h, st_, qc = s
                    keys = slice(0, T) if st_ else slice(0, S)
                    col = 4 * (h % 2) + 2 * st_ + qc
                    n = ITEM_NO[s[1:]] % 4
                    link(v.tensor_reduce(nmax[n], A[:, 0, keys], AX.X, ALU.max))
                    last = v.tensor_scalar(nbias[n], nmax[n], rq[h // 2 % 2][:, col:col + 1], -1.0,
                                           ALU.mult, ALU.mult)
                elif kind == "SN":
                    _, _, h, st_, qc = s
                    dve.wait_ge(act_step_done, acts(("SC",) + s[1:]))
                    keys = slice(0, T) if st_ else slice(0, S)
                    n = ITEM_NO[s[1:]] % 4
                    link(v.reciprocal(rinv[n], rsum[n]))
                    last = v.tensor_scalar(PR[n][:, keys], PR[n][:, keys], rinv[n], None, ALU.mult)
                elif kind == "PV":
                    _, _, h, st_, qc = s
                    dve.wait_ge(act_step_done, acts(s))
                    at = st_ * S + qc * P
                    last = v.tensor_tensor(ol[:, h, at:at + P], A[:, 0, 0:P], oh[:, h, at:at + P].bitcast(F32),
                                           ALU.subtract)
                elif kind == "lnp":
                    last = v.tensor_scalar(ln_mean[:, cs], A[:, 0, cs], 4.0 / D, None, ALU.mult)
                elif kind == "lnd":
                    for c in (2 * s[3], 2 * s[3] + 1):
                        last = v.tensor_tensor(X[:, c, cs], X[:, c, cs], ln_mean[:, cs], ALU.subtract)
                        if c % 2 == 0:
                            also(last)
                elif kind == "lnf":
                    q = s[3]
                    if q == 2:
                        also(v.tensor_tensor(pairs[:, :, cs], X[:, 2:4, cs], X[:, 4:6, cs], ALU.add))
                    dve.wait_ge(act_step_done, acts(("lnsq",) + s[1:]))
                    last = v.tensor_tensor(M[:, 0:2, cs], M[:, 0:2, cs], M[:, 2 * q:2 * q + 2, cs], ALU.add)
                elif kind == "lnm":
                    dve.wait_ge(act_step_done, acts(s))
                    also(v.tensor_scalar(ln_off[:, cs], A[:, 0, cs], 1.0 / D, None, ALU.mult))
                    last = v.scalar_tensor_tensor(out=ln_rstd[:, cs], in0=A[:, 1, cs], scalar=1.0 / D,
                                                  in1=st[:, 1, cs], op0=ALU.mult, op1=ALU.subtract)
                elif kind == "lnr":
                    dve.wait_ge(act_step_done, acts(s))
                    last = v.reciprocal(ln_rstd[:, cs], ln_rstd[:, cs])
                elif kind == "lnn":
                    c = s[3]
                    if c % 2 == 0:
                        for k in (c, c + 1):
                            also(v.tensor_tensor(X[:, k, cs], X[:, k, cs], ln_off[:, cs], ALU.subtract))
                        own()
                    last = v.tensor_tensor(X[:, c, cs], X[:, c, cs], ln_rstd[:, cs], ALU.mult)
                last.then_inc(dve_step_done, 1)
                done["parts"] += 1

            def residual(l, which, j, y):
                m = 5 if which else 2
                for i in range(2):
                    c = 2 * j + i
                    for x in streams(l):
                        also(v.tensor_scalar(st[:, i, tok(x)], y(i)[:, tok(x)], mods[:, l, m * NC + c, x:x + 1],
                                             gateb[:, l, which, c, x:x + 1], ALU.mult, ALU.add))
                own()
                cs = cols(l)
                v.scalar_tensor_tensor(out=X[:, 2 * j:2 * j + 2, cs], in0=X[:, 2 * j:2 * j + 2, cs], scalar=ALPHA,
                                       in1=st[:, 0:2, cs], op0=ALU.mult, op1=ALU.add).then_inc(dve_step_done, 1)
                done["parts"] += 1

            def late(s):
                return s[0] == "out" and s[2] in (2, 3) or s[0] == "mlp2" and s[2:] in ((3, 2), (3, 3))

            for s in SCHEDULE:
                if s in AHEAD:
                    ahead = AHEAD[s]
                    if ahead in SPLIT_NO and not late(s):
                        lo(ahead)
                if s[0] in DVE_PART:
                    part(s)
                if s in AHEAD and late(s) and s[-1] == 2:
                    lo(AHEAD[s])
                if s[0] == "lnd" and s[3] == 3:
                    u = ("mlp2", s[1], 3, 3) if s[2] else ("out", s[1], 3)
                    if u in AHEAD:
                        lo(AHEAD[u])



def constants():
    con = np.zeros((P, NCON), np.float64)

    def put(name, x):
        con[:x.shape[0], CON[name]:CON[name] + x.shape[1]] = x

    t = np.arange(S).reshape(P, 2).T
    ang = np.pi * (2 * np.arange(P)[None, None, :] + 1) * t[:, :, None] / T
    f = np.stack([np.cos(ang), np.sin(ang)])
    put("hy_fwd", f.transpose(2, 0, 1, 3).reshape(P, -1))
    put("hy_inv", f.transpose(3, 0, 1, 2).reshape(P, -1))
    w = 2 * np.pi * (np.outer(np.arange(S), np.arange(S)) % S) / S
    put("fnet", np.stack([np.cos(w), np.sin(w)], 1).reshape(2, P, 2, S).transpose(1, 0, 2, 3).reshape(P, -1))
    inv_freq = 10000.0 ** (-np.arange(32) * 2.0 / 64)
    pos = np.stack([np.arange(S) // GRID_W, np.arange(S) % GRID_W])
    p = np.arange(P)
    a = inv_freq[p % 32][:, None] * pos[p // 64]
    put("rope_cos", np.cos(a))
    put("rope_sin", np.sin(a) * np.where(p % 64 < 32, -1.0, 1.0)[:, None])
    put("swap", np.eye(P)[p ^ 32])
    put("ident", np.eye(P))
    put("ones", np.ones((P, P)))
    tt = np.linspace(0.0, 1.0, S)
    ww = (2 * np.pi / S) * np.arange(S)
    ff = np.linspace(1e-4, BANDS - 1, BANDS)
    emb = np.concatenate([tt[None], np.cos(ff[:, None] * ww), -np.sin(ff[:, None] * ww)])
    emb = np.ascontiguousarray(emb.reshape(EMB, P, 2).transpose(0, 2, 1).reshape(EMB, S).astype(np.float32))
    put("notfirst", (p > 0).astype(float)[:, None])
    for n, e in (("epsln", LN_EPS), ("epsrms", RMS_EPS), ("epskern", KERN_EPS)):
        put(n, np.full((P, 1), e))
    lo, hi = math.log(1e-2) / 0.3, math.log(1e-2) / 1.5
    deltas = np.abs(np.linspace(lo, hi, D))
    decay = np.exp(-tt[:, None] * deltas)
    decay = decay.reshape(P, 2, NG, UC).transpose(2, 0, 1, 3)
    return con.astype(np.float32), emb, np.ascontiguousarray(decay.astype(np.float32))


def unit_source(w, s):
    kind, l = s[0], s[1]
    col = {"ada": lambda: 256 * s[2], "hy": lambda: OFF_HY + D * s[3] + UC * s[2],
           "gate": lambda: OFF_G + D * s[2] + UC * s[3], "fn": lambda: OFF_FN + UC * s[2],
           "k": lambda: OFF_K, "v": lambda: OFF_V, "q": lambda: UC * s[2], "out": lambda: UC * s[2],
           "proj": lambda: UC * s[3], "mlp1": lambda: D * s[2] + UC * s[3], "mlp2": lambda: UC * s[3]}[kind]()
    name = {"ada": "w_ada", "out": "w_out", "mlp1": "w_mlp1", "mlp2": "w_mlp2"}.get(kind, "w_in")
    if kind == "proj":
        name = ("w_att_o", "w_hy_o", "w_fn_o")[s[2]]
    rows = np.arange(D) + (D * s[2] if kind == "mlp2" else 0)
    if kind == "proj" and s[2] == 2:
        rows = rows.reshape(NG, 2, P)
        rows[:, 1] = rows[:, 1, ::-1].copy()
        rows = rows.reshape(-1)
    return w[name][l][rows, col:col + UC].reshape(NC, P, UC).transpose(1, 0, 2)


def kernel(**inputs):
    from concourse import bacc
    from concourse.bass_utils import run_bass_kernel_spmd

    w = {k: np.asarray(x) for k, x in inputs.items()}
    chunks = lambda x: x.reshape(-1, P).T
    wts = np.empty((len(UNITS), P, NC, UC), np.float32)
    for u, s in enumerate(UNITS):
        wts[u] = unit_source(w, s)
    vecs = np.zeros((P, DEPTH, NVEC), np.float32)
    for l in range(DEPTH):
        for name, at in VEC.items():
            x = w[name][l].reshape(-1)
            if x.size < P:
                vecs[:x.size, l, at] = x
            else:
                vecs[:, l, at:at + x.size // P] = chunks(x)
    tokens = np.concatenate([w["ctx"][0], w["x"][0]])
    con, emb, decay = constants()
    arrays = {
        "wts": wts.reshape(len(UNITS), P, UW),
        "vecs": vecs,
        "cons": con,
        "dec": decay,
        "emb": emb,
        "xt": np.ascontiguousarray(tokens.T.reshape(NC, P, T).transpose(1, 0, 2)),
        "ct": np.ascontiguousarray(np.stack([w["c_ctx"], w["c"][0]], -1).reshape(NC, P, 2).transpose(1, 0, 2)),
        "fw1": np.ascontiguousarray(w["hy_w1"].transpose(1, 0, 2)),
        "fw2": np.ascontiguousarray(w["hy_w2"].transpose(1, 0, 2)),
        "fw3": np.ascontiguousarray(w["hy_w3"].reshape(DEPTH, FH, 2, 2, NG, UC).transpose(0, 4, 3, 1, 2, 5))
        .reshape(DEPTH, NG, 2, FH, 2 * UC),
        "bv": np.ascontiguousarray(w["b_in"][None, :, OFF_V:OFF_HY]),
    }
    nc = bacc.Bacc("TRN2", target_bir_lowering=False, num_devices=1, dynamic_dma_scratch_size=4096)
    aps = {k: nc.dram_tensor("in_" + k, x.shape, F32, kind="ExternalInput").ap() for k, x in arrays.items()}
    out = nc.dram_tensor("out", (P, NC, S), F32, kind="ExternalOutput").ap()
    build_program(nc, aps, out)
    r = run_bass_kernel_spmd(nc, [{"in_" + k: x for k, x in arrays.items()}], core_ids=[0])
    y = np.asarray(r.results[0]["out"])
    return np.ascontiguousarray(y.transpose(2, 1, 0).reshape(1, S, D))
```
